# Optimizing a Trainium2 kernel written in Bass

```python
import jax, jax.numpy as jnp
from jax import lax
import numpy as np
import math

D_MODEL = 1024
BATCH = 1
SEQ = 256
DEPTH = 2

HEAD_DIM = 64
ROPE_THETA = 10000.0
GM_HEADS = D_MODEL // 2 // HEAD_DIM
GM_CHUNK = 128
NSA_HEADS = D_MODEL // 2 // HEAD_DIM
NSA_KV = NSA_HEADS // 4
NSA_HPG = NSA_HEADS // NSA_KV
CMP_LEN = 32
CMP_STRIDE = 16
SEL_BLOCK = 64
SEL_TOPN = 8
WINDOW = 512
Q_BLOCK = 128
POOL_WIDTH = D_MODEL // 2
POOL_WINDOWS = (2, 4, 8, 16)
POOL_GROUP = POOL_WIDTH // len(POOL_WINDOWS)
S5_WIDTH = D_MODEL // 2
S5_GROUP_CH = 16
S5_GROUPS = S5_WIDTH // S5_GROUP_CH
S5_STATE = 64
FFN_DIM = ((8 * D_MODEL // 3 + 255) // 256) * 256
N_EVEN = (DEPTH + 1) // 2
N_ODD = DEPTH // 2
GM_W = GM_HEADS * HEAD_DIM
NSA_W = NSA_HEADS * HEAD_DIM
KV_W = NSA_KV * HEAD_DIM
EVEN_SPLITS = (GM_W, GM_W, NSA_W, KV_W, KV_W, KV_W, KV_W, KV_W, KV_W, 3 * NSA_HEADS)
EVEN_IN = sum(EVEN_SPLITS)
EVEN_OUT = GM_W + NSA_W
ODD_IN = POOL_WIDTH + S5_WIDTH
ODD_OUT = POOL_WIDTH + S5_WIDTH
RMS_EPS = 1e-6
LN_EPS = 1e-5
NEG_INF = -1e30
SEL_FORCE = 1e4


def rmsnorm(x, g):
    xf = x.astype(jnp.float32)
    y = xf * lax.rsqrt(jnp.mean(xf * xf, axis=-1, keepdims=True) + RMS_EPS)
    return (y * g.astype(jnp.float32)).astype(x.dtype)

def swiglu(h, w_gate, w_up, w_down):
    return (jax.nn.silu(h @ w_gate) * (h @ w_up)) @ w_down

def rope(x, pos):
    half = HEAD_DIM // 2
    inv = ROPE_THETA ** (-jnp.arange(half, dtype=jnp.float32) / half)
    ang = pos[:, None] * inv[None, :]
    cos, sin = jnp.cos(ang)[:, None, :], jnp.sin(ang)[:, None, :]
    xf = x.astype(jnp.float32)
    x1, x2 = xf[..., :half], xf[..., half:]
    return jnp.concatenate([x1 * cos - x2 * sin, x2 * cos + x1 * sin], axis=-1).astype(x.dtype)

def gmlp_spatial_gate(u, v, w_s, b):
    B, S = u.shape[0], u.shape[1]
    u = jax.nn.gelu(u)
    v = jax.nn.gelu(v).astype(jnp.float32)
    mu = jnp.mean(v, axis=-1, keepdims=True)
    var = jnp.mean(jnp.square(v - mu), axis=-1, keepdims=True)
    v = ((v - mu) * lax.rsqrt(var + LN_EPS)).astype(u.dtype)
    causal = jnp.tril(jnp.ones((GM_CHUNK, GM_CHUNK), dtype=w_s.dtype))
    vc = v.reshape(B, S // GM_CHUNK, GM_CHUNK, GM_HEADS, HEAD_DIM)
    s = jnp.einsum('hts,bcshd->bcthd', w_s * causal, vc) + b.T[None, None, :, :, None]
    return u * s.reshape(B, S, GM_HEADS, HEAD_DIM)

def nsa_compress(t, pe, w1, w2, idx):
    B = t.shape[0]
    nc = idx.shape[0]
    blocks = t[:, idx] + pe[:, None, :]
    flat = blocks.transpose(0, 1, 3, 2, 4).reshape(B, nc, NSA_KV, CMP_LEN * HEAD_DIM)
    return jax.nn.gelu(flat @ w1) @ w2

def nsa_attention(q, k_c, v_c, k_s, v_s, k_w, v_w, gate_logits, pe, w1, w2):
    B, S = q.shape[0], q.shape[1]
    G, HPG = NSA_KV, NSA_HPG
    scale = HEAD_DIM ** -0.5
    t = jnp.arange(S, dtype=jnp.int32)
    qg = q.reshape(B, S, G, HPG, HEAD_DIM)

    nc = (S - CMP_LEN) // CMP_STRIDE + 1
    cmp_start = jnp.arange(nc, dtype=jnp.int32) * CMP_STRIDE
    cidx = cmp_start[:, None] + jnp.arange(CMP_LEN, dtype=jnp.int32)[None, :]
    kc = nsa_compress(k_c, pe[0], w1[0], w2[0], cidx)
    vc = nsa_compress(v_c, pe[1], w1[1], w2[1], cidx)
    end_pos = cmp_start + (CMP_LEN - 1)
    kc = rope(kc, end_pos.astype(jnp.float32))
    s_c = jnp.einsum('btgqd,bngd->bgqtn', qg, kc).astype(jnp.float32) * scale
    valid_c = end_pos[None, :] <= t[:, None]
    s_c = jnp.where(valid_c, s_c, NEG_INF)
    p_c = jax.nn.softmax(s_c, axis=-1) * jnp.any(valid_c, axis=-1)[:, None].astype(jnp.float32)
    o_c = jnp.einsum('bgqtn,bngd->btgqd', p_c.astype(vc.dtype), vc)

    nsel = S // SEL_BLOCK
    blk_start = jnp.arange(nsel, dtype=jnp.int32) * SEL_BLOCK
    overlap = ((cmp_start[:, None] < blk_start[None, :] + SEL_BLOCK)
               & (cmp_start[:, None] + CMP_LEN > blk_start[None, :])).astype(jnp.float32)
    imp = jnp.einsum('bgqtn,nj->btgj', p_c, overlap)
    cur = t // SEL_BLOCK
    j = jnp.arange(nsel, dtype=jnp.int32)
    forced = (j[None, :] == 0) | (j[None, :] == cur[:, None]) | (j[None, :] == cur[:, None] - 1)
    causal_blk = blk_start[None, :] <= t[:, None]
    imp = jnp.where(forced[:, None, :], SEL_FORCE,
                    jnp.where(causal_blk[:, None, :], imp, -SEL_FORCE))
    n_top = min(SEL_TOPN, nsel)
    _, sel_idx = lax.top_k(imp, n_top)

    kb = k_s.reshape(B, nsel, SEL_BLOCK, G, HEAD_DIM).transpose(0, 3, 1, 2, 4)
    vb = v_s.reshape(B, nsel, SEL_BLOCK, G, HEAD_DIM).transpose(0, 3, 1, 2, 4)
    nq = S // Q_BLOCK
    q_chunks = qg.reshape(B, nq, Q_BLOCK, G, HPG, HEAD_DIM).transpose(1, 0, 2, 3, 4, 5)
    i_chunks = sel_idx.reshape(B, nq, Q_BLOCK, G, n_top).transpose(1, 0, 2, 3, 4)
    t_chunks = t.reshape(nq, Q_BLOCK)
    bi = jnp.arange(B)[:, None, None, None]
    gi = jnp.arange(G)[None, None, :, None]
    in_blk = jnp.arange(SEL_BLOCK, dtype=jnp.int32)

    def selected_block(args):
        q_i, idx_i, t_i = args
        ks = kb[bi, gi, idx_i]
        vs = vb[bi, gi, idx_i]
        kpos = idx_i[..., None] * SEL_BLOCK + in_blk
        s = jnp.einsum('btgqd,btgnld->btgqnl', q_i, ks).astype(jnp.float32) * scale
        mask = kpos <= t_i[None, :, None, None, None]
        s = jnp.where(mask[:, :, :, None], s, NEG_INF)
        s = s.reshape(B, Q_BLOCK, G, HPG, n_top * SEL_BLOCK)
        p = jax.nn.softmax(s, axis=-1).astype(vs.dtype)
        return jnp.einsum('btgqk,btgkd->btgqd', p, vs.reshape(B, Q_BLOCK, G, n_top * SEL_BLOCK, HEAD_DIM))

    o_s = lax.map(selected_block, (q_chunks, i_chunks, t_chunks))
    o_s = o_s.transpose(1, 0, 2, 3, 4, 5).reshape(B, S, G, HPG, HEAD_DIM)

    span = WINDOW + Q_BLOCK
    kp = jnp.pad(k_w, ((0, 0), (WINDOW, 0), (0, 0), (0, 0)))
    vp = jnp.pad(v_w, ((0, 0), (WINDOW, 0), (0, 0), (0, 0)))
    widx = jnp.arange(nq, dtype=jnp.int32)[:, None] * Q_BLOCK + jnp.arange(span, dtype=jnp.int32)[None, :]
    kw = kp[:, widx]
    vw = vp[:, widx]
    kpos = widx - WINDOW
    qw = qg.reshape(B, nq, Q_BLOCK, G, HPG, HEAD_DIM)
    s_w = jnp.einsum('bitgqd,bikgd->bigqtk', qw, kw).astype(jnp.float32) * scale
    diff = t_chunks[:, :, None] - kpos[:, None, :]
    wmask = (kpos[:, None, :] >= 0) & (diff >= 0) & (diff < WINDOW)
    s_w = jnp.where(wmask[None, :, None, None], s_w, NEG_INF)
    p_w = jax.nn.softmax(s_w, axis=-1).astype(vw.dtype)
    o_w = jnp.einsum('bigqtk,bikgd->bitgqd', p_w, vw).reshape(B, S, G, HPG, HEAD_DIM)

    g = jax.nn.sigmoid(gate_logits.astype(jnp.float32)).reshape(B, S, G, HPG, 3)
    o = g[..., 0:1] * o_c + g[..., 1:2] * o_s + g[..., 2:3] * o_w
    return o.reshape(B, S, NSA_W).astype(q.dtype)

def even_mixer(h, w_in, w_out, gm_w_s, gm_b, cmp_pe, cmp_w1, cmp_w2):
    B, S = h.shape[0], h.shape[1]
    z = h @ w_in
    cuts = list(np.cumsum(EVEN_SPLITS)[:-1])
    u, v, q, kc, vc, ks, vs, kw, vw, gl = jnp.split(z, cuts, axis=-1)
    heads = lambda a, n: a.reshape(B, S, n, HEAD_DIM)
    pos = jnp.arange(S, dtype=jnp.float32)
    out_a = gmlp_spatial_gate(heads(u, GM_HEADS), heads(v, GM_HEADS), gm_w_s, gm_b).reshape(B, S, GM_W)
    out_b = nsa_attention(rope(heads(q, NSA_HEADS), pos),
                          heads(kc, NSA_KV), heads(vc, NSA_KV),
                          rope(heads(ks, NSA_KV), pos), heads(vs, NSA_KV),
                          rope(heads(kw, NSA_KV), pos), heads(vw, NSA_KV),
                          gl, cmp_pe, cmp_w1, cmp_w2)
    return jnp.concatenate([out_a, out_b.astype(out_a.dtype)], axis=-1) @ w_out

def odd_mixer(h, w_in, w_out, pool_w, pool_scale, lam_re, lam_im, b_re, b_im, c_re, c_im, d_skip, log_dt, w_glu):
    B, S = h.shape[0], h.shape[1]
    z = h @ w_in
    zc, zd = z[..., :POOL_WIDTH], z[..., POOL_WIDTH:]
    t = jnp.arange(S, dtype=jnp.int32)

    n_grp = len(POOL_WINDOWS)
    zg = zc.reshape(B, S, n_grp, POOL_GROUP).astype(jnp.float32)
    cs = jnp.concatenate([jnp.zeros((B, 1, n_grp, POOL_GROUP), jnp.float32), jnp.cumsum(zg, axis=1)], axis=1)
    win = jnp.array(POOL_WINDOWS, dtype=jnp.int32)
    lo = jnp.maximum(t[:, None] + 1 - win[None, :], 0)
    lower = cs[:, lo, jnp.arange(n_grp)[None, :]]
    cnt = (t[:, None] + 1 - lo).astype(jnp.float32)
    pooled = (cs[:, 1:] - lower) / cnt[..., None] - zg
    y_c = jnp.einsum('bsgc,gcd->bsgd', pooled, pool_w.astype(jnp.float32))
    y_c = (y_c.reshape(B, S, POOL_WIDTH) * pool_scale.astype(jnp.float32)).astype(h.dtype)

    u = zd.reshape(B, S, S5_GROUPS, S5_GROUP_CH).astype(jnp.float32)
    lam = lax.complex(lam_re.astype(jnp.float32), lam_im.astype(jnp.float32))
    dt = jnp.exp(log_dt.astype(jnp.float32))[:, None]
    lam_bar = jnp.exp(lam * dt)
    b_c = lax.complex(b_re.astype(jnp.float32), b_im.astype(jnp.float32))
    c_c = lax.complex(c_re.astype(jnp.float32), c_im.astype(jnp.float32))
    b_bar = ((lam_bar - 1.0) / lam)[..., None] * b_c
    bu = jnp.einsum('gpc,bsgc->sbgp', b_bar, u.astype(jnp.complex64))
    a = jnp.broadcast_to(lam_bar, (S, 1, S5_GROUPS, S5_STATE))

    def combine(e1, e2):
        a1, b1 = e1
        a2, b2 = e2
        return a2 * a1, a2 * b1 + b2

    _, states = lax.associative_scan(combine, (a, bu), axis=0)
    y = jnp.einsum('gcp,sbgp->bsgc', c_c, states).real + d_skip.astype(jnp.float32) * u
    y = jax.nn.gelu(y.reshape(B, S, S5_WIDTH))
    ab = y @ w_glu.astype(jnp.float32)
    y_d = (ab[..., :S5_WIDTH] * jax.nn.sigmoid(ab[..., S5_WIDTH:])).astype(h.dtype)

    return jnp.concatenate([y_c, y_d], axis=-1) @ w_out

def first_inputs(seed: int = 0) -> dict:
    key = jax.random.key(seed)
    k = jax.random.split(key, 26)
    f32 = jnp.float32
    nrm = lambda kk, shape, sc: jax.random.normal(kk, shape, f32) * sc
    lam_im = jnp.pi * jnp.broadcast_to(jnp.arange(S5_STATE, dtype=f32), (N_ODD, S5_GROUPS, S5_STATE))
    return {
        'x': nrm(k[0], (BATCH, SEQ, D_MODEL), 1.0),
        'norm_w': 1.0 + nrm(k[1], (DEPTH, 3, D_MODEL), 0.01),
        'ffn_w_gate': nrm(k[2], (DEPTH, 2, D_MODEL, FFN_DIM), D_MODEL ** -0.5),
        'ffn_w_up': nrm(k[3], (DEPTH, 2, D_MODEL, FFN_DIM), D_MODEL ** -0.5),
        'ffn_w_down': nrm(k[4], (DEPTH, 2, FFN_DIM, D_MODEL), FFN_DIM ** -0.5),
        'final_norm_w': 1.0 + nrm(k[5], (D_MODEL,), 0.01),
        'ev_w_in': nrm(k[6], (N_EVEN, D_MODEL, EVEN_IN), D_MODEL ** -0.5),
        'ev_w_out': nrm(k[7], (N_EVEN, EVEN_OUT, D_MODEL), EVEN_OUT ** -0.5),
        'gm_w_s': nrm(k[8], (N_EVEN, GM_HEADS, GM_CHUNK, GM_CHUNK), GM_CHUNK ** -0.5),
        'gm_b': 1.0 + nrm(k[9], (N_EVEN, GM_HEADS, GM_CHUNK), 0.01),
        'nsa_cmp_pe': nrm(k[10], (N_EVEN, 2, CMP_LEN, HEAD_DIM), 0.02),
        'nsa_cmp_w1': nrm(k[11], (N_EVEN, 2, CMP_LEN * HEAD_DIM, HEAD_DIM), (CMP_LEN * HEAD_DIM) ** -0.5),
        'nsa_cmp_w2': nrm(k[12], (N_EVEN, 2, HEAD_DIM, HEAD_DIM), HEAD_DIM ** -0.5),
        'od_w_in': nrm(k[13], (N_ODD, D_MODEL, ODD_IN), D_MODEL ** -0.5),
        'od_w_out': nrm(k[14], (N_ODD, ODD_OUT, D_MODEL), ODD_OUT ** -0.5),
        'pool_w': nrm(k[15], (N_ODD, len(POOL_WINDOWS), POOL_GROUP, POOL_GROUP), POOL_GROUP ** -0.5),
        'pool_scale': 1.0 + nrm(k[16], (N_ODD, POOL_WIDTH), 0.02),
        's5_lam_re': -0.5 + nrm(k[17], (N_ODD, S5_GROUPS, S5_STATE), 0.01),
        's5_lam_im': lam_im + nrm(k[18], (N_ODD, S5_GROUPS, S5_STATE), 0.01),
        's5_b_re': nrm(k[19], (N_ODD, S5_GROUPS, S5_STATE, S5_GROUP_CH), (2 * S5_GROUP_CH) ** -0.5),
        's5_b_im': nrm(k[20], (N_ODD, S5_GROUPS, S5_STATE, S5_GROUP_CH), (2 * S5_GROUP_CH) ** -0.5),
        's5_c_re': nrm(k[21], (N_ODD, S5_GROUPS, S5_GROUP_CH, S5_STATE), (2 * S5_STATE) ** -0.5),
        's5_c_im': nrm(k[22], (N_ODD, S5_GROUPS, S5_GROUP_CH, S5_STATE), (2 * S5_STATE) ** -0.5),
        's5_d': nrm(k[23], (N_ODD, S5_GROUPS, S5_GROUP_CH), 1.0),
        's5_log_dt': jax.random.uniform(k[24], (N_ODD, S5_GROUPS), f32, float(np.log(1e-3)), float(np.log(1e-1))),
        's5_w_glu': nrm(k[25], (N_ODD, S5_WIDTH, 2 * S5_WIDTH), S5_WIDTH ** -0.5),
    }

def first_block(x, norm_w, ffn_w_gate, ffn_w_up, ffn_w_down, final_norm_w, ev_w_in, ev_w_out,
              gm_w_s, gm_b, nsa_cmp_pe, nsa_cmp_w1, nsa_cmp_w2, od_w_in, od_w_out, pool_w, pool_scale,
              s5_lam_re, s5_lam_im, s5_b_re, s5_b_im, s5_c_re, s5_c_im, s5_d, s5_log_dt, s5_w_glu):
    for l in range(DEPTH):
        x = x + 0.5 * swiglu(rmsnorm(x, norm_w[l, 0]), ffn_w_gate[l, 0], ffn_w_up[l, 0], ffn_w_down[l, 0])
        h = rmsnorm(x, norm_w[l, 1])
        i = l // 2
        if l % 2 == 0:
            m = even_mixer(h, ev_w_in[i], ev_w_out[i], gm_w_s[i], gm_b[i],
                           nsa_cmp_pe[i], nsa_cmp_w1[i], nsa_cmp_w2[i])
        else:
            m = odd_mixer(h, od_w_in[i], od_w_out[i], pool_w[i], pool_scale[i],
                          s5_lam_re[i], s5_lam_im[i], s5_b_re[i], s5_b_im[i], s5_c_re[i], s5_c_im[i],
                          s5_d[i], s5_log_dt[i], s5_w_glu[i])
        x = x + m.astype(x.dtype)
        x = x + 0.5 * swiglu(rmsnorm(x, norm_w[l, 2]), ffn_w_gate[l, 1], ffn_w_up[l, 1], ffn_w_down[l, 1])
    return rmsnorm(x, final_norm_w)


_first_inputs = first_inputs


def first_inputs(seed=0):
    import zlib

    import numpy as np

    out = dict(_first_inputs(seed))
    spreads = {}
    factors = {'norm_w': 14.117,
     'final_norm_w': 156.403,
     'gm_b': 200.0,
     'nsa_cmp_pe': 200.0,
     'pool_scale': 145.979,
     's5_lam_re': 64.0,
     's5_lam_im': 39.656,
     's5_b_re': 54.808,
     's5_b_im': 54.752,
     's5_c_re': 55.736,
     's5_c_im': 55.088,
     's5_log_dt': 41.728,
     'gm_w_s': 3.254,
     'nsa_cmp_w1': 4.485,
     'nsa_cmp_w2': 3.747,
     's5_d': 5.232,
     's5_w_glu': 4.372}
    for name, (base, spread) in spreads.items():
        noise = np.random.default_rng([zlib.crc32(name.encode()), seed]).standard_normal(out[name].shape)
        drawn = base * np.exp(spread * noise) if base else spread * noise
        out[name] = __import__('jax').numpy.asarray(drawn.astype(out[name].dtype))
    for name, factor in factors.items():
        out[name] = (out[name] * factor).astype(out[name].dtype)
    return out


_narrow_inputs = first_inputs


def first_inputs(seed=0):
    out = dict(_narrow_inputs(seed))
    wider = {'final_norm_w': 6.06, 'gm_w_s': 5.01, 'gm_b': 6.04, 'pool_scale': 5.31}
    for name, times in wider.items():
        mean = out[name].mean()
        out[name] = (mean + times * (out[name] - mean)).astype(out[name].dtype)
    return out


CHUNK = 64
RET_HEADS = 4
RET_DK = 128
RET_DV = 256
RET_QK = RET_HEADS * RET_DK
RET_V = RET_HEADS * RET_DV
ROPE_BASE = 10000.0
HG_HEADS = 8
HG_DK = 128
HG_DV = 128
HG_K = HG_HEADS * HG_DK
HG_V = HG_HEADS * HG_DV
HG_BLOCK = 16
SWA_HQ = 16
SWA_HKV = 4
SWA_HD = 64
SWA_Q = SWA_HQ * SWA_HD
SWA_KV = SWA_HKV * SWA_HD
SWA_WINDOW = 128
SWA_WIN_CHUNKS = SWA_WINDOW // CHUNK
D_FF = 2816
N_EXPERTS = 8
TOP_K = 2
D_EXP = 3584
N_DENSE = (DEPTH + 1) // 2
N_MOE = DEPTH // 2
DN_ALPHA = (2.0 * DEPTH) ** 0.25
DN_BETA = (8.0 * DEPTH) ** -0.25
IN_SPLITS = (RET_QK, RET_QK, RET_V, RET_V,
             HG_K, HG_K, HG_V, HG_V,
             SWA_Q, SWA_KV, SWA_KV,
             D_MODEL, D_MODEL, D_MODEL)
N_IN = sum(IN_SPLITS)


def layer_norm(x, g, b):
    xf = x.astype(jnp.float32)
    mu = jnp.mean(xf, -1, keepdims=True)
    var = jnp.mean(jnp.square(xf - mu), -1, keepdims=True)
    return ((xf - mu) * lax.rsqrt(var + LN_EPS) * g + b).astype(x.dtype)

def rms_norm(x):
    xf = x.astype(jnp.float32)
    return xf * lax.rsqrt(jnp.mean(xf * xf, -1, keepdims=True) + RMS_EPS)

def rotary(x, pos):
    half = x.shape[-1] // 2
    inv = 1.0 / (ROPE_BASE ** jnp.linspace(0.0, 1.0, half, dtype=jnp.float32))
    ang = pos[:, None] * inv[None, :]
    cos = jnp.cos(ang)[None, :, None, :]
    sin = jnp.sin(ang)[None, :, None, :]
    x1, x2 = x[..., :half], x[..., half:]
    return jnp.concatenate([x1 * cos - x2 * sin, x1 * sin + x2 * cos], axis=-1)

def retention(q, k, v):
    B, S, H, DK = q.shape
    DV = v.shape[-1]
    n = S // CHUNK
    log_gamma = jnp.log(1.0 - 2.0 ** (-5.0 - jnp.arange(H, dtype=jnp.float32)))
    k = k * DK ** -0.5
    qc = q.reshape(B, n, CHUNK, H, DK)
    kc = k.reshape(B, n, CHUNK, H, DK)
    vc = v.reshape(B, n, CHUNK, H, DV)
    idx = jnp.arange(CHUNK, dtype=jnp.float32)
    diff = idx[:, None] - idx[None, :]
    decay = jnp.where(diff[None] >= 0,
                      jnp.exp(jnp.maximum(diff, 0.0)[None] * log_gamma[:, None, None]), 0.0)
    scores = jnp.einsum('bnthd,bnshd->bnhts', qc, kc) * decay
    o_intra = jnp.einsum('bnhts,bnshv->bnthv', scores, vc)
    k_decay = jnp.exp((CHUNK - 1.0 - idx)[:, None] * log_gamma[None, :])
    q_decay = jnp.exp((idx + 1.0)[:, None] * log_gamma[None, :])
    chunk_decay = jnp.exp(CHUNK * log_gamma)[None, :, None, None]

    def step(state, inp):
        q_n, k_n, v_n = inp
        o = jnp.einsum('bthd,th,bhdv->bthv', q_n, q_decay, state)
        state = chunk_decay * state + jnp.einsum('bshd,sh,bshv->bhdv', k_n, k_decay, v_n)
        return state, o

    init = jnp.zeros((B, H, DK, DV), jnp.float32)
    _, o_inter = lax.scan(step, init, (jnp.moveaxis(qc, 1, 0), jnp.moveaxis(kc, 1, 0),
                                       jnp.moveaxis(vc, 1, 0)))
    return (o_intra + jnp.moveaxis(o_inter, 0, 1)).reshape(B, S, H, DV)

def hgrn2_scan(q, log_f, k, v):
    B, S, H, DK = q.shape
    DV = v.shape[-1]
    n = S // HG_BLOCK
    L = HG_BLOCK
    qc = q.reshape(B, n, L, H, DK)
    kc = k.reshape(B, n, L, H, DK)
    vc = v.reshape(B, n, L, H, DV)
    bcum = jnp.cumsum(log_f.reshape(B, n, L, H, DK), axis=2)
    q_t = qc * jnp.exp(bcum)
    k_t = kc * jnp.exp(-bcum)
    causal = jnp.tril(jnp.ones((L, L), dtype=bool))
    a = jnp.where(causal, jnp.einsum('bnthd,bnshd->bnhts', q_t, k_t), 0.0)
    o_intra = jnp.einsum('bnhts,bnshv->bnthv', a, vc)
    b_last = bcum[:, :, -1]
    k_state = kc * jnp.exp(b_last[:, :, None] - bcum)
    blk_decay = jnp.exp(b_last)

    def step(state, inp):
        q_n, ks_n, v_n, d_n = inp
        o = jnp.einsum('bthd,bhdv->bthv', q_n, state)
        state = d_n[..., None] * state + jnp.einsum('bshd,bshv->bhdv', ks_n, v_n)
        return state, o

    init = jnp.zeros((B, H, DK, DV), jnp.float32)
    _, o_inter = lax.scan(step, init, (jnp.moveaxis(q_t, 1, 0), jnp.moveaxis(k_state, 1, 0),
                                       jnp.moveaxis(vc, 1, 0), jnp.moveaxis(blk_decay, 1, 0)))
    return (o_intra + jnp.moveaxis(o_inter, 0, 1)).reshape(B, S, H, DV)

def swa_with_sinks(q, k, v, sinks):
    B, S, HQ, HD = q.shape
    HKV = k.shape[2]
    G = HQ // HKV
    W = SWA_WIN_CHUNKS
    n = S // CHUNK
    qc = q.astype(jnp.float32).reshape(B, n, CHUNK, HKV, G, HD)
    kc = k.astype(jnp.float32).reshape(B, n, CHUNK, HKV, HD)
    vc = v.astype(jnp.float32).reshape(B, n, CHUNK, HKV, HD)
    padw = ((0, 0), (W, 0), (0, 0), (0, 0), (0, 0))
    kp = jnp.pad(kc, padw)
    vp = jnp.pad(vc, padw)
    kb = jnp.concatenate([kp[:, j:j + n] for j in range(W + 1)], axis=2)
    vb = jnp.concatenate([vp[:, j:j + n] for j in range(W + 1)], axis=2)
    chunk_ids = jnp.arange(n)[:, None] - W + jnp.arange(W + 1)[None, :]
    valid = jnp.repeat(chunk_ids >= 0, CHUNK, axis=1)
    s = jnp.einsum('bntkgd,bnskd->bnkgts', qc, kb) * HD ** -0.5
    s = jnp.where(valid[None, :, None, None, None, :], s, -jnp.inf)
    sink = sinks.astype(jnp.float32).reshape(HKV, G)[None, None, :, :, None, None]
    m = jnp.maximum(jnp.max(s, -1, keepdims=True), sink)
    p = jnp.exp(s - m)
    p = p / (jnp.sum(p, -1, keepdims=True) + jnp.exp(sink - m))
    o = jnp.einsum('bnkgts,bnskd->bntkgd', p, vb)
    return o.reshape(B, S, HQ * HD)

def swiglu_2(h, w_gate, w_up, w_down):
    return (jax.nn.silu(h @ w_gate) * (h @ w_up)) @ w_down

def moe_swiglu(h2, w_router, w_gate, w_up, w_down):
    logits = (h2 @ w_router).astype(jnp.float32)
    top_logits, top_idx = lax.top_k(logits, TOP_K)
    top_w = jax.nn.softmax(top_logits, axis=-1)
    flat_e = top_idx.reshape(-1)
    order = jnp.argsort(flat_e)
    tok = order // TOP_K
    xs = h2[tok]
    sizes = jnp.bincount(flat_e, length=N_EXPERTS).astype(jnp.int32)
    hid = jax.nn.silu(lax.ragged_dot(xs, w_gate, sizes)) * lax.ragged_dot(xs, w_up, sizes)
    y = lax.ragged_dot(hid, w_down, sizes)
    y = y * top_w.reshape(-1)[order][:, None].astype(y.dtype)
    return jnp.zeros_like(h2).at[tok].add(y.astype(h2.dtype))

def second_inputs(seed: int = 0) -> dict:
    key = jax.random.key(seed)
    ks = jax.random.split(key, 24)
    f32 = jnp.float32
    D = D_MODEL

    def nrm(k, shape, scale):
        return jax.random.normal(k, shape, f32) * scale

    return {
        'x': nrm(ks[0], (BATCH, SEQ, D), 1.0),
        'ln_in_g': 1.0 + nrm(ks[1], (D,), 0.02),
        'ln_in_b': nrm(ks[2], (D,), 0.02),
        'w_in': nrm(ks[3], (DEPTH, D, N_IN), D ** -0.5),
        'ret_w_out': nrm(ks[4], (DEPTH, RET_V, D), DN_BETA * RET_V ** -0.5),
        'hgrn_lower_bounds': 1.0 + nrm(ks[5], (DEPTH, HG_K), 0.5),
        'hgrn_norm_g': 1.0 + nrm(ks[6], (DEPTH, HG_DV), 0.02),
        'hgrn_w_out': nrm(ks[7], (DEPTH, HG_V, D), DN_BETA * HG_V ** -0.5),
        'swa_sinks': nrm(ks[8], (DEPTH, SWA_HQ), 0.5),
        'swa_w_out': nrm(ks[9], (DEPTH, SWA_Q, D), DN_BETA * SWA_Q ** -0.5),
        'w_o': nrm(ks[10], (DEPTH, D, D), DN_BETA * D ** -0.5),
        'ln_mix_g': 1.0 + nrm(ks[11], (DEPTH, D), 0.02),
        'ln_mix_b': nrm(ks[12], (DEPTH, D), 0.02),
        'ffn_w_gate': nrm(ks[13], (N_DENSE, D, D_FF), D ** -0.5),
        'ffn_w_up': nrm(ks[14], (N_DENSE, D, D_FF), D ** -0.5),
        'ffn_w_down': nrm(ks[15], (N_DENSE, D_FF, D), DN_BETA * D_FF ** -0.5),
        'moe_router': nrm(ks[16], (N_MOE, D, N_EXPERTS), D ** -0.5),
        'moe_w_gate': nrm(ks[17], (N_MOE, N_EXPERTS, D, D_EXP), D ** -0.5),
        'moe_w_up': nrm(ks[18], (N_MOE, N_EXPERTS, D, D_EXP), D ** -0.5),
        'moe_w_down': nrm(ks[19], (N_MOE, N_EXPERTS, D_EXP, D), DN_BETA * D_EXP ** -0.5),
        'ln_ffn_g': 1.0 + nrm(ks[20], (DEPTH, D), 0.02),
        'ln_ffn_b': nrm(ks[21], (DEPTH, D), 0.02),
    }

def second_block(x, ln_in_g, ln_in_b, w_in, ret_w_out, hgrn_lower_bounds, hgrn_norm_g, hgrn_w_out,
              swa_sinks, swa_w_out, w_o, ln_mix_g, ln_mix_b, ffn_w_gate, ffn_w_up, ffn_w_down,
              moe_router, moe_w_gate, moe_w_up, moe_w_down, ln_ffn_g, ln_ffn_b):
    B, S, D = x.shape
    f32 = jnp.float32
    pos = jnp.arange(S, dtype=f32)
    split_points = np.cumsum(np.array(IN_SPLITS))[:-1].tolist()
    lb_all = jnp.cumsum(jax.nn.softmax(hgrn_lower_bounds.astype(f32), axis=0), axis=0)
    lb_all = lb_all - lb_all[0]

    h = layer_norm(x, ln_in_g, ln_in_b)
    for layer in range(DEPTH):
        proj = jnp.einsum('bsd,dc->bsc', h, w_in[layer])
        (rq, rk, rv, rg, hq, hf, hi, hg, sq, sk, sv, ga, gb, gc) = jnp.split(proj, split_points, axis=-1)

        r_q = rotary(rq.astype(f32).reshape(B, S, RET_HEADS, RET_DK), pos)
        r_k = rotary(rk.astype(f32).reshape(B, S, RET_HEADS, RET_DK), pos)
        r_v = rv.astype(f32).reshape(B, S, RET_HEADS, RET_DV)
        r_o = rms_norm(retention(r_q, r_k, r_v)).reshape(B, S, RET_V)
        y_a = (jax.nn.silu(rg.astype(f32)) * r_o) @ ret_w_out[layer]

        lb = lb_all[layer].reshape(HG_HEADS, HG_DK)
        z = hf.astype(f32).reshape(B, S, HG_HEADS, HG_DK)
        log_f = jnp.logaddexp(jnp.log(lb), jnp.log1p(-lb) + jax.nn.log_sigmoid(z))
        h_k = -jnp.expm1(log_f)
        h_q = hq.astype(f32).reshape(B, S, HG_HEADS, HG_DK)
        h_v = hi.astype(f32).reshape(B, S, HG_HEADS, HG_DV)
        h_o = rms_norm(hgrn2_scan(h_q, log_f, h_k, h_v)) * hgrn_norm_g[layer]
        y_b = (jax.nn.silu(hg.astype(f32)) * h_o.reshape(B, S, HG_V)) @ hgrn_w_out[layer]

        s_o = swa_with_sinks(sq.reshape(B, S, SWA_HQ, SWA_HD), sk.reshape(B, S, SWA_HKV, SWA_HD),
                             sv.reshape(B, S, SWA_HKV, SWA_HD), swa_sinks[layer])
        y_c = s_o @ swa_w_out[layer]

        merged = (jax.nn.sigmoid(ga.astype(f32)) * y_a + jax.nn.sigmoid(gb.astype(f32)) * y_b
                  + jax.nn.sigmoid(gc.astype(f32)) * y_c)
        mix = merged @ w_o[layer]
        h = layer_norm((DN_ALPHA * h + mix).astype(h.dtype), ln_mix_g[layer], ln_mix_b[layer])

        j = layer // 2
        if layer % 2 == 0:
            ff = swiglu_2(h, ffn_w_gate[j], ffn_w_up[j], ffn_w_down[j])
        else:
            ff = moe_swiglu(h.reshape(B * S, D), moe_router[j], moe_w_gate[j], moe_w_up[j],
                            moe_w_down[j]).reshape(B, S, D)
        h = layer_norm((DN_ALPHA * h + ff).astype(h.dtype), ln_ffn_g[layer], ln_ffn_b[layer])
    return h


def setup_inputs(seed=0):
    out = dict(first_inputs(seed))
    for name, value in second_inputs(seed + 1).items():
        if name != "x":
            out[name + "_2"] = value
    return out


def reference(
    x, norm_w, ffn_w_gate, ffn_w_up, ffn_w_down, final_norm_w, ev_w_in, ev_w_out, gm_w_s, gm_b,
    nsa_cmp_pe, nsa_cmp_w1, nsa_cmp_w2, od_w_in, od_w_out, pool_w, pool_scale, s5_lam_re,
    s5_lam_im, s5_b_re, s5_b_im, s5_c_re, s5_c_im, s5_d, s5_log_dt, s5_w_glu, ln_in_g_2,
    ln_in_b_2, w_in_2, ret_w_out_2, hgrn_lower_bounds_2, hgrn_norm_g_2, hgrn_w_out_2,
    swa_sinks_2, swa_w_out_2, w_o_2, ln_mix_g_2, ln_mix_b_2, ffn_w_gate_2, ffn_w_up_2,
    ffn_w_down_2, moe_router_2, moe_w_gate_2, moe_w_up_2, moe_w_down_2, ln_ffn_g_2, ln_ffn_b_2,
):
    x = first_block(
        x, norm_w, ffn_w_gate, ffn_w_up, ffn_w_down, final_norm_w, ev_w_in, ev_w_out, gm_w_s,
        gm_b, nsa_cmp_pe, nsa_cmp_w1, nsa_cmp_w2, od_w_in, od_w_out, pool_w, pool_scale,
        s5_lam_re, s5_lam_im, s5_b_re, s5_b_im, s5_c_re, s5_c_im, s5_d, s5_log_dt, s5_w_glu,
    )
    return second_block(
        x, ln_in_g_2, ln_in_b_2, w_in_2, ret_w_out_2, hgrn_lower_bounds_2, hgrn_norm_g_2,
        hgrn_w_out_2, swa_sinks_2, swa_w_out_2, w_o_2, ln_mix_g_2, ln_mix_b_2, ffn_w_gate_2,
        ffn_w_up_2, ffn_w_down_2, moe_router_2, moe_w_gate_2, moe_w_up_2, moe_w_down_2,
        ln_ffn_g_2, ln_ffn_b_2,
    )


_drawn_inputs = setup_inputs


def setup_inputs(seed=0):
    import zlib

    import numpy as np

    out = dict(_drawn_inputs(seed))
    spreads = {}
    factors = {'hgrn_norm_g_2': 21.609, 'swa_sinks_2': 23.381}
    for name, (base, spread) in spreads.items():
        noise = np.random.default_rng([zlib.crc32(name.encode()), seed]).standard_normal(out[name].shape)
        drawn = base * np.exp(spread * noise) if base else spread * noise
        out[name] = __import__('jax').numpy.asarray(drawn.astype(out[name].dtype))
    for name, factor in factors.items():
        out[name] = (out[name] * factor).astype(out[name].dtype)
    return out
```

```python
from contextlib import ExitStack

import numpy as np
import concourse.bass as bass
from concourse import mybir

F32 = mybir.dt.float32
ALU = mybir.AluOpType
ACT = mybir.ActivationFunctionType
AX = mybir.AxisListType

P = 128
T = 256
D = 1024
TT = T // P
KD = D // P
GW = 256
HD = 64
START = 8
RMS_EPS = 1e-6
LN_EPS = 1e-5
NEG = -1e30


class Core:

    def __init__(self, nc, dram, stack):
        self.nc, self.dram, self.stack, self.sig = nc, dram, stack, {}


class Product:

    def __init__(self, w, groups, take, tm, src, cols, kd):
        self.w, self.groups, self.take, self.tm, self.src, self.cols, self.kd = w, groups, take, tm, src, cols, kd


class Pass:

    def __init__(self, q, k, nk, v, mask, sinks, gates, valid):
        self.q, self.k, self.nk, self.v = q, k, nk, v
        self.mask, self.sinks, self.gates, self.valid = mask, sinks, gates, valid


class Signal:

    def __init__(self, sem):
        self.sem, self.base = sem, START

    def advance(self, n):
        self.base += n


class Chain:

    def __init__(self, sem):
        self.sem, self.n = sem, START

    def __call__(self, eng, ins):
        self.n += 1
        ins.then_inc(self.sem, 1)
        eng.wait_ge(self.sem, self.n)


def signals(c, *names):
    for n in names:
        if n not in c.sig:
            c.sig[n] = Signal(c.stack.enter_context(c.nc.semaphore(n)))
    return [c.sig[n] for n in names]


def norm_stage(c, gain_fm=None, gain_tm=None, layer=None):
    nc, x, hT, ps = c.nc, c.x, c.hT, c.ps
    stat_ready, root_ready, normed, packed, unloaded, gains = signals(
        c, "stat_ready", "root_ready", "normed", "packed", "unloaded", "gains_loaded")
    b0, r0, n0, p0, u0, g0 = (s.base for s in (stat_ready, root_ready, normed, packed, unloaded, gains))
    inplace = gain_fm is None
    xs = x if inplace else c.work.rearrange("p (t d) -> p t d", t=TT)[:, :, 0:D]
    rows = [gain_tm] if gain_tm is not None else (list(layer) if layer else [])

    with nc.Block() as block:
        @block.sync
        def _(sp):
            for n, row in enumerate(rows):
                sp.dma_start(c.rowbuf[:, n, :], row.partition_broadcast(P)).then_inc(gains.sem, 16)

        @block.scalar
        def _(act):
            act.wait_ge(stat_ready.sem, b0 + 1)
            nc.scalar.activation(c.small[:, 2:4], c.small[:, 0:2], ACT.Sqrt).then_inc(root_ready.sem, 1)

        @block.vector
        def _(dve):
            link = lambda ins: c.vchain(dve, ins)
            if layer:
                for t in range(TT):
                    for h in range(2):
                        link(nc.vector.bn_stats(c.small[:, 32 + 16 * t + 6 * h:38 + 16 * t + 6 * h],
                                                x[:, t, 512 * h:512 * h + 512]))
                for t in range(TT):
                    link(nc.vector.bn_aggr(c.small[:, 16 + 2 * t:18 + 2 * t], c.small[:, 32 + 16 * t:44 + 16 * t]))
                var = c.small[:, 16:20].rearrange("p (t two) -> p t two", two=2)[:, :, 1]
                nc.vector.tensor_scalar(c.small[:, 0:2], var, LN_EPS, None, ALU.add).then_inc(stat_ready.sem, 1)
            else:
                for t in range(TT):
                    link(nc.vector.tensor_tensor_reduce(
                        out=c.work[:, 0:D], in0=x[:, t, :], in1=x[:, t, :], scale=1.0, scalar=0.0,
                        op0=ALU.mult, op1=ALU.add, accum_out=c.small[:, 4 + t:5 + t]))
                nc.vector.tensor_scalar(c.small[:, 0:2], c.small[:, 4:6], 1.0 / D, RMS_EPS,
                                        ALU.mult, ALU.add).then_inc(stat_ready.sem, 1)
            dve.wait_ge(root_ready.sem, r0 + 1)
            link(nc.vector.reciprocal(c.small[:, 6:8], c.small[:, 2:4]))
            if rows:
                dve.wait_ge(gains.sem, g0 + 16 * len(rows))
            for t in range(TT):
                if layer:
                    link(nc.vector.tensor_scalar(xs[:, t, :], x[:, t, :], c.small[:, 16 + 2 * t:17 + 2 * t],
                                                 c.small[:, 6 + t:7 + t], ALU.subtract, ALU.mult))
                    link(nc.vector.tensor_tensor(xs[:, t, :], xs[:, t, :], c.rowbuf[:, 0, :], ALU.mult))
                    nc.vector.tensor_tensor(xs[:, t, :], xs[:, t, :], c.rowbuf[:, 1, :],
                                            ALU.add).then_inc(normed.sem, 1)
                elif gain_tm is not None:
                    nc.vector.scalar_tensor_tensor(
                        out=xs[:, t, :], in0=x[:, t, :], scalar=c.small[:, 6 + t:7 + t], in1=c.rowbuf[:, 0, :],
                        op0=ALU.mult, op1=ALU.mult).then_inc(normed.sem, 1)
                else:
                    nc.vector.tensor_scalar(xs[:, t, :], x[:, t, :], c.small[:, 6 + t:7 + t], None,
                                            ALU.mult).then_inc(normed.sem, 1)
            for n in range(4):
                t, q = n // 2, n % 2
                dve.wait_ge(packed.sem, p0 + n + 1)
                src = ps[:, n, :].rearrange("p (k f) -> p k f", k=4)
                dst = hT[:, 4 * q:4 * q + 4, P * t:P * t + P]
                if gain_fm is not None:
                    g = gain_fm[:, 4 * q:4 * q + 4].unsqueeze(2).to_broadcast([P, 4, P])
                    nc.vector.tensor_tensor(dst, src, g, ALU.mult).then_inc(unloaded.sem, 1)
                else:
                    nc.vector.tensor_copy(dst, src).then_inc(unloaded.sem, 1)

        @block.tensor
        def _(pe):
            for t in range(TT):
                pe.wait_ge(normed.sem, n0 + t + 1)
                for q in range(2):
                    for k in range(4):
                        last = nc.tensor.transpose(ps[:, 2 * t + q, P * k:P * k + P],
                                                   xs[:, t, P * (4 * q + k):P * (4 * q + k) + P], c.ident)
                    last.then_inc(packed.sem, 1)
    stat_ready.advance(1)
    root_ready.advance(1)
    normed.advance(2)
    packed.advance(4)
    unloaded.advance(4)
    gains.advance(16 * len(rows))


def ffn_stage(c, w_gate, w_up, w_down, per_expert, experts=1, mix=None, keep=1.0, add=0.5):
    nc, x, hT, ps = c.nc, c.x, c.hT, c.ps
    G = per_expert
    loaded = signals(c, "ffn_loaded0", "ffn_loaded1")
    gate_made, up_made, silu_made, weighed, hidden_made, hidden_used, summed = signals(
        c, "gate_made", "up_made", "silu_made", "weighed", "hidden_made", "hidden_used", "summed")
    steps = experts * G
    lb = [s.base for s in loaded]
    gb, pb, sb, wb, hb, hub, smb = (s.base for s in (gate_made, up_made, silu_made, weighed, hidden_made,
                                                    hidden_used, summed))
    wg = [c.ring[:, 3 * s, :].rearrange("p (k f) -> p k f", k=KD) for s in range(2)]
    wu = [c.ring[:, 3 * s + 1, :].rearrange("p (k f) -> p k f", k=KD) for s in range(2)]
    wd = [c.ring[:, 3 * s + 2, :].rearrange("p (h n) -> p h n", h=2) for s in range(2)]
    silu = [c.work[:, T * n:T * n + T] for n in range(4)]
    mixed = [c.work[:, T * (4 + n):T * (5 + n)] for n in range(4)]
    hidden = [c.work[:, T * (8 + n):T * (9 + n)] for n in range(4)]

    def each_step(eng, body):
        if experts > 1:
            assert G % 2 == 0
            with eng.Fori(0, experts) as e:
                with eng.Fori(0, G // 2) as i:
                    for s in range(2):
                        body(s, e * (G // 2) + i, e, e * G + i * 2 + s)
        else:
            with eng.Fori(0, G // 2) as i:
                for s in range(2):
                    body(s, i, 0, i * 2 + s)
            if G % 2:
                body(0, G // 2, 0, G - 1)

    with nc.Block() as block:
        @block.sync
        def _(sp):
            def load(s, pair, e, step):
                sp.wait_ge(hidden_used.sem, step * 2 + (hub - 2))
                for w, dst in ((w_gate, 3 * s), (w_up, 3 * s + 1), (w_down, 3 * s + 2)):
                    src = w[bass.ds(step, 1), :, :].rearrange("o p n -> p (o n)")
                    sp.dma_start(c.ring[:, dst, :], src).then_inc(loaded[s].sem, 16)
            each_step(sp, load)

        @block.scalar
        def _(act):
            def gate(s, pair, e, step):
                for h in range(2):
                    act.wait_ge(gate_made.sem, step * 2 + (gb + h + 1))
                    act.wait_ge(hidden_made.sem, step * 2 + (hb + h - 3))
                    nc.scalar.activation(silu[2 * s + h], ps[:, 2 * h, 0:T], ACT.Silu).then_inc(silu_made.sem, 1)
            each_step(act, gate)

        @block.gpsimd
        def _(pool):
            def make(s, pair, e, step):
                for h in range(2):
                    pool.wait_ge(silu_made.sem, step * 2 + (sb + h + 1))
                    pool.wait_ge(weighed.sem, step * 2 + (wb + h + 1))
                    pool.wait_ge(hidden_used.sem, step * 2 + (hub + h - 3))
                    nc.gpsimd.tensor_tensor(hidden[2 * s + h], mixed[2 * s + h], silu[2 * s + h], ALU.mult)\
                        .then_inc(hidden_made.sem, 1)
            if mix is not None:
                each_step(pool, make)

        @block.vector
        def _(dve):
            def weigh(s, pair, e, step):
                for h in range(2):
                    dve.wait_ge(up_made.sem, step * 2 + (pb + h + 1))
                    dve.wait_ge(hidden_made.sem, step * 2 + (hb + h - 3))
                    m = mix[:, bass.ds(e, 1), :].rearrange("p o t -> p (o t)")
                    nc.vector.tensor_tensor(mixed[2 * s + h], ps[:, 2 * h + 1, 0:T], m, ALU.mult)\
                        .then_inc(weighed.sem, 1)

            def make(s, pair, e, step):
                for h in range(2):
                    dve.wait_ge(silu_made.sem, step * 2 + (sb + h + 1))
                    dve.wait_ge(up_made.sem, step * 2 + (pb + h + 1))
                    dve.wait_ge(hidden_used.sem, step * 2 + (hub + h - 3))
                    nc.vector.tensor_tensor(hidden[2 * s + h], silu[2 * s + h], ps[:, 2 * h + 1, 0:T], ALU.mult)\
                        .then_inc(hidden_made.sem, 1)
            each_step(dve, make if mix is None else weigh)
            dve.wait_ge(hidden_used.sem, hub + 2 * steps)
            dve.wait_ge(summed.sem, smb + 2)
            if keep != 1.0:
                for t in range(TT):
                    c.vchain(dve, nc.vector.tensor_scalar(x[:, t, :], x[:, t, :], keep, None, ALU.mult))
            for t in range(TT):
                for n in range(2):
                    xn = x[:, t, 512 * n:512 * n + 512]
                    c.vchain(dve, nc.vector.scalar_tensor_tensor(
                        out=xn, in0=ps[:, 4 + 2 * t + n, :], scalar=add, in1=xn, op0=ALU.mult, op1=ALU.add))

        @block.tensor
        def _(pe):
            def down(s, h, start=False, stop=False):
                for t in range(TT):
                    for n in range(2):
                        last = nc.tensor.matmul(ps[:, 4 + 2 * t + n, :], hidden[2 * s + h][:, P * t:P * t + P],
                                                wd[s][:, h, 512 * n:512 * n + 512], start=start, stop=stop,
                                                skip_group_check=True)
                return last

            def clear(start, stop):
                for t in range(TT):
                    for n in range(2):
                        last = nc.tensor.matmul(ps[:, 4 + 2 * t + n, :], c.zeros[0:32, 0:P], c.zeros[0:32, :],
                                                start=start, stop=stop, skip_group_check=True)
                return last

            def products(s, pair, e, step):
                pe.wait_ge(loaded[s].sem, pair * 48 + (lb[s] + 48))
                for h in range(2):
                    pe.wait_ge(hidden_made.sem, step * 2 + (hb + h - 1))
                    for w, bank, made in ((wg, 2 * h, gate_made), (wu, 2 * h + 1, up_made)):
                        for k in range(KD):
                            last = nc.tensor.matmul(ps[:, bank, 0:T], w[s][:, k, P * h:P * h + P], hT[:, k, :],
                                                    start=(k == 0), stop=(k == KD - 1))
                        last.then_inc(made.sem, 1)
                for h in range(2):
                    pe.wait_ge(hidden_made.sem, step * 2 + (hb + h + 1))
                    last = down(s, h)
                    last.then_inc(hidden_used.sem, 1)
            clear(True, False).then_inc(summed.sem, 1)
            each_step(pe, products)
            clear(False, True).then_inc(summed.sem, 1)
    for s in range(2):
        n = (steps + 1 - s) // 2
        loaded[s].advance(48 * n)
    gate_made.advance(2 * steps)
    up_made.advance(2 * steps)
    silu_made.advance(2 * steps)
    if mix is not None:
        weighed.advance(2 * steps)
    hidden_made.advance(2 * steps)
    hidden_used.advance(2 * steps)
    summed.advance(2)


def product(c, w, groups, take, tm=False, src=None, cols=GW):
    return Product(w=w, groups=groups, take=take, tm=tm, src=c.hT if src is None else src, cols=cols,
                           kd=w.shape[2] // GW)


def project_stage(c, runs, unloader="scalar"):
    nc, ps = c.nc, c.ps
    loaded = signals(c, "weights_loaded0", "weights_loaded1")
    made, taken = signals(c, "product_made", "product_taken")
    lb, mb, tb = [s.base for s in loaded], made.base, taken.base
    total = sum(r.groups for r in runs)

    def each_step(eng, body):
        n = 0
        for r in runs:
            if r.groups >= 4:
                with eng.Fori(0, r.groups // 2) as i:
                    for j in range(2):
                        body(r, (n + j) % 2, i * 2 + j, i * 2 + (n + j), i + (n + j) // 2)
                rest = range(r.groups - r.groups % 2, r.groups)
            else:
                rest = range(r.groups)
            for g in rest:
                body(r, (n + g) % 2, g, n + g, (n + g) // 2)
            n += r.groups

    with nc.Block() as block:
        @block.sync
        def _(sp):
            def load(r, s, g, step, uses):
                sp.wait_ge(made.sem, step + (mb - 1))
                src = r.w[bass.ds(g, 1), :, :].rearrange("o p n -> p (o n)")
                sp.dma_start(c.ring[:, s, 0:r.kd * GW], src).then_inc(loaded[s].sem, 16)
            each_step(sp, load)

        @block.tensor
        def _(pe):
            def multiply(r, s, g, step, uses):
                pe.wait_ge(loaded[s].sem, uses * 16 + (lb[s] + 16))
                pe.wait_ge(taken.sem, step + (tb - 1))
                w = c.ring[:, s, 0:r.kd * GW].rearrange("p (k f) -> p k f", f=GW)
                for a in range(2):
                    for k in range(r.kd):
                        part = slice(P * a, P * a + P)
                        still, moving = (r.src[:, k, part], w[:, k, 0:r.cols]) if r.tm else (w[:, k, part], r.src[:, k, :])
                        last = nc.tensor.matmul(ps[:, 2 * s + a, 0:r.cols], still, moving,
                                                start=(k == 0), stop=(k == r.kd - 1))
                last.then_inc(made.sem, 1)
            each_step(pe, multiply)

        def unload(eng):
            def one(r, s, g, step, uses):
                eng.wait_ge(made.sem, step + (mb + 1))
                r.take(g, ps[:, 2 * s:2 * s + 2, 0:r.cols]).then_inc(taken.sem, 1)
            each_step(eng, one)

        if unloader == "scalar":
            block.scalar(unload)
        else:
            block.vector(unload)
    for s in range(2):
        loaded[s].advance(16 * ((total + 1 - s) // 2))
    made.advance(total)
    taken.advance(total)


def to_fm(c, dst, func=ACT.Copy):
    return lambda g, r: c.nc.scalar.activation(dst[:, bass.ds(g * 2, 2), :], r, func)


def to_tm(c, dst, func=ACT.Copy, cols=GW):
    return lambda g, r: c.nc.scalar.activation(dst[:, :, bass.ds(g * GW, cols)], r, func)


def add_to_x(c, keep=1.0):
    def take(g, r):
        xg = c.x[:, :, bass.ds(g * GW, GW)]
        return c.nc.vector.scalar_tensor_tensor(out=xg, in0=xg, scalar=keep, in1=r, op0=ALU.mult, op1=ALU.add)
    return take


def rope_stage(c, chunks, rotation, cos, sin):
    nc, ps = c.nc, c.ps
    turned, scaled, roped = signals(c, "rope_turned", "rope_scaled", "roped")
    tb, sb, rb = turned.base, scaled.base, roped.base
    n = chunks.shape[1] // 2
    prod = [c.work[:, 512 * k:512 * k + 512].rearrange("p (a t) -> p a t", a=2) for k in range(4)]

    with nc.Block() as block:
        @block.tensor
        def _(pe):
            for k in range(n):
                if k >= 4:
                    pe.wait_ge(roped.sem, rb + k - 3)
                nc.tensor.matmul(ps[:, k % 4, :], rotation, chunks[:, 2 * k:2 * k + 2, :].rearrange("p a t -> p (a t)"),
                                 start=True, stop=True).then_inc(turned.sem, 1)

        @block.gpsimd
        def _(pool):
            for k in range(n):
                if k >= 2:
                    pool.wait_ge(roped.sem, rb + k - 1)
                nc.gpsimd.tensor_tensor(prod[k % 2], chunks[:, 2 * k:2 * k + 2, :],
                                        cos.unsqueeze(1).to_broadcast([P, 2, T]), ALU.mult).then_inc(scaled.sem, 1)

        @block.vector
        def _(dve):
            for k in range(n):
                dve.wait_ge(turned.sem, tb + k + 1)
                c.vchain(dve, nc.vector.tensor_tensor(prod[2 + k % 2], ps[:, k % 4, :].rearrange("p (a t) -> p a t", a=2),
                                                      sin.unsqueeze(1).to_broadcast([P, 2, T]), ALU.mult))
                dve.wait_ge(scaled.sem, sb + k + 1)
                nc.vector.tensor_tensor(chunks[:, 2 * k:2 * k + 2, :], prod[k % 2], prod[2 + k % 2],
                                        ALU.add).then_inc(roped.sem, 1)
    for s in (turned, scaled, roped):
        s.advance(n)


def attention_stage(c, groups, scale):
    nc, ps = c.nc, c.ps
    scored, biased, exped, factored, weighted, turned, turned_taken, attended, output = signals(
        c, "scored", "biased", "exped", "factored", "weighted", "probs_turned", "turned_taken", "attended",
        "output_taken")
    zb, bb, eb, fb, wb, tb, kb, ab, ob = (s.base for s in (scored, biased, exped, factored, weighted, turned,
                                                           turned_taken, attended, output))
    passes = []
    for gi, (members, _) in enumerate(groups):
        slab = 0
        for m in members:
            passes.append((m, gi, slab, m is members[-1]))
            slab += len(m.v)
    N = len(passes)
    S = [c.work[:, 1024 * b:1024 * b + 1024].rearrange("p (a k) -> p a k", a=4) for b in range(2)]
    turned_sb = [c.ring[:, 2 + 2 * b:4 + 2 * b, :].rearrange("p s n -> p (s n)")[:, 0:5 * 512]
                 .rearrange("p (l a q) -> p l a q", l=5, a=4) for b in range(2)]
    st = lambda b, n: c.small[:, 32 * b + 4 * n:32 * b + 4 * n + 4]

    with nc.Block() as block:
        @block.tensor
        def _(pe):
            def score(n):
                m, b = passes[n][0], n % 2
                if n >= 2:
                    pe.wait_ge(biased.sem, bb + n - 1)
                for p in range(2):
                    for j in range(2):
                        last = nc.tensor.matmul(ps[:, 2 * b + p, T * j:T * j + m.nk], m.q(p, j), m.k(p),
                                                start=True, stop=True)
                last.then_inc(scored.sem, 1)

            def turn(n):
                m, b = passes[n][0], n % 2
                pe.wait_ge(weighted.sem, wb + n + 1)
                if n:
                    pe.wait_ge(turned_taken.sem, kb + n)
                for l in range(len(m.v)):
                    w = min(P, m.nk - P * l)
                    for a in range(4):
                        last = nc.tensor.transpose(ps[0:w, 4 + l, P * a:P * a + P], S[b][:, a, P * l:P * l + w], c.ident)
                last.then_inc(turned.sem, 1)

            def attend(gi):
                members, _ = groups[gi]
                pe.wait_ge(turned_taken.sem, kb + sum(len(groups[g][0]) for g in range(gi + 1)))
                if gi >= 2:
                    pe.wait_ge(output.sem, ob + gi - 1)
                for p in range(2):
                    for j in range(2):
                        parts = [(m, l) for m in members for l in range(len(m.v))]
                        for n, (m, l) in enumerate(parts):
                            w = min(P, m.nk - P * l)
                            last = nc.tensor.matmul(ps[HD * p:HD * p + HD, 6 + gi % 2, P * j:P * j + P], m.v[l],
                                                    turned_sb[gi % 2][0:w, n, 2 * p + j, :],
                                                    start=(n == 0), stop=(n == len(parts) - 1))
                last.then_inc(attended.sem, 1)

            score(0)
            if N > 1:
                score(1)
            for n in range(N):
                turn(n)
                if n + 2 < N:
                    score(n + 2)
                if passes[n][3]:
                    attend(passes[n][1])

        @block.vector
        def _(dve):
            link = lambda ins: c.vchain(dve, ins)

            def bias(n):
                m, b = passes[n][0], n % 2
                dve.wait_ge(scored.sem, zb + n + 1)
                if n >= 2:
                    dve.wait_ge(turned.sem, tb + n - 1)
                src = ps[:, 2 * b:2 * b + 2, :].rearrange("p h (j k) -> p (h j) k", j=2)[:, :, 0:m.nk]
                link(nc.vector.tensor_tensor(S[b][:, :, 0:m.nk], src, m.mask.unsqueeze(1).to_broadcast([P, 4, m.nk]),
                                             ALU.add))
                link(nc.vector.tensor_reduce(st(b, 0), S[b][:, :, 0:m.nk], axis=AX.X, op=ALU.max))
                if m.sinks is None:
                    nc.vector.tensor_scalar(st(b, 1), st(b, 0), -scale, None, ALU.mult).then_inc(biased.sem, 1)
                else:
                    link(nc.vector.scalar_tensor_tensor(out=st(b, 0), in0=st(b, 0), scalar=scale, in1=m.sinks,
                                                        op0=ALU.mult, op1=ALU.max))
                    link(nc.vector.tensor_scalar(st(b, 1), st(b, 0), -1.0, None, ALU.mult))
                    nc.vector.tensor_tensor(st(b, 2), m.sinks, st(b, 0), ALU.subtract).then_inc(biased.sem, 1)

            def factor(n):
                m, b = passes[n][0], n % 2
                dve.wait_ge(exped.sem, eb + n + 1)
                if m.sinks is not None:
                    link(nc.vector.tensor_tensor(st(b, 4), st(b, 4), st(b, 3), ALU.add))
                ins = nc.vector.reciprocal(st(b, 5), st(b, 4))
                if m.gates is not None:
                    link(ins)
                    ins = nc.vector.tensor_tensor(st(b, 5).rearrange("p (h j) -> p h j", h=2),
                                                  st(b, 5).rearrange("p (h j) -> p h j", h=2), m.gates, ALU.mult)
                if m.valid is not None:
                    link(ins)
                    ins = nc.vector.tensor_scalar(st(b, 5), st(b, 5), m.valid, None, ALU.mult)
                ins.then_inc(factored.sem, 1)

            bias(0)
            for n in range(N):
                if n + 1 < N:
                    bias(n + 1)
                factor(n)

        @block.scalar
        def _(act):
            def exps(n):
                m, b = passes[n][0], n % 2
                act.wait_ge(biased.sem, bb + n + 1)
                if m.sinks is not None:
                    nc.scalar.activation(st(b, 3), st(b, 2), ACT.Exp)
                for a in range(4):
                    last = nc.scalar.activation(S[b][:, a, 0:m.nk], S[b][:, a, 0:m.nk], ACT.Exp, bias=st(b, 1)[:, a:a + 1],
                                                scale=scale, accum_out=st(b, 4)[:, a:a + 1])
                last.then_inc(exped.sem, 1)

            def take_turned(n):
                m, gi, slab, _ = passes[n]
                act.wait_ge(turned.sem, tb + n + 1)
                if gi >= 2:
                    act.wait_ge(attended.sem, ab + gi - 1)
                for l in range(len(m.v)):
                    w = min(P, m.nk - P * l)
                    last = nc.scalar.activation(turned_sb[gi % 2][0:w, slab + l, :, :].rearrange("p a q -> p (a q)"),
                                                ps[0:w, 4 + l, :], ACT.Copy)
                last.then_inc(turned_taken.sem, 1)

            def take_output(gi):
                act.wait_ge(attended.sem, ab + gi + 1)
                nc.scalar.activation(groups[gi][1], ps[:, 6 + gi % 2, 0:T].rearrange("p (j q) -> p j q", j=2),
                                     ACT.Copy).then_inc(output.sem, 1)

            exps(0)
            for n in range(N):
                if n + 1 < N:
                    exps(n + 1)
                take_turned(n)
                if passes[n][3]:
                    take_output(passes[n][1])

        @block.gpsimd
        def _(pool):
            for n in range(N):
                m, b = passes[n][0], n % 2
                pool.wait_ge(factored.sem, fb + n + 1)
                nc.gpsimd.tensor_tensor(S[b][:, :, 0:m.nk], S[b][:, :, 0:m.nk],
                                        st(b, 5).unsqueeze(2).to_broadcast([P, 4, m.nk]), ALU.mult)\
                    .then_inc(weighted.sem, 1)
    for s in (scored, biased, exped, factored, weighted, turned, turned_taken):
        s.advance(N)
    attended.advance(len(groups))
    output.advance(len(groups))


CMP_LEN, CMP_STRIDE = 32, 16
NCMP = (T - CMP_LEN) // CMP_STRIDE + 1


def load_stage(c, loads):
    nc = c.nc
    first, = signals(c, "tables_loaded")
    with nc.Block() as block:
        @block.sync
        def _(sp):
            for dst, src in loads:
                sp.dma_start(dst, src).then_inc(first.sem, 16)
            sp.wait_ge(first.sem, first.base + 16 * len(loads))
    first.advance(16 * len(loads))


def gmlp_stage(c, u, v, out, wT, bias, causal):
    nc, ps = c.nc, c.ps
    H = 8
    var_made, root_made, normed, mixed = signals(c, "gm_var_made", "gm_root_made", "gm_normed", "gm_mixed")
    vh = v.rearrange("p t (h d) -> p t h d", h=H)
    sq = c.work[:, 0:TT * H * HD].rearrange("p (t n) -> p t n", t=TT)
    sqh = sq.rearrange("p t (h d) -> p t h d", h=H)
    st = lambda n: c.small[:, 16 * n:16 * n + 16]
    with nc.Block() as block:
        @block.vector
        def _(dve):
            link = lambda ins: c.vchain(dve, ins)
            link(nc.vector.tensor_tensor(wT, wT, causal.unsqueeze(1).to_broadcast([P, H, P]), ALU.mult))
            link(nc.vector.tensor_reduce(st(0).rearrange("p (t h) -> p t h", t=TT), vh, axis=AX.X, op=ALU.add))
            link(nc.vector.tensor_scalar(st(0), st(0), 1.0 / HD, None, ALU.mult))
            for t in range(TT):
                link(nc.vector.tensor_tensor(vh[:, t], vh[:, t], st(0)[:, H * t:H * t + H].unsqueeze(2)
                                             .to_broadcast([P, H, HD]), ALU.subtract))
            link(nc.vector.tensor_tensor(sq, v, v, ALU.mult))
            link(nc.vector.tensor_reduce(st(1), sq.rearrange("p t (h d) -> p (t h) d", h=H), axis=AX.X, op=ALU.add))
            nc.vector.tensor_scalar(st(1), st(1), 1.0 / HD, LN_EPS, ALU.mult, ALU.add).then_inc(var_made.sem, 1)
            dve.wait_ge(root_made.sem, root_made.base + 1)
            link(nc.vector.reciprocal(st(3), st(2)))
            for t in range(TT):
                nc.vector.tensor_tensor(vh[:, t], vh[:, t], st(3)[:, H * t:H * t + H].unsqueeze(2)
                                        .to_broadcast([P, H, HD]), ALU.mult).then_inc(normed.sem, 1)
            for b in range(2):
                dve.wait_ge(mixed.sem, mixed.base + b + 1)
                spread = sq.rearrange("p t n -> p (t n)")[:, 512 * b:512 * b + 512].rearrange("p (j t) -> p j t", j=2)
                link(nc.vector.tensor_tensor(spread, ps[:, b, :].rearrange("p (j t) -> p j t", j=2),
                                             bias[:, 2 * b:2 * b + 2, :], ALU.add))
                link(nc.vector.tensor_tensor(out[:, 2 * b:2 * b + 2, :], spread, u[:, 2 * b:2 * b + 2, :], ALU.mult))

        @block.scalar
        def _(act):
            act.wait_ge(var_made.sem, var_made.base + 1)
            nc.scalar.activation(st(2), st(1), ACT.Sqrt).then_inc(root_made.sem, 1)

        @block.tensor
        def _(pe):
            pe.wait_ge(normed.sem, normed.base + TT)
            for b in range(2):
                for h in range(4 * b, 4 * b + 4):
                    for t in range(TT):
                        at = T * (h // 2 % 2) + P * t
                        last = nc.tensor.matmul(ps[HD * (h % 2):HD * (h % 2) + HD, b, at:at + P],
                                                v[:, t, HD * h:HD * h + HD], wT[:, h, :], start=True, stop=True)
                last.then_inc(mixed.sem, 1)
    var_made.advance(1)
    root_made.advance(1)
    normed.advance(TT)
    mixed.advance(2)


def compress_stage(c, kv, w1, w2, pe_cols, cos, sin, kT, vT):
    nc, ps = c.nc, c.ps
    hid_made, pe_made, pe_taken, gelued, second, ready, flipped = signals(
        c, "cmp_hidden", "cmp_pe_made", "cmp_pe_taken", "cmp_gelued", "cmp_second", "cmp_rotated", "cmp_flipped")
    h1 = c.work[0:HD, 0:4 * 16].rearrange("p (a n) -> p a n", a=4)
    peb = c.work[0:HD, 64:66]
    kc = c.work[0:NCMP, 128:256].rearrange("p (g h d) -> p g h d", g=2, h=2)
    rot = c.work[0:NCMP, 256:512].rearrange("p (g u h d) -> p g u h d", g=2, u=2, h=2)
    tmp = c.work[0:NCMP, 512:640].rearrange("p (n g d) -> p n g d", n=2, g=2)
    with nc.Block() as block:
        @block.tensor
        def _(pe):
            for m in range(2):
                for l in range(CMP_LEN):
                    last = nc.tensor.matmul(ps[0:HD, 4 + m, 0:1], w1[0:HD, m, l, :], pe_cols[0:HD, m, l:l + 1],
                                            start=(l == 0), stop=(l == CMP_LEN - 1))
            last.then_inc(pe_made.sem, 1)
            for m in range(2):
                for g in range(2):
                    at = slice(HD * g, HD * g + HD)
                    for l in range(CMP_LEN):
                        last = nc.tensor.matmul(ps[0:HD, 2 * m + g, 0:NCMP], w1[at, m, l, :],
                                                kv[at, m, l:l + CMP_STRIDE * (NCMP - 1) + 1:CMP_STRIDE],
                                                start=(l == 0), stop=(l == CMP_LEN - 1))
            last.then_inc(hid_made.sem, 1)
            pe.wait_ge(gelued.sem, gelued.base + 1)
            for m in range(2):
                for g in range(2):
                    last = nc.tensor.matmul(ps[0:NCMP, 6 + m, HD * g:HD * g + HD], h1[:, 2 * m + g, 0:NCMP],
                                            w2[0:HD, m, :], start=True, stop=True)
            last.then_inc(second.sem, 1)
            pe.wait_ge(ready.sem, ready.base + 1)
            for g in range(2):
                last = nc.tensor.transpose(ps[:, 4, 16 * g:16 * g + NCMP], rot[:, g].rearrange("p u h d -> p (u h d)"),
                                           c.ident[0:NCMP, 0:NCMP])
            last.then_inc(flipped.sem, 1)

        @block.scalar
        def _(act):
            act.wait_ge(pe_taken.sem, pe_taken.base + 1)
            act.wait_ge(hid_made.sem, hid_made.base + 1)
            for m in range(2):
                last = nc.scalar.activation(h1[:, 2 * m:2 * m + 2, 0:NCMP], ps[0:HD, 2 * m:2 * m + 2, 0:NCMP],
                                            ACT.Gelu_apprx_tanh, bias=peb[:, m:m + 1])
            last.then_inc(gelued.sem, 1)

        @block.vector
        def _(dve):
            link = lambda ins: c.vchain(dve, ins)
            dve.wait_ge(pe_made.sem, pe_made.base + 1)
            nc.vector.tensor_copy(peb, ps[0:HD, 4:6, 0:1].rearrange("p a o -> p (a o)")).then_inc(pe_taken.sem, 1)
            dve.wait_ge(second.sem, second.base + 1)
            link(nc.vector.tensor_copy(vT, ps[0:NCMP, 7, 0:128].rearrange("p (g d) -> p g d", g=2)))
            link(nc.vector.tensor_copy(kc, ps[0:NCMP, 6, 0:128].rearrange("p (g h d) -> p g h d", g=2, h=2)))
            cb = cos[0:NCMP].unsqueeze(1).to_broadcast([NCMP, 2, 32])
            sb = sin[0:NCMP].unsqueeze(1).to_broadcast([NCMP, 2, 32])
            for half, op in ((0, ALU.subtract), (1, ALU.add)):
                link(nc.vector.tensor_tensor(tmp[:, 0], kc[:, :, half, :], cb, ALU.mult))
                link(nc.vector.tensor_tensor(tmp[:, 1], kc[:, :, 1 - half, :], sb, ALU.mult))
                link(nc.vector.tensor_tensor(rot[:, :, 0, half, :], tmp[:, 0], tmp[:, 1], op))
            nc.vector.tensor_copy(rot[:, :, 1], rot[:, :, 0]).then_inc(ready.sem, 1)
            dve.wait_ge(flipped.sem, flipped.base + 1)
            link(nc.vector.tensor_copy(kT[:, :, 0:NCMP], ps[:, 4, 0:32].rearrange("p (g n) -> p g n", g=2)[:, :, 0:NCMP]))
    for s in (hid_made, pe_made, pe_taken, gelued, second, ready, flipped):
        s.advance(1)


def even_mixer(c):
    d = c.dram
    norm_stage(c, gain_fm=c.gains[:, KD:2 * KD])
    seg = c.seg
    vtm = c.vtm
    t = c.tables
    wT = t[:, 0:1024].rearrange("p (h t) -> p h t", h=8)
    bias = t[:, 1024:2048].rearrange("p (a t) -> p a t", a=4)
    causal = t[:, 2048:2176]
    w2 = t[:, 2176:2304].rearrange("p (m o) -> p m o", m=2)
    pe_cols = t[:, 2304:2368].rearrange("p (m l) -> p m l", m=2)
    rot64 = t[:, 2368:2496]
    cos, sin = t[:, 2496:2752], t[:, 2752:3008]
    ccos, csin = t[:, 3008:3040], t[:, 3040:3072]
    amask = t[:, 3072:3584].rearrange("p (t k) -> p t k", t=2)
    cmask = t[:, 3584:3616].rearrange("p (t k) -> p t k", t=2)
    valid = t[:, 3616:3618]
    kT = t[:, 3618:3650].rearrange("p (g n) -> p g n", g=2)
    vT = t[0:NCMP, 3650:3778].rearrange("p (g d) -> p g d", g=2)
    w1 = c.ring[:, 2:4, :].rearrange("p m (l o) -> p m l o", l=CMP_LEN)
    load_stage(c, [(t[:, 0:3618], d["l_even_tables"]), (c.ring[:, 2:4, :].rearrange("p m n -> p (m n)"), d["l_cmp_w1"])])
    wi = d["l_ev_in"]
    project_stage(c, [
        product(c, wi[0:2], 2, to_fm(c, seg[:, 0:4], ACT.Gelu_apprx_tanh)),
        product(c, wi[7:9], 2, to_tm(c, vtm, ACT.Gelu_apprx_tanh), tm=True),
        product(c, wi[2:7], 5, to_fm(c, seg[:, 4:14])),
        product(c, wi[9:10], 1, to_tm(c, vtm[:, :, 512:768]), tm=True),
        product(c, wi[10:11], 1, to_tm(c, vtm[:, :, 768:792], ACT.Sigmoid, cols=24), tm=True, cols=24)])
    gmlp_stage(c, seg[:, 0:4], vtm[:, :, 0:512], c.cat[:, 0:4], wT, bias, causal)
    compress_stage(c, seg[:, 12:14], w1, w2, pe_cols, ccos, csin, kT, vT)
    rope_stage(c, seg[:, 4:12], rot64, cos, sin)
    groups = []
    for g in range(2):
        for qt in range(TT):
            def q(p, j, g=g, qt=qt):
                return seg[HD * p:HD * p + HD, 4 + 2 * g + j, P * qt:P * qt + P]
            gates = vtm[:, qt, 768 + 12 * g:780 + 12 * g].rearrange("p (j h c) -> p c h j", j=2, h=2)
            nk = P * (qt + 1)
            members = [Pass(
                q=q, k=lambda p, g=g: kT[HD * p:HD * p + HD, g, 0:NCMP], nk=NCMP, v=[vT[:, g, :]],
                mask=cmask[:, qt, 0:NCMP], sinks=None, gates=gates[:, 0], valid=valid[:, qt:qt + 1])]
            for b in range(2):
                members.append(Pass(
                    q=q, k=lambda p, g=g, b=b, nk=nk: seg[HD * p:HD * p + HD, 8 + 2 * b + g, 0:nk], nk=nk,
                    v=[vtm[:, l, 512 + P * b + HD * g:512 + P * b + HD * g + HD] for l in range(qt + 1)],
                    mask=amask[:, qt, 0:nk], sinks=None, gates=gates[:, 1 + b], valid=None))
            groups.append((members, c.cat[:, 4 + 2 * g:6 + 2 * g, P * qt:P * qt + P]))
    attention_stage(c, groups, HD ** -0.5)
    project_stage(c, [product(c, d["l_ev_out"], 4, add_to_x(c), tm=True, src=c.cat)], "vector")


POOL_WINDOWS = (2, 4, 8, 16)
NT = 16
CH = 32


def pool_stage(c, z, operators, weights, scale, out):
    nc, ps = c.nc, c.ps
    pooled, taken, mixed = signals(c, "pooled", "pooled_taken", "pool_mixed")
    buf = c.work[:, 0:4 * T].rearrange("p (g t) -> p g t", g=4)
    with nc.Block() as block:
        @block.tensor
        def _(pe):
            for g in range(4):
                for t in range(TT):
                    last = nc.tensor.matmul(ps[:, g, 0:T], z[:, t, P * g:P * g + P], operators[:, g, t, :],
                                            start=(t == 0), stop=(t == TT - 1))
                last.then_inc(pooled.sem, 1)
            for g in range(4):
                pe.wait_ge(taken.sem, taken.base + g + 1)
                nc.tensor.matmul(ps[:, 4 + g, 0:T], weights[:, g, :], buf[:, g, :], start=True,
                                 stop=True).then_inc(mixed.sem, 1)

        @block.scalar
        def _(act):
            for g in range(4):
                act.wait_ge(pooled.sem, pooled.base + g + 1)
                nc.scalar.activation(buf[:, g, :], ps[:, g, 0:T], ACT.Copy).then_inc(taken.sem, 1)

        @block.vector
        def _(dve):
            for g in range(4):
                dve.wait_ge(mixed.sem, mixed.base + g + 1)
                c.vchain(dve, nc.vector.tensor_scalar(out[:, g, :], ps[:, 4 + g, 0:T], scale[:, g:g + 1], None, ALU.mult))
    for s in (pooled, taken, mixed):
        s.advance(4)


def s5_tables_stage(c, lam_re, lam_im, log_dt, c_re, c_im, decay, phases, readout):
    nc = c.nc
    V = nc.vector
    reduced, sines = signals(c, "s5_angle_reduced", "s5_sines")
    st = lambda n: c.rowbuf[:, 0, NT * n:NT * n + NT]
    dt, a, theta, k, half, sh, sn, m, cs, cm1, nr, ni, inv, cr, ci, t1, t2 = (st(n) for n in range(17))
    two_pi = 2 * np.pi
    parts = [6.28125, 0.0019340515136718750]
    parts.append(float(np.float32(two_pi - sum(parts))))
    ln2 = [0.693359375, float(np.float32(np.log(2.0) - 0.693359375))]
    big = 1.5 * 2.0 ** 23
    pi = 3.1415925
    with nc.Block() as block:
        @block.scalar
        def _(act):
            act.wait_ge(reduced.sem, reduced.base + 1)
            nc.scalar.activation(sh, half, ACT.Sin)
            nc.scalar.activation(sn, theta, ACT.Sin).then_inc(sines.sem, 1)

        @block.vector
        def _(dve):
            link = lambda ins: c.vchain(dve, ins)
            mul = lambda o, x, y: link(V.tensor_tensor(o, x, y, ALU.mult))
            add = lambda o, x, y: link(V.tensor_tensor(o, x, y, ALU.add))
            sub = lambda o, x, y: link(V.tensor_tensor(o, x, y, ALU.subtract))
            fma = lambda o, x, s, y: link(V.scalar_tensor_tensor(out=o, in0=x, scalar=s, in1=y, op0=ALU.mult, op1=ALU.add))

            def round_to(o, x, s):
                link(V.tensor_scalar(o, x, float(s), None, ALU.mult))
                link(V.tensor_scalar(o, o, big, None, ALU.add))
                link(V.tensor_scalar(o, o, -big, None, ALU.add))

            round_to(k, log_dt, 1 / np.log(2.0))
            link(V.tensor_scalar(a, log_dt, 1.0, None, ALU.mult))
            for part in ln2:
                fma(a, k, -part, a)
            link(V.memset(dt, 1.0))
            for n in range(9, 0, -1):
                mul(dt, dt, a)
                link(V.tensor_scalar(dt, dt, 1.0 / n, 1.0, ALU.mult, ALU.add))
            link(V.tensor_scalar(k, k, -127.0, 128.0, ALU.max, ALU.min))
            link(V.tensor_scalar(t1.bitcast(mybir.dt.int32), k, 127.0, 2.0 ** 23, ALU.add, ALU.mult))
            mul(dt, dt, t1)
            mul(theta, lam_im, dt)
            round_to(k, theta, 1 / two_pi)
            for part in parts:
                fma(theta, k, -part, theta)
            link(V.tensor_scalar(theta, theta, -pi, pi, ALU.max, ALU.min))
            V.tensor_scalar(half, theta, 0.5, None, ALU.mult).then_inc(reduced.sem, 1)
            mul(a, lam_re, dt)
            link(V.tensor_scalar(a, a, -104.0, 104.0, ALU.max, ALU.min))
            link(V.tensor_scalar(a, a, 1.0 / 128, None, ALU.mult))
            link(V.memset(m, 1.0))
            for n in range(9, 1, -1):
                mul(m, m, a)
                link(V.tensor_scalar(m, m, 1.0 / n, 1.0, ALU.mult, ALU.add))
            mul(m, m, a)
            for _ in range(7):
                link(V.scalar_tensor_tensor(out=m, in0=m, scalar=2.0, in1=m, op0=ALU.add, op1=ALU.mult))
            link(V.tensor_scalar(decay, m, 1.0, None, ALU.add))
            dve.wait_ge(sines.sem, sines.base + 1)
            mul(cm1, sh, sh)
            link(V.tensor_scalar(cm1, cm1, -2.0, None, ALU.mult))
            link(V.tensor_scalar(cs, cm1, 1.0, None, ALU.add))
            mul(nr, decay, cm1)
            add(nr, nr, m)
            mul(ni, decay, sn)
            mul(t1, lam_re, lam_re)
            mul(inv, lam_im, lam_im)
            add(inv, inv, t1)
            link(V.reciprocal(inv, inv))
            mul(cr, nr, lam_re)
            mul(t1, ni, lam_im)
            add(cr, cr, t1)
            mul(cr, cr, inv)
            mul(ci, ni, lam_re)
            mul(t1, nr, lam_im)
            sub(ci, ci, t1)
            mul(ci, ci, inv)
            out = [readout[:, n, :].rearrange("p (n c) -> p n c", n=NT) for n in range(3)]
            wide = lambda s: s.unsqueeze(2).to_broadcast([P, NT, CH])
            mul(out[0], c_re, wide(cr))
            mul(out[1], c_im, wide(ci))
            sub(out[0], out[0], out[1])
            mul(out[1], c_im, wide(cr))
            mul(out[2], c_re, wide(ci))
            link(V.scalar_tensor_tensor(out=readout[:, 2, :], in0=readout[:, 1, :], scalar=-1.0, in1=readout[:, 2, :],
                                        op0=ALU.mult, op1=ALU.subtract))
            link(V.tensor_scalar(readout[:, 1, :], readout[:, 0, :], -1.0, None, ALU.mult))
            mul(t1, cs, cs)
            mul(t2, sn, sn)
            add(t1, t1, t2)
            link(V.tensor_scalar(t1, t1, -0.5, 1.5, ALU.mult, ALU.add))
            mul(cs, cs, t1)
            mul(sn, sn, t1)
            pr, pi_ = phases[:, 0], phases[:, 1]
            link(V.memset(pr[:, :, 0:1], 1.0))
            link(V.memset(pi_[:, :, 0:1], 0.0))
            n = 1
            while n < T:
                wide = lambda s: s.unsqueeze(2).to_broadcast([P, NT, n])
                tmp = c.work[:, 0:NT * n].rearrange("p (a k) -> p a k", a=NT)
                new = slice(n, 2 * n)
                mul(pr[:, :, new], pr[:, :, 0:n], wide(cs))
                mul(tmp, pi_[:, :, 0:n], wide(sn))
                sub(pr[:, :, new], pr[:, :, new], tmp)
                mul(pi_[:, :, new], pi_[:, :, 0:n], wide(cs))
                mul(tmp, pr[:, :, 0:n], wide(sn))
                add(pi_[:, :, new], pi_[:, :, new], tmp)
                n *= 2
                mul(t1, cs, sn)
                mul(t2, sn, sn)
                mul(cs, cs, cs)
                sub(cs, cs, t2)
                link(V.tensor_scalar(sn, t1, 2.0, None, ALU.mult))
    for s in (reduced, sines):
        s.advance(1)


def s5_stage(c, u, b_in, decay, phases, readout, skip, y):
    nc, ps = c.nc, c.ps
    driven, rotated, scanned, unrotated, read, skipped = signals(
        c, "s5_driven", "s5_rotated", "s5_scanned", "s5_unrotated", "s5_read", "s5_skipped")
    two = lambda s: s.rearrange("p (r t) -> p r t", r=2)
    cosw = [two(c.work[:, 512 * b:512 * b + 512]) for b in range(2)]
    sinw = [two(c.work[:, 1024 + 512 * b:1536 + 512 * b]) for b in range(2)]
    w = [two(c.work[:, 2048 + 512 * b:2560 + 512 * b]) for b in range(2)]
    turned = [c.rowbuf[:, b, :].rearrange("p (e r t) -> p e r t", e=2, r=2) for b in range(2)]
    wide = lambda s, n: phases[:, s, n, :].unsqueeze(1).to_broadcast([P, 2, T])
    with nc.Block() as block:
        @block.tensor
        def _(pe):
            def drive(n):
                if n >= 2:
                    pe.wait_ge(rotated.sem, rotated.base + n - 1)
                at = slice(CH * (n % 4), CH * (n % 4) + CH)
                for r in range(2):
                    last = nc.tensor.matmul(ps[:, n % 2, T * r:T * r + T], b_in[at, r, n // 4, :], u[at, n // 4, :],
                                            start=True, stop=True)
                last.then_inc(driven.sem, 1)

            def readout_of(n):
                pe.wait_ge(unrotated.sem, unrotated.base + n + 1)
                cols = slice(CH * n, CH * n + CH)
                e = turned[n % 2]
                for k, (m, v) in enumerate(((0, e[:, 0, 0]), (1, e[:, 1, 1]), (2, e[:, 0, 1]), (2, e[:, 1, 0]))):
                    last = nc.tensor.matmul(ps[CH * (n % 4):CH * (n % 4) + CH, 4 + n // 4, 0:T], readout[:, m, cols], v,
                                            start=(k == 0), stop=(k == 3))
                last.then_inc(read.sem, 1)

            drive(0)
            drive(1)
            for n in range(NT):
                if n + 2 < NT:
                    drive(n + 2)
                readout_of(n)

        @block.vector
        def _(dve):
            link = lambda ins: c.vchain(dve, ins)
            for n in range(NT):
                b = n % 2
                dve.wait_ge(driven.sem, driven.base + n + 1)
                bu = two(ps[:, b, :])
                nc.vector.tensor_tensor(cosw[b], bu, wide(0, n), ALU.mult)
                ins = nc.vector.tensor_tensor(sinw[b], bu, wide(1, n), ALU.mult)
                ins.then_inc(rotated.sem, 1)
                dve.wait_ge(rotated.sem, rotated.base + n + 1)
                nc.vector.tensor_tensor(cosw[b][:, 0], cosw[b][:, 0], sinw[b][:, 1], ALU.add)
                link(nc.vector.tensor_tensor(cosw[b][:, 1], cosw[b][:, 1], sinw[b][:, 0], ALU.subtract))
                if n >= 2:
                    dve.wait_ge(unrotated.sem, unrotated.base + n - 1)
                rate = decay[:, n:n + 1].to_broadcast([P, T])
                for r in range(2):
                    last = nc.vector.tensor_tensor_scan(w[b][:, r], rate, cosw[b][:, r], 0.0, ALU.mult, ALU.add)
                last.then_inc(scanned.sem, 1)
            for m in range(4):
                dve.wait_ge(read.sem, read.base + 4 * m + 4)
                nc.vector.scalar_tensor_tensor(out=y[:, m, :], in0=u[:, m, :], scalar=skip[:, m:m + 1], in1=ps[:, 4 + m, 0:T],
                                               op0=ALU.mult, op1=ALU.add).then_inc(skipped.sem, 1)

        @block.gpsimd
        def _(pool):
            for n in range(NT):
                b = n % 2
                pool.wait_ge(scanned.sem, scanned.base + n + 1)
                if n >= 2:
                    pool.wait_ge(read.sem, read.base + n - 1)
                for e in range(2):
                    last = nc.gpsimd.tensor_tensor(turned[b][:, e], w[b], wide(e, n), ALU.mult)
                last.then_inc(unrotated.sem, 1)

        @block.scalar
        def _(act):
            act.wait_ge(skipped.sem, skipped.base + 4)
            c.achain(act, nc.scalar.activation(y, y, ACT.Gelu_apprx_tanh))
    for s in (driven, rotated, scanned, unrotated, read):
        s.advance(NT)
    skipped.advance(4)


def multiply_stage(c, out, a, b):
    with c.nc.Block() as block:
        @block.vector
        def _(dve):
            c.vchain(dve, c.nc.vector.tensor_tensor(out, a, b, ALU.mult))


def odd_mixer(c):
    d, seg, t = c.dram, c.seg, c.tables
    norm_stage(c, gain_fm=c.gains[:, 4 * KD:5 * KD])
    operators = t[:, 0:2048].rearrange("p (g t s) -> p g t s", g=4, t=TT)
    weights = t[:, 2048:2560].rearrange("p (g d) -> p g d", g=4)
    scale, skip = t[:, 2560:2564], t[:, 2564:2568]
    lam_re, lam_im, log_dt = (t[:, 2568 + NT * n:2568 + NT * n + NT] for n in range(3))
    b_in = t[:, 2616:3640].rearrange("p (r m s) -> p r m s", r=2, m=4)
    c_re, c_im = (t[:, 3640 + 512 * n:4152 + 512 * n].rearrange("p (n c) -> p n c", n=NT) for n in range(2))
    decay = t[:, 4664:4664 + NT]
    phases = c.ring[:, 2:6, :].rearrange("p s n -> p (s n)").rearrange("p (r n t) -> p r n t", r=2, n=NT)
    readout = c.vtm.rearrange("p t n -> p (t n)")[:, 0:1536].rearrange("p (m n) -> p m n", m=3)
    load_stage(c, [(t[:, 0:4664], d["l_odd_tables"])])
    zc, u, y, ab = c.vtm[:, :, 0:512], seg[:, 0:4], seg[:, 4:8], seg[:, 8:16]
    wi = d["l_od_in"]
    project_stage(c, [product(c, wi[0:2], 2, to_tm(c, zc), tm=True), product(c, wi[2:4], 2, to_fm(c, u))])
    pool_stage(c, zc, operators, weights, scale, c.cat[:, 0:4])
    s5_tables_stage(c, lam_re, lam_im, log_dt, c_re, c_im, decay, phases, readout)
    s5_stage(c, u, b_in, decay, phases, readout, skip, y)
    wg = d["l_glu"]
    project_stage(c, [product(c, wg[0:2], 2, to_fm(c, ab[:, 0:4]), src=y),
                      product(c, wg[2:4], 2, to_fm(c, ab[:, 4:8], ACT.Sigmoid), src=y)])
    multiply_stage(c, c.cat[:, 4:8], ab[:, 0:4], ab[:, 4:8])
    project_stage(c, [product(c, d["l_od_out"], 4, add_to_x(c), tm=True, src=c.cat)], "vector")


RET_HEADS = 4


def retention_stage(c, q, k, v, decay, gate, out):
    nc, ps = c.nc, c.ps
    scored, decayed, summed, kept, square_made, square_summed, rooted, scaled, gated = signals(
        c, "ret_scored", "ret_decayed", "ret_summed", "ret_kept", "ret_squared", "ret_square_summed", "ret_rooted",
        "ret_scaled", "ret_gated")
    A = [c.work[:, 512 * h:512 * h + 512].rearrange("p (s t) -> p s t", s=TT) for h in range(RET_HEADS)]
    sq = [c.work[:, 2048 + 512 * b:2560 + 512 * b].rearrange("p (j t) -> p j t", j=2) for b in range(2)]
    root = [c.work[:, 3072 + T * b:3072 + T * b + T] for b in range(2)]
    two = lambda s: s.rearrange("p (j t) -> p j t", j=2)
    with nc.Block() as block:
        @block.tensor
        def _(pe):
            def score(h):
                if h >= 2:
                    pe.wait_ge(decayed.sem, decayed.base + h - 1)
                for s in range(TT):
                    last = nc.tensor.matmul(ps[:, h % 2, T * s:T * s + T], k[:, h, P * s:P * s + P], q[:, h, :],
                                            start=True, stop=True)
                last.then_inc(scored.sem, 1)

            def combine(h):
                pe.wait_ge(decayed.sem, decayed.base + h + 1)
                if h >= 2:
                    pe.wait_ge(square_made.sem, square_made.base + h - 1)
                for j in range(2):
                    for s in range(TT):
                        at = 2 * P * h + P * j
                        last = nc.tensor.matmul(ps[:, 2 + h % 2, T * j:T * j + T], v[:, s, at:at + P], A[h][:, s, :],
                                                start=(s == 0), stop=(s == TT - 1))
                last.then_inc(summed.sem, 1)

            def square_sum(h):
                pe.wait_ge(square_made.sem, square_made.base + h + 1)
                if h >= 2:
                    pe.wait_ge(rooted.sem, rooted.base + h - 1)
                for j in range(2):
                    last = nc.tensor.matmul(ps[:, 4 + h % 2, 0:T], c.ones, sq[h % 2][:, j, :], start=(j == 0), stop=(j == 1))
                last.then_inc(square_summed.sem, 1)

            score(0)
            for h in range(RET_HEADS):
                if h + 1 < RET_HEADS:
                    score(h + 1)
                combine(h)
                if h:
                    square_sum(h - 1)
            square_sum(RET_HEADS - 1)

        @block.scalar
        def _(act):
            def root_of(h):
                act.wait_ge(square_summed.sem, square_summed.base + h + 1)
                if h >= 2:
                    act.wait_ge(scaled.sem, scaled.base + h - 1)
                nc.scalar.activation(root[h % 2], ps[:, 4 + h % 2, 0:T], ACT.Sqrt, scale=1.0 / 256,
                                     bias=c.eps[:, 0:1]).then_inc(rooted.sem, 1)

            for h in range(RET_HEADS):
                act.wait_ge(summed.sem, summed.base + h + 1)
                nc.scalar.activation(out[:, 2 * h:2 * h + 2, :], two(ps[:, 2 + h % 2, :]), ACT.Copy).then_inc(kept.sem, 1)
                if h >= 2:
                    act.wait_ge(square_summed.sem, square_summed.base + h - 1)
                nc.scalar.activation(sq[h % 2], two(ps[:, 2 + h % 2, :]), ACT.Square).then_inc(square_made.sem, 1)
                if h:
                    root_of(h - 1)
            root_of(RET_HEADS - 1)

        @block.vector
        def _(dve):
            for h in range(RET_HEADS):
                dve.wait_ge(scored.sem, scored.base + h + 1)
                nc.vector.tensor_tensor(A[h], two(ps[:, h % 2, :]), decay[:, h], ALU.mult).then_inc(decayed.sem, 1)
            for h in range(RET_HEADS):
                dve.wait_ge(rooted.sem, rooted.base + h + 1)
                c.vchain(dve, nc.vector.reciprocal(root[h % 2], root[h % 2]))
                dve.wait_ge(kept.sem, kept.base + h + 1)
                o = out[:, 2 * h:2 * h + 2, :]
                nc.vector.tensor_tensor(o, o, root[h % 2].unsqueeze(1).to_broadcast([P, 2, T]), ALU.mult)\
                    .then_inc(scaled.sem, 1)

        @block.gpsimd
        def _(pool):
            for h in range(RET_HEADS):
                pool.wait_ge(scaled.sem, scaled.base + h + 1)
                o = out[:, 2 * h:2 * h + 2, :]
                nc.gpsimd.tensor_tensor(o, o, gate[:, 2 * h:2 * h + 2, :], ALU.mult).then_inc(gated.sem, 1)
    for s in (scored, decayed, summed, kept, square_made, square_summed, rooted, scaled, gated):
        s.advance(RET_HEADS)


HG = 8
L = 32
NB = T // L


def hgrn_stage(c, q, z, v, gate, bound, rest, first_layer, norm_gain, out):
    nc, ps = c.nc, c.ps
    names = ("hg_sigmoid", "hg_bounded", "hg_logged", "hg_summed", "hg_exped", "hg_queries", "hg_keys",
             "hg_scored", "hg_turned_taken", "hg_masked", "hg_driven", "hg_drive_taken", "hg_stated", "hg_made",
             "hg_kept", "hg_square_summed", "hg_sums_taken")
    (sigmoid, bounded, logged, bsummed, exped, queries, keys, scored, turned_taken, masked, driven, drive_taken, stated,
     made, kept, square_summed, sums_taken) = signals(c, *names)
    rooted, scaled = signals(c, "hg_rooted", "hg_scaled")
    R = [c.ring[:, 2 + n, :].rearrange("p (h t) -> p h t", h=HG) for n in range(4)]
    K, E1, E2, M = R
    lo = -43.0
    st = [c.work[:, 1024 * b:1024 * b + 1024].rearrange("p (n v) -> p n v", n=NB) for b in range(2)]
    mk = [c.work[:, 2048 + T * b:2048 + T * b + T].rearrange("p (t s) -> p t s", t=TT) for b in range(2)]
    kt = [c.work[:, 2560 + T * b:2560 + T * b + T].rearrange("p (t s) -> p t s", t=TT) for b in range(2)]
    sq = [c.work[:, 3072 + T * b:3072 + T * b + T] for b in range(2)]
    drive = [c.rowbuf[:, b, :].rearrange("p (n v) -> p n v", n=NB) for b in range(2)]
    sums = K
    blocks = lambda s: s.rearrange("p (n l) -> p n l", n=NB)
    with nc.Block() as block:
        @block.scalar
        def _(act):
            for h in range(HG):
                nc.scalar.activation(K[:, h, :], z[:, h, :], ACT.Sigmoid, scale=-1.0)
                if first_layer:
                    nc.scalar.activation(E1[:, h, :], z[:, h, :], ACT.Sigmoid).then_inc(sigmoid.sem, 1)
                else:
                    nc.scalar.activation(z[:, h, :], z[:, h, :], ACT.Sigmoid).then_inc(sigmoid.sem, 1)
            for h in range(HG):
                act.wait_ge(bounded.sem, bounded.base + h + 1)
                nc.scalar.activation(E1[:, h, :] if first_layer else z[:, h, :], E1[:, h, :] if first_layer else z[:, h, :],
                                     ACT.Ln).then_inc(logged.sem, 1)
            for h in range(HG):
                act.wait_ge(bsummed.sem, bsummed.base + h + 1)
                nc.scalar.activation(E1[:, h, :], M[:, h, :], ACT.Exp)
                nc.scalar.activation(E2[:, h, :], M[:, h, :], ACT.Exp, scale=-1.0)
                nc.scalar.activation(out[:, h, :], out[:, h, :], ACT.Exp)
                nc.scalar.activation(z[:, h, :], z[:, h, :], ACT.Exp).then_inc(exped.sem, 1)

            def take_turned(h):
                act.wait_ge(scored.sem, scored.base + h + 1)
                if h >= 2:
                    act.wait_ge(driven.sem, driven.base + h - 1)
                nc.scalar.activation(kt[h % 2].rearrange("p t s -> p (t s)"), ps[:, 5, 0:T], ACT.Copy)\
                    .then_inc(turned_taken.sem, 1)

            def take_drive(h):
                act.wait_ge(driven.sem, driven.base + h + 1)
                if h >= 2:
                    act.wait_ge(stated.sem, stated.base + h - 1)
                nc.scalar.activation(drive[h % 2].rearrange("p (t n) v -> p n t v", t=TT),
                                     ps[:, 0:4, 0:T].rearrange("p n (t v) -> p n t v", t=TT), ACT.Copy)\
                    .then_inc(drive_taken.sem, 1)

            def take_output(h):
                act.wait_ge(made.sem, made.base + h + 1)
                if h >= 2:
                    act.wait_ge(square_summed.sem, square_summed.base + h - 1)
                nc.scalar.activation(out[:, h, :], ps[:, 6, 0:T], ACT.Copy)
                nc.scalar.activation(sq[h % 2], ps[:, 6, 0:T], ACT.Square).then_inc(kept.sem, 1)

            take_turned(0)
            for h in range(HG):
                take_drive(h)
                if h + 1 < HG:
                    take_turned(h + 1)
                if h:
                    take_output(h - 1)
            take_output(HG - 1)
            act.wait_ge(sums_taken.sem, sums_taken.base + HG)
            nc.scalar.activation(sums, sums, ACT.Sqrt, scale=1.0 / P, bias=c.eps[:, 0:1]).then_inc(rooted.sem, 1)

        @block.vector
        def _(dve):
            link = lambda ins: c.vchain(dve, ins)
            for h in range(HG):
                dve.wait_ge(sigmoid.sem, sigmoid.base + h + 1)
                if first_layer:
                    link(nc.vector.tensor_scalar(z[:, h, :], z[:, h, :], -lo, 0.0, ALU.add, ALU.min))
                    nc.vector.tensor_scalar(E1[:, h, :], E1[:, h, :], float(np.exp(lo)), None, ALU.max).then_inc(bounded.sem, 1)
                else:
                    nc.vector.tensor_scalar(K[:, h, :], K[:, h, :], rest[:, h:h + 1], None, ALU.mult)
                    nc.vector.tensor_scalar(z[:, h, :], z[:, h, :], rest[:, h:h + 1], bound[:, h:h + 1], ALU.mult,
                                            ALU.add).then_inc(bounded.sem, 1)
            for h in range(HG):
                dve.wait_ge(logged.sem, logged.base + h + 1)
                if first_layer:
                    link(nc.vector.tensor_tensor(z[:, h, :], z[:, h, :], E1[:, h, :], ALU.add))
                link(nc.vector.tensor_tensor_scan(z[:, h, :], c.block_reset, z[:, h, :], 0.0, ALU.mult, ALU.add))
                B = blocks(z[:, h, :])
                nc.vector.tensor_tensor(blocks(M[:, h, :]), B, B[:, :, L // 2 - 1:L // 2].to_broadcast([P, NB, L]), ALU.subtract)
                nc.vector.tensor_tensor(blocks(out[:, h, :]), B[:, :, L - 1:L].to_broadcast([P, NB, L]), B, ALU.subtract)\
                    .then_inc(bsummed.sem, 1)
            for h in range(HG):
                dve.wait_ge(exped.sem, exped.base + h + 1)
                nc.vector.tensor_tensor(E1[:, h, :], E1[:, h, :], q[:, h, :], ALU.mult)
                nc.vector.tensor_tensor(q[:, h, :], q[:, h, :], z[:, h, :], ALU.mult).then_inc(queries.sem, 1)

            def mask(h):
                dve.wait_ge(scored.sem, scored.base + h + 1)
                if h >= 2:
                    dve.wait_ge(made.sem, made.base + h - 1)
                nc.vector.tensor_tensor(mk[h % 2], ps[:, 4, 0:T].rearrange("p (t s) -> p t s", t=TT),
                                        c.block_causal.unsqueeze(1).to_broadcast([P, TT, P]), ALU.mult).then_inc(masked.sem, 1)

            def states(h):
                dve.wait_ge(drive_taken.sem, drive_taken.base + h + 1)
                if h >= 2:
                    dve.wait_ge(made.sem, made.base + h - 1)
                ins = nc.vector.tensor_copy(st[h % 2][:, 0, :], drive[h % 2][:, 0, :])
                for n in range(1, NB - 1):
                    link(ins)
                    ins = nc.vector.scalar_tensor_tensor(
                        out=st[h % 2][:, n, :], in0=st[h % 2][:, n - 1, :], scalar=z[:, h, L * n + L - 1:L * n + L],
                        in1=drive[h % 2][:, n, :], op0=ALU.mult, op1=ALU.add)
                ins.then_inc(stated.sem, 1)

            def take_sums(h):
                dve.wait_ge(square_summed.sem, square_summed.base + h + 1)
                nc.vector.tensor_copy(sums[:, h, :], ps[:, 7, 0:T]).then_inc(sums_taken.sem, 1)

            mask(0)
            for h in range(HG):
                states(h)
                if h + 1 < HG:
                    mask(h + 1)
                if h >= 2:
                    take_sums(h - 2)
            take_sums(HG - 2)
            take_sums(HG - 1)
            dve.wait_ge(rooted.sem, rooted.base + 1)
            link(nc.vector.reciprocal(sums, sums))
            for h in range(HG):
                nc.vector.scalar_tensor_tensor(out=out[:, h, :], in0=out[:, h, :], scalar=norm_gain, in1=sums[:, h, :],
                                               op0=ALU.mult, op1=ALU.mult).then_inc(scaled.sem, 1)

        @block.gpsimd
        def _(pool):
            for h in range(HG):
                pool.wait_ge(exped.sem, exped.base + h + 1)
                nc.gpsimd.tensor_tensor(E2[:, h, :], E2[:, h, :], K[:, h, :], ALU.mult)
                nc.gpsimd.tensor_tensor(out[:, h, :], out[:, h, :], K[:, h, :], ALU.mult).then_inc(keys.sem, 1)
            for h in range(HG):
                pool.wait_ge(scaled.sem, scaled.base + h + 1)
                nc.gpsimd.tensor_tensor(out[:, h, :], out[:, h, :], gate[:, h, :], ALU.mult)

        @block.tensor
        def _(pe):
            def score(h):
                pe.wait_ge(queries.sem, queries.base + h + 1)
                pe.wait_ge(keys.sem, keys.base + h + 1)
                if h:
                    pe.wait_ge(turned_taken.sem, turned_taken.base + h)
                    pe.wait_ge(masked.sem, masked.base + h)
                for t in range(TT):
                    at = slice(P * t, P * t + P)
                    nc.tensor.matmul(ps[:, 4, at], E2[:, h, at], E1[:, h, at], start=True, stop=True)
                    last = nc.tensor.transpose(ps[:, 5, at], out[:, h, at], c.ident)
                last.then_inc(scored.sem, 1)

            def drives(h):
                pe.wait_ge(turned_taken.sem, turned_taken.base + h + 1)
                if h:
                    pe.wait_ge(drive_taken.sem, drive_taken.base + h)
                for t in range(TT):
                    for n in range(4):
                        rows = slice(L * n, L * n + L)
                        last = nc.tensor.matmul(ps[:, n, P * t:P * t + P], kt[h % 2][rows, t, :],
                                                v[rows, t, P * h:P * h + P], start=True, stop=True)
                last.then_inc(driven.sem, 1)

            def output(h):
                pe.wait_ge(masked.sem, masked.base + h + 1)
                pe.wait_ge(stated.sem, stated.base + h + 1)
                if h:
                    pe.wait_ge(kept.sem, kept.base + h)
                for t in range(TT):
                    nc.tensor.matmul(ps[:, 6, P * t:P * t + P], v[:, t, P * h:P * h + P], mk[h % 2][:, t, :],
                                     start=(t == 0), stop=False, skip_group_check=True)
                for n in range(1, NB):
                    last = nc.tensor.matmul(ps[:, 6, L * n:L * n + L], st[h % 2][:, n - 1, :], q[:, h, L * n:L * n + L],
                                            start=False, stop=(n == NB - 1), skip_group_check=True)
                last.then_inc(made.sem, 1)

            def square_sum(h):
                pe.wait_ge(kept.sem, kept.base + h + 1)
                if h:
                    pe.wait_ge(sums_taken.sem, sums_taken.base + h)
                nc.tensor.matmul(ps[:, 7, 0:T], c.ones, sq[h % 2], start=True, stop=True).then_inc(square_summed.sem, 1)

            score(0)
            for h in range(HG):
                drives(h)
                if h + 1 < HG:
                    score(h + 1)
                if h:
                    output(h - 1)
                if h >= 2:
                    square_sum(h - 2)
            output(HG - 1)
            square_sum(HG - 2)
            square_sum(HG - 1)
    for s in signals(c, *names):
        s.advance(HG)
    rooted.advance(1)
    scaled.advance(HG)


ALPHA = (2.0 * 2) ** 0.25
EXPERTS = 8


def bounds_stage(c, raw, bound, rest):
    nc = c.nc
    diff_made, = signals(c, "bound_diff_made")
    with nc.Block() as block:
        @block.vector
        def _(dve):
            nc.vector.tensor_tensor(bound, raw[:, HG:2 * HG], raw[:, 0:HG], ALU.subtract).then_inc(diff_made.sem, 1)

        @block.scalar
        def _(act):
            act.wait_ge(diff_made.sem, diff_made.base + 1)
            nc.scalar.activation(rest, bound, ACT.Sigmoid, scale=-1.0).then_inc(c.achain.sem, 1)
            c.achain.n += 1
            act.wait_ge(c.achain.sem, c.achain.n)
            c.achain(act, nc.scalar.activation(bound, bound, ACT.Sigmoid))
    diff_made.advance(1)


def weigh_add_stage(c, total, part):
    with c.nc.Block() as block:
        @block.vector
        def _(dve):
            c.vchain(dve, c.nc.vector.tensor_tensor(total, total, part, ALU.add))


def gated_fm(c, dst, gate):
    return lambda g, r: c.nc.vector.tensor_tensor(dst[:, bass.ds(g * 2, 2), :], r, gate[:, bass.ds(g * 2, 2), :], ALU.mult)


def route_stage(c, router, lower, mix):
    nc, ps = c.nc, c.ps
    E = EXPERTS
    logits_made, diff_made, exp_made, mix_made, spread, = signals(
        c, "logits_made", "logit_diff_made", "logit_exp_made", "mix_made", "mix_spread")
    w = c.work
    lg = w[:, 0:2 * E].rearrange("p (t e) -> p t e", t=TT)
    gt = w[:, 64:64 + 2 * E * E].rearrange("p (t e f) -> p t e f", t=TT, e=E)
    eq = w[:, 256:256 + 2 * E * E].rearrange("p (t e f) -> p t e f", t=TT, e=E)
    rank, one, two_ = (w[:, 400 + 16 * n:416 + 16 * n].rearrange("p (t e) -> p t e", t=TT) for n in range(3))
    tmp, mx = (w[:, 448 + 16 * n:464 + 16 * n].rearrange("p (t e) -> p t e", t=TT) for n in range(2))
    s = lambda n: w[:, 500 + 2 * n:502 + 2 * n]
    with nc.Block() as block:
        @block.tensor
        def _(pe):
            for t in range(TT):
                for k in range(KD):
                    last = nc.tensor.matmul(ps[:, t, 0:E], c.hT[:, k, P * t:P * t + P], router[:, k, :], start=(k == 0),
                                            stop=(k == KD - 1))
            last.then_inc(logits_made.sem, 1)
            pe.wait_ge(mix_made.sem, mix_made.base + 1)
            for e in range(E):
                for t in range(TT):
                    at = T * (e % 2) + P * t
                    last = nc.tensor.matmul(ps[:, 4 + e // 2, at:at + P], mx[:, t, e:e + 1].to_broadcast([P, P]), c.ident,
                                            start=True, stop=True)
                if e % 2:
                    last.then_inc(spread.sem, 1)

        @block.vector
        def _(dve):
            link = lambda ins: c.vchain(dve, ins)
            V = nc.vector
            dve.wait_ge(logits_made.sem, logits_made.base + 1)
            link(V.tensor_copy(lg, ps[:, 0:TT, 0:E]))
            for t in range(TT):
                other = lg[:, t].unsqueeze(1).to_broadcast([P, E, E])
                own = lg[:, t].unsqueeze(2).to_broadcast([P, E, E])
                link(V.tensor_tensor(gt[:, t], other, own, ALU.is_gt))
                link(V.tensor_tensor(eq[:, t], other, own, ALU.is_equal))
                link(V.tensor_tensor(eq[:, t], eq[:, t], lower, ALU.mult))
                link(V.tensor_tensor(gt[:, t], gt[:, t], eq[:, t], ALU.add))
            link(V.tensor_reduce(rank, gt, axis=AX.X, op=ALU.add))
            link(V.tensor_scalar(one, rank, 0.0, None, ALU.is_equal))
            link(V.tensor_scalar(two_, rank, 1.0, None, ALU.is_equal))
            link(V.tensor_tensor(tmp, one, two_, ALU.subtract))
            link(V.tensor_tensor(tmp, tmp, lg, ALU.mult))
            link(V.tensor_reduce(s(0), tmp, axis=AX.X, op=ALU.add))
            V.tensor_scalar(s(1), s(0), -1.0, None, ALU.mult).then_inc(diff_made.sem, 1)
            dve.wait_ge(exp_made.sem, exp_made.base + 1)
            link(V.tensor_scalar(s(3), s(2), 1.0, None, ALU.add))
            link(V.reciprocal(s(4), s(3)))
            link(V.tensor_tensor(s(5), s(2), s(4), ALU.mult))
            for t in range(TT):
                link(V.tensor_scalar(tmp[:, t], two_[:, t], s(5)[:, t:t + 1], None, ALU.mult))
                ins = V.scalar_tensor_tensor(out=mx[:, t], in0=one[:, t], scalar=s(4)[:, t:t + 1], in1=tmp[:, t],
                                             op0=ALU.mult, op1=ALU.add)
                if t == 0:
                    link(ins)
            ins.then_inc(mix_made.sem, 1)
            for b in range(4):
                dve.wait_ge(spread.sem, spread.base + b + 1)
                link(V.tensor_copy(mix[:, 2 * b:2 * b + 2, :], ps[:, 4 + b, :].rearrange("p (e t) -> p e t", e=2)))

        @block.scalar
        def _(act):
            act.wait_ge(diff_made.sem, diff_made.base + 1)
            nc.scalar.activation(s(2), s(1), ACT.Exp).then_inc(exp_made.sem, 1)
    for sig in (logits_made, diff_made, exp_made, mix_made):
        sig.advance(1)
    spread.advance(4)


def second_start(c):
    d, t = c.dram, c.tables
    norm_stage(c, gain_tm=d["final_norm_w"])
    norm_stage(c, layer=(d["ln_in_g"], d["ln_in_b"]))
    second_tables(c)


def second_tables(c):
    load_stage(c, [(c.tables[:, 0:4392], c.dram["l_second_tables"])])
    bounds_stage(c, c.tables[:, 4224:4240], c.bound[:, 0:HG], c.bound[:, HG:2 * HG])


def second_layer(c, layer):
    d, seg, vtm, t = c.dram, c.seg, c.vtm, c.tables
    decay = t[:, 0:2048].rearrange("p (h s t) -> p h s t", h=RET_HEADS, s=TT)
    rot, cos, sin = t[:, 2048:2176], t[:, 2176:2432], t[:, 2432:2688]
    c.block_causal, c.block_reset = t[:, 2688:2816], t[:, 2816:3072]
    mask = t[:, 3072:3584].rearrange("p (t k) -> p t k", t=TT)
    router = t[:, 3584:3648].rearrange("p (k e) -> p k e", k=KD)
    lower = t[:, 3648:3712].rearrange("p (e f) -> p e f", e=EXPERTS)
    sinks = t[:, 3712 + 16 * layer:3728 + 16 * layer]
    hg_gain = t[:, 3744 + layer:3745 + layer]
    w, wo = d["l_w_in"][46 * layer:46 * layer + 46], d["l_outs"][16 * layer:16 * layer + 16]

    def gated(n, gate, first):
        dst = c.merged if first else seg[:, 8:16]
        project_stage(c, [product(c, wo[4 * n:4 * n + 4], 4, gated_fm(c, dst, gate), src=c.cat)], "vector")
        if not first:
            weigh_add_stage(c, c.merged, dst)

    project_stage(c, [product(c, w[0:4], 4, to_fm(c, seg[:, 0:8])), product(c, w[4:8], 4, to_tm(c, vtm), tm=True),
                      product(c, w[8:12], 4, to_fm(c, seg[:, 8:16], ACT.Silu)),
                      product(c, w[34:38], 4, to_fm(c, seg[:, 16:24], ACT.Sigmoid))])
    rope_stage(c, seg[:, 0:8], rot, cos, sin)
    retention_stage(c, seg[:, 0:4], seg[:, 4:8], vtm, decay, seg[:, 8:16], c.cat)
    gated(0, seg[:, 16:24], True)
    project_stage(c, [product(c, w[12:20], 8, to_fm(c, seg[:, 0:16])), product(c, w[20:24], 4, to_tm(c, vtm), tm=True),
                      product(c, w[24:28], 4, to_fm(c, seg[:, 16:24], ACT.Silu)),
                      product(c, w[38:42], 4, to_fm(c, seg[:, 24:32], ACT.Sigmoid))])
    hgrn_stage(c, seg[:, 0:8], seg[:, 8:16], vtm, seg[:, 16:24], c.bound[:, 0:HG], c.bound[:, HG:2 * HG], layer == 0,
               hg_gain, c.cat)
    gated(1, seg[:, 24:32], False)
    project_stage(c, [product(c, w[28:32], 4, to_fm(c, seg[:, 0:8])),
                      product(c, d["l_twice_sk"][2 * layer:2 * layer + 2], 2, to_fm(c, seg[:, 16:20])),
                      product(c, w[33:34], 1, to_tm(c, vtm), tm=True),
                      product(c, w[42:46], 4, to_fm(c, seg[:, 24:32], ACT.Sigmoid))])
    groups = []
    for g in range(4):
        for qt in range(TT):
            nk = P * (qt + 1)
            groups.append(([Pass(
                q=lambda p, j, g=g, qt=qt: seg[HD * p:HD * p + HD, 2 * g + j, P * qt:P * qt + P],
                k=lambda p, g=g, nk=nk: seg[HD * p:HD * p + HD, 16 + g, 0:nk], nk=nk,
                v=[vtm[:, l, HD * g:HD * g + HD] for l in range(qt + 1)], mask=mask[:, qt, 0:nk],
                sinks=sinks[:, 4 * g:4 * g + 4], gates=None, valid=None)],
                c.cat[:, 2 * g:2 * g + 2, P * qt:P * qt + P]))
    attention_stage(c, groups, HD ** -0.5)
    gated(2, seg[:, 24:32], False)
    project_stage(c, [product(c, wo[12:16], 4, add_to_x(c, ALPHA), tm=True, src=c.merged)], "vector")
    norm_stage(c, layer=(d["ln_mix_g"][layer], d["ln_mix_b"][layer]))
    if layer == 0:
        ffn_stage(c, d["l_ffn2_gate"], d["l_ffn2_up"], d["l_ffn2_down"], d["l_ffn2_gate"].shape[0], keep=ALPHA, add=1.0)
    else:
        mix = seg[:, 0:8]
        route_stage(c, router, lower, mix)
        ffn_stage(c, d["l_moe_gate"], d["l_moe_up"], d["l_moe_down"], d["l_moe_gate"].shape[0] // EXPERTS, EXPERTS, mix,
                  keep=ALPHA, add=1.0)
    norm_stage(c, layer=(d["ln_ffn_g"][layer], d["ln_ffn_b"][layer]))


def start_stage(c):
    nc = c.nc
    loads = [(c.x, c.dram["x"].rearrange("o (t p) d -> p (o t) d", p=P)), (c.ident, c.dram["c_ident"]),
             (c.gains, c.dram["l_gains"])]
    first, = signals(c, "first_loaded")
    with nc.Block() as block:
        @block.sync
        def _(sp):
            for dst, src in loads:
                sp.dma_start(dst, src).then_inc(first.sem, 16)
            sp.wait_ge(first.sem, START + 16 * len(loads))

        @block.vector
        def _(dve):
            nc.vector.memset(c.zeros, 0.0)
            nc.vector.memset(c.ones, 1.0)
            nc.vector.memset(c.eps, RMS_EPS)


def end_stage(c):
    nc = c.nc
    stored, = signals(c, "stored")
    with nc.Block() as block:
        @block.sync
        def _(sp):
            sp.dma_start(c.dram["out"].rearrange("o (t p) d -> p (o t) d", p=P), c.x).then_inc(stored.sem, 16)
            sp.wait_ge(stored.sem, START + 16)


SIGNALS = ("stat_ready root_ready normed packed unloaded gains_loaded ffn_loaded0 ffn_loaded1 gate_made up_made "
           "silu_made weighed hidden_made hidden_used summed first_loaded stored vector_chain scalar_chain "
           "weights_loaded0 weights_loaded1 product_made product_taken rope_turned rope_scaled roped scored biased "
           "exped factored weighted probs_turned turned_taken attended output_taken tables_loaded gm_var_made "
           "gm_root_made gm_normed gm_mixed cmp_hidden cmp_pe_made cmp_pe_taken cmp_gelued cmp_second cmp_rotated "
           "cmp_flipped pooled pooled_taken pool_mixed s5_angle_reduced s5_sines s5_driven s5_rotated "
           "s5_scanned s5_unrotated s5_read s5_skipped ret_scored ret_decayed ret_summed ret_kept ret_squared "
           "ret_square_summed ret_rooted ret_scaled ret_gated hg_sigmoid hg_bounded hg_logged hg_summed hg_exped "
           "hg_queries hg_keys hg_scored hg_turned_taken hg_masked hg_driven hg_drive_taken hg_stated hg_made hg_kept "
           "hg_square_summed hg_sums_taken hg_rooted hg_scaled bound_diff_made logits_made logit_diff_made "
           "logit_exp_made mix_made mix_spread").split()


def allocate(c):
    nc = c.nc

    def sb(name, *shape):
        c.bytes = c.bytes + int(np.prod(shape)) * 4
        return c.stack.enter_context(nc.sbuf_tensor(name, [P, *shape], F32))[...]

    c.bytes = 0
    c.x = sb("x", TT, D)
    c.hT = sb("hT", KD, T)
    c.ring = sb("ring", 6, KD * GW)
    c.work = sb("work", 4096)
    c.rowbuf = sb("rowbuf", 2, D)
    c.small = sb("small", 64)
    c.ident = sb("ident", P)
    c.gains = sb("gains_fm", 6 * KD)
    c.zeros = sb("zeros", 512)
    c.ones = sb("ones", P)
    c.seg = sb("seg", 32, T)
    c.merged = sb("merged", KD, T)
    c.bound = sb("bound", 2 * HG)
    c.eps = sb("eps", 1)
    c.vtm = sb("vtm", TT, D)
    c.cat = sb("cat", KD, T)
    c.tables = sb("tables", 4800)
    c.ps = c.stack.enter_context(nc.psum_tensor("ps", [P, 8, 512], F32))[...]


def program(nc, dram, stages):
    with ExitStack() as stack:
        c = Core(nc, dram, stack)
        allocate(c)
        signals(c, *SIGNALS)
        c.vchain = Chain(c.sig["vector_chain"].sem)
        c.achain = Chain(c.sig["scalar_chain"].sem)
        with nc.Block() as block:
            @block.gpsimd
            def _(pool):
                for s in c.sig.values():
                    nc.gpsimd.sem_inc(s.sem, START)
        start_stage(c)
        for s in stages:
            run_stage(c, s)
        end_stage(c)


def run_stage(c, s):
    d = c.dram
    kind, *a = s
    if kind == "ffn1":
        layer, half = a
        n = 3 * layer + 2 * half
        norm_stage(c, gain_fm=c.gains[:, KD * n:KD * n + KD])
        i = 2 * layer + half
        g = d["l_ffn_gate"].shape[0] // 4
        ffn_stage(c, *(d[w][i * g:(i + 1) * g] for w in ("l_ffn_gate", "l_ffn_up", "l_ffn_down")), g)
    if kind == "even":
        even_mixer(c)
    if kind == "odd":
        odd_mixer(c)
    if kind == "second":
        second_start(c)
    if kind == "tables":
        second_tables(c)
    if kind == "ln":
        norm_stage(c, layer=(d["ln_in_g"], d["ln_in_b"]))
    if kind == "layer":
        second_layer(c, *a)


def pack_in(w):
    k, n = w.shape
    return np.ascontiguousarray(w.reshape(k // P, P, n // GW, GW).transpose(2, 1, 0, 3)).reshape(n // GW, P, -1)


def pack_down(w):
    f, n = w.shape
    return np.ascontiguousarray(w.reshape(f // GW, 2, P, n).transpose(0, 2, 1, 3)).reshape(f // GW, P, -1)


def columns(v):
    return np.ascontiguousarray(v.reshape(-1, P).T)


def layout(i):
    i = {k: np.asarray(v) for k, v in i.items()}
    a = {"x": i["x"]}
    a["c_ident"] = np.eye(P, dtype=np.float32)
    a["l_gains"] = columns(i["norm_w"])
    a["l_ffn_gate"] = np.concatenate([pack_in(w) for l in i["ffn_w_gate"] for w in l])
    a["l_ffn_up"] = np.concatenate([pack_in(w) for l in i["ffn_w_up"] for w in l])
    a["l_ffn_down"] = np.concatenate([pack_down(w) for l in i["ffn_w_down"] for w in l])
    even_layout(i, a)
    odd_layout(i, a)
    second_layout(i, a)
    return a


def rope_tables(pos, half, steps):
    inv = (np.float32(10000.0) ** -steps).astype(np.float32)
    ang = (pos.astype(np.float32)[:, None] * inv[None, :]).astype(np.float32)
    return np.cos(ang).astype(np.float32), np.sin(ang).astype(np.float32)


def rotation(width):
    r, h = np.zeros((P, P), np.float32), width // 2
    for o in range(0, P, width):
        for n in range(h):
            r[o + h + n, o + n] = -1.0
            r[o + n, o + h + n] = 1.0
    return r


def even_layout(i, a):
    w = i["ev_w_in"][0]
    cut = np.cumsum([0, 512, 512, 512, 128, 128, 128, 128, 128, 128, 24])
    u, v, q, kc, vc, ks, vs, kw, vw, gl = (w[:, cut[n]:cut[n + 1]] for n in range(10))
    twice = lambda k: [k[:, 0:64], k[:, 0:64], k[:, 64:128], k[:, 64:128]]
    a["l_ev_in"] = pack_in(np.concatenate(
        [u, q, *twice(ks), *twice(kw), kc, vc, v, vs, vw, gl, np.zeros((D, GW - 24), np.float32)], axis=1))
    a["l_ev_out"] = pack_in(i["ev_w_out"][0])
    t = np.arange(T)
    qt = t.reshape(TT, P).T
    wT = i["gm_w_s"][0].transpose(2, 0, 1).reshape(P, -1)
    b = i["gm_b"][0]
    bias = np.repeat(np.tile(b, (1, TT)).reshape(4, 2, T), HD, axis=1).transpose(1, 0, 2).reshape(P, -1)
    causal = (np.arange(P)[:, None] <= np.arange(P)[None, :]).astype(np.float32)
    w2 = np.tile(i["nsa_cmp_w2"][0].transpose(1, 0, 2).reshape(HD, -1), (2, 1))
    pe = np.tile(i["nsa_cmp_pe"][0].transpose(2, 0, 1).reshape(HD, -1), (2, 1))
    steps = np.arange(32, dtype=np.float32) / 32
    cos, sin = rope_tables(t, 32, steps)
    fm = lambda m: np.tile(m.T, (4, 1))
    end = np.arange(NCMP) * CMP_STRIDE + CMP_LEN - 1
    cc, cs = rope_tables(end, 32, steps)
    pad = lambda m: np.concatenate([m, np.zeros((P - NCMP, 32), np.float32)])
    amask = np.where(t[None, None, :] <= qt[:, :, None], 0.0, NEG).astype(np.float32)
    cm = np.where(end[None, None, :] <= qt[:, :, None], 0.0, NEG).astype(np.float32)
    cmask = np.concatenate([cm, np.full((P, TT, 1), NEG, np.float32)], axis=2)
    valid = (qt >= end[0]).astype(np.float32)
    a["l_even_tables"] = np.concatenate(
        [wT, bias, causal, w2, pe, rotation(64), fm(cos), fm(sin), pad(cc), pad(cs), amask.reshape(P, -1),
         cmask.reshape(P, -1), valid], axis=1).astype(np.float32)
    a["l_cmp_w1"] = np.tile(i["nsa_cmp_w1"][0].reshape(2, CMP_LEN, HD, HD).transpose(2, 0, 1, 3).reshape(HD, -1), (2, 1))


def odd_layout(i, a):
    a["l_od_in"], a["l_od_out"], a["l_glu"] = (pack_in(i[n][0]) for n in ("od_w_in", "od_w_out", "s5_w_glu"))
    t = np.arange(T)
    ops = []
    for w in POOL_WINDOWS:
        seen = (t[:, None] <= t[None, :]) & (t[:, None] > t[None, :] - w)
        ops.append(seen / np.minimum(t + 1, w)[None, :] - np.eye(T))
    ops = np.stack(ops).astype(np.float32).reshape(4, TT, P, T).transpose(2, 0, 1, 3).reshape(P, -1)
    pw = i["pool_w"][0].transpose(1, 0, 2).reshape(P, -1)
    dt = np.repeat(i["s5_log_dt"][0], 64)
    b_in = np.zeros((2, 4, 4, 2, 16, 2, 64), np.float32)
    c_out = np.zeros((2, NT, 2, 64, 2, 16), np.float32)
    for n, (b, o) in enumerate(((i["s5_b_re"][0], i["s5_c_re"][0]), (i["s5_b_im"][0], i["s5_c_im"][0]))):
        for g in range(2):
            b_in[n, :, :, g, :, g, :] = b.reshape(4, 4, 2, 64, 16)[:, :, g].transpose(0, 1, 3, 2)
            c_out[n, :, g, :, g, :] = o.reshape(NT, 2, 16, 64)[:, g].transpose(0, 2, 1)
    b_in = b_in.reshape(2, 4, P, P).transpose(2, 0, 1, 3).reshape(P, -1)
    c_out = c_out.reshape(2, NT, P, CH).transpose(2, 0, 1, 3).reshape(P, -1)
    a["l_odd_tables"] = np.concatenate(
        [ops, pw, columns(i["pool_scale"]), columns(i["s5_d"]), columns(i["s5_lam_re"]), columns(i["s5_lam_im"]),
         columns(dt), b_in, c_out], axis=1)


def second_layout(i, a):
    for n in ("ln_in_g", "ln_in_b", "ln_mix_g", "ln_mix_b", "ln_ffn_g", "ln_ffn_b"):
        a[n] = i[n + "_2"]
    a["final_norm_w"] = i["final_norm_w"]
    w = i["w_in_2"]
    a["l_w_in"] = np.concatenate([pack_in(m) for m in w])
    sk = w[:, :, 8192:8448]
    a["l_twice_sk"] = np.concatenate([pack_in(np.repeat(m.reshape(D, 4, 1, HD), 2, axis=2).reshape(D, -1)) for m in sk])
    a["l_outs"] = np.concatenate([pack_in(i[n][l]) for l in range(2)
                                  for n in ("ret_w_out_2", "hgrn_w_out_2", "swa_w_out_2", "w_o_2")])
    a["l_ffn2_gate"], a["l_ffn2_up"] = pack_in(i["ffn_w_gate_2"][0]), pack_in(i["ffn_w_up_2"][0])
    a["l_ffn2_down"] = pack_down(i["ffn_w_down_2"][0])
    if "moe_w_gate_2" in i:
        a["l_moe_gate"] = np.concatenate([pack_in(m) for m in i["moe_w_gate_2"][0]])
        a["l_moe_up"] = np.concatenate([pack_in(m) for m in i["moe_w_up_2"][0]])
        a["l_moe_down"] = np.concatenate([pack_down(m) for m in i["moe_w_down_2"][0]])
    t = np.arange(T)
    gap = t[None, :] - t[:, None]
    gamma = 1.0 - 2.0 ** (-5.0 - np.arange(RET_HEADS))
    dec = np.where(gap >= 0, gamma[:, None, None] ** np.maximum(gap, 0), 0.0) * P ** -0.5
    dec = dec.reshape(RET_HEADS, TT, P, T).transpose(2, 0, 1, 3).reshape(P, -1)
    cos, sin = rope_tables(t, 64, np.linspace(0.0, 1.0, 64, dtype=np.float32))
    fm = lambda m: np.tile(m.T, (2, 1))
    p = np.arange(P)
    causal = (p[:, None] <= p[None, :]) & (p[:, None] // L == p[None, :] // L)
    reset = np.broadcast_to(t % L != 0, (P, T))
    chunk = np.arange(T) // 64
    qc = chunk.reshape(TT, P).T[:, :, None]
    mask = np.where((chunk <= qc) & (chunk >= qc - 2), 0.0, NEG).reshape(P, -1)
    router = i["moe_router_2"][0].reshape(KD, P, EXPERTS).transpose(1, 0, 2).reshape(P, -1)
    e = np.arange(EXPERTS)
    lower = np.broadcast_to((e[None, :] < e[:, None]).reshape(1, -1), (P, EXPERTS ** 2))
    sinks = np.broadcast_to(i["swa_sinks_2"].reshape(2, 4, 2, 2).transpose(0, 1, 3, 2).reshape(1, -1), (P, 32))
    gain = i["hgrn_norm_g_2"].T
    fill = np.zeros((P, 4224 - 3746))
    raw = columns(i["hgrn_lower_bounds_2"])
    a["l_second_tables"] = np.concatenate(
        [dec, rotation(P), fm(cos), fm(sin), causal, reset, mask, router, lower, sinks, gain, fill, raw,
         np.zeros((P, 4392 - 4240))], axis=1).astype(np.float32)


STAGES = [("ffn1", 0, 0), ("even",), ("ffn1", 0, 1), ("ffn1", 1, 0), ("odd",), ("ffn1", 1, 1), ("second",),
          ("layer", 0), ("layer", 1)]


def build(nc, arrays):
    dram = {n: nc.dram_tensor("in_" + n, v.shape, F32, kind="ExternalInput").ap() for n, v in arrays.items()}
    dram["out"] = nc.dram_tensor("out", (1, T, D), F32, kind="ExternalOutput").ap()
    program(nc, dram, STAGES)


def kernel(**inputs):
    import concourse.bacc as bacc
    from concourse.bass_utils import run_bass_kernel_spmd as run

    arrays = layout(inputs)
    nc = bacc.Bacc("TRN2", target_bir_lowering=False, num_devices=1)
    build(nc, arrays)
    r = run(nc, [{"in_" + n: v for n, v in arrays.items()}], core_ids=[0])
    return r.results[0]["out"]
```

```python
from contextlib import ExitStack

import numpy as np
import concourse.bass as bass
from concourse import mybir

F32 = mybir.dt.float32
ALU = mybir.AluOpType
ACT = mybir.ActivationFunctionType
AX = mybir.AxisListType

P = 128
T = 256
D = 1024
TT = T // P
KD = D // P
GW = 256
HD = 64
START = 8
RMS_EPS = 1e-6
LN_EPS = 1e-5
NEG = -1e30


class Core:

    def __init__(self, nc, dram, stack):
        self.nc, self.dram, self.stack, self.sig = nc, dram, stack, {}
        self.condition = None


class Product:

    def __init__(self, w, groups, take, tm, src, cols, kd):
        self.w, self.groups, self.take, self.tm, self.src, self.cols, self.kd = w, groups, take, tm, src, cols, kd


class Pass:

    def __init__(self, q, k, nk, v, mask, sinks, gates, valid):
        self.q, self.k, self.nk, self.v = q, k, nk, v
        self.mask, self.sinks, self.gates, self.valid = mask, sinks, gates, valid


class Signal:

    def __init__(self, sem):
        self.sem, self.base = sem, START

    def advance(self, n):
        self.base += n


class Chain:

    def __init__(self, sem):
        self.sem, self.n = sem, START

    def __call__(self, eng, ins):
        self.n += 1
        ins.then_inc(self.sem, 1)
        eng.wait_ge(self.sem, self.n)


def when(c):
    def wrap(body):
        if c.condition is None:
            return body

        def guarded(eng):
            with eng.If(c.condition(eng.value_load(c.most, min_val=0, max_val=T))):
                body(eng)
        return guarded
    return wrap


def signals(c, *names):
    for n in names:
        if n not in c.sig:
            c.sig[n] = Signal(c.stack.enter_context(c.nc.semaphore(n)))
    return [c.sig[n] for n in names]


def norm_stage(c, gain_fm=None, gain_tm=None, layer=None):
    nc, x, hT, ps = c.nc, c.x, c.hT, c.ps
    stat_ready, root_ready, normed, packed, unloaded, gains = signals(
        c, "stat_ready", "root_ready", "normed", "packed", "unloaded", "gains_loaded")
    high, = signals(c, "input_high")
    b0, r0, n0, p0, u0, g0 = (s.base for s in (stat_ready, root_ready, normed, packed, unloaded, gains))
    inplace = gain_fm is None
    c.parts_of_hT = True
    xs = x if inplace else c.work.rearrange("p (t d) -> p t d", t=TT)[:, :, 0:D]
    rows = [gain_tm] if gain_tm is not None else (list(layer) if layer else [])

    with nc.Block() as block:
        @block.sync
        def _(sp):
            for n, row in enumerate(rows):
                sp.dma_start(c.rowbuf[:, n, :], row.partition_broadcast(P)).then_inc(gains.sem, 16)

        @block.scalar
        def _(act):
            act.wait_ge(stat_ready.sem, b0 + 1)
            nc.scalar.activation(c.small[:, 2:4], c.small[:, 0:2], ACT.Sqrt).then_inc(root_ready.sem, 1)
            for n in range(4):
                act.wait_ge(unloaded.sem, u0 + n + 1)
                part = (slice(None), slice(4 * (n % 2), 4 * (n % 2) + 4), slice(P * (n // 2), P * (n // 2) + P))
                nc.scalar.activation(c.act_high[part], hT[part], ACT.Copy).then_inc(high.sem, 1)

        @block.vector
        def _(dve):
            link = lambda ins: c.vchain(dve, ins)
            if layer:
                for t in range(TT):
                    for h in range(2):
                        link(nc.vector.bn_stats(c.small[:, 32 + 16 * t + 6 * h:38 + 16 * t + 6 * h],
                                                x[:, t, 512 * h:512 * h + 512]))
                for t in range(TT):
                    link(nc.vector.bn_aggr(c.small[:, 16 + 2 * t:18 + 2 * t], c.small[:, 32 + 16 * t:44 + 16 * t]))
                var = c.small[:, 16:20].rearrange("p (t two) -> p t two", two=2)[:, :, 1]
                nc.vector.tensor_scalar(c.small[:, 0:2], var, LN_EPS, None, ALU.add).then_inc(stat_ready.sem, 1)
            else:
                for t in range(TT):
                    link(nc.vector.tensor_tensor_reduce(
                        out=c.work[:, 0:D], in0=x[:, t, :], in1=x[:, t, :], scale=1.0, scalar=0.0,
                        op0=ALU.mult, op1=ALU.add, accum_out=c.small[:, 4 + t:5 + t]))
                nc.vector.tensor_scalar(c.small[:, 0:2], c.small[:, 4:6], 1.0 / D, RMS_EPS,
                                        ALU.mult, ALU.add).then_inc(stat_ready.sem, 1)
            dve.wait_ge(root_ready.sem, r0 + 1)
            link(nc.vector.reciprocal(c.small[:, 6:8], c.small[:, 2:4]))
            if rows:
                dve.wait_ge(gains.sem, g0 + 16 * len(rows))
            for t in range(TT):
                if layer:
                    link(nc.vector.tensor_scalar(xs[:, t, :], x[:, t, :], c.small[:, 16 + 2 * t:17 + 2 * t],
                                                 c.small[:, 6 + t:7 + t], ALU.subtract, ALU.mult))
                    link(nc.vector.tensor_tensor(xs[:, t, :], xs[:, t, :], c.rowbuf[:, 0, :], ALU.mult))
                    nc.vector.tensor_tensor(xs[:, t, :], xs[:, t, :], c.rowbuf[:, 1, :],
                                            ALU.add).then_inc(normed.sem, 1)
                elif gain_tm is not None:
                    nc.vector.scalar_tensor_tensor(
                        out=xs[:, t, :], in0=x[:, t, :], scalar=c.small[:, 6 + t:7 + t], in1=c.rowbuf[:, 0, :],
                        op0=ALU.mult, op1=ALU.mult).then_inc(normed.sem, 1)
                else:
                    nc.vector.tensor_scalar(xs[:, t, :], x[:, t, :], c.small[:, 6 + t:7 + t], None,
                                            ALU.mult).then_inc(normed.sem, 1)
            for n in range(4):
                t, q = n // 2, n % 2
                dve.wait_ge(packed.sem, p0 + n + 1)
                src = ps[:, n, :].rearrange("p (k f) -> p k f", k=4)
                dst = hT[:, 4 * q:4 * q + 4, P * t:P * t + P]
                if gain_fm is not None:
                    g = gain_fm[:, 4 * q:4 * q + 4].unsqueeze(2).to_broadcast([P, 4, P])
                    nc.vector.tensor_tensor(dst, src, g, ALU.mult).then_inc(unloaded.sem, 1)
                else:
                    nc.vector.tensor_copy(dst, src).then_inc(unloaded.sem, 1)
            for n in range(4):
                part = (slice(None), slice(4 * (n % 2), 4 * (n % 2) + 4), slice(P * (n // 2), P * (n // 2) + P))
                dve.wait_ge(high.sem, high.base + n + 1)
                nc.vector.tensor_tensor(c.act_low[part], hT[part], c.act_high[part].bitcast(F32), ALU.subtract)

        @block.tensor
        def _(pe):
            for t in range(TT):
                pe.wait_ge(normed.sem, n0 + t + 1)
                for q in range(2):
                    for k in range(4):
                        last = nc.tensor.transpose(ps[:, 2 * t + q, P * k:P * k + P],
                                                   xs[:, t, P * (4 * q + k):P * (4 * q + k) + P], c.ident)
                    last.then_inc(packed.sem, 1)
    stat_ready.advance(1)
    root_ready.advance(1)
    normed.advance(2)
    packed.advance(4)
    unloaded.advance(4)
    high.advance(4)
    gains.advance(16 * len(rows))


def ffn_stage(c, w_gate, w_up, w_down, per_expert, experts=1, mix=None, keep=1.0, add=0.5):
    nc, x, hT, ps = c.nc, c.x, c.hT, c.ps
    G = per_expert
    loaded = signals(c, "ffn_loaded0", "ffn_loaded1")
    gate_made, up_made, silu_made, weighed, hidden_made, hidden_used, summed = signals(
        c, "gate_made", "up_made", "silu_made", "weighed", "hidden_made", "hidden_used", "summed")
    steps = experts * G
    lb = [s.base for s in loaded]
    gb, pb, sb, wb, hb, hub, smb = (s.base for s in (gate_made, up_made, silu_made, weighed, hidden_made,
                                                    hidden_used, summed))
    wg = [c.slots[3 * s].rearrange("p (k f) -> p k f", k=KD) for s in range(2)]
    wu = [c.slots[3 * s + 1].rearrange("p (k f) -> p k f", k=KD) for s in range(2)]
    wd = [c.slots[3 * s + 2].rearrange("p (h n) -> p h n", h=2) for s in range(2)]
    silu = [c.work[:, T * n:T * n + T] for n in range(4)]
    mixed = [c.work[:, T * (4 + n):T * (5 + n)] for n in range(4)]
    hidden = [c.work[:, T * (8 + n):T * (9 + n)] for n in range(4)]

    def each_step(eng, body):
        if experts > 1:
            assert G % 2 == 0
            with eng.Fori(0, experts) as e:
                with eng.Fori(0, G // 2) as i:
                    for s in range(2):
                        body(s, e * (G // 2) + i, e, e * G + i * 2 + s)
        else:
            with eng.Fori(0, G // 2) as i:
                for s in range(2):
                    body(s, i, 0, i * 2 + s)
            if G % 2:
                body(0, G // 2, 0, G - 1)

    with nc.Block() as block:
        @block.sync
        @when(c)
        def _(sp):
            def load(s, pair, e, step):
                sp.wait_ge(hidden_used.sem, step * 2 + (hub - 2))
                for w, dst in ((w_gate, 3 * s), (w_up, 3 * s + 1), (w_down, 3 * s + 2)):
                    src = w[bass.ds(step, 1), :, :].rearrange("o p n -> p (o n)")
                    sp.dma_start(c.slots[dst], src).then_inc(loaded[s].sem, 16)
            each_step(sp, load)

        @block.scalar
        @when(c)
        def _(act):
            def gate(s, pair, e, step):
                for h in range(2):
                    act.wait_ge(gate_made.sem, step * 2 + (gb + h + 1))
                    act.wait_ge(hidden_made.sem, step * 2 + (hb + h - 3))
                    nc.scalar.activation(silu[2 * s + h], ps[:, 2 * h, 0:T], ACT.Silu).then_inc(silu_made.sem, 1)
            each_step(act, gate)

        @block.gpsimd
        @when(c)
        def _(pool):
            def make(s, pair, e, step):
                for h in range(2):
                    pool.wait_ge(silu_made.sem, step * 2 + (sb + h + 1))
                    pool.wait_ge(weighed.sem, step * 2 + (wb + h + 1))
                    pool.wait_ge(hidden_used.sem, step * 2 + (hub + h - 3))
                    nc.gpsimd.tensor_tensor(hidden[2 * s + h], mixed[2 * s + h], silu[2 * s + h], ALU.mult)\
                        .then_inc(hidden_made.sem, 1)
            if mix is not None:
                each_step(pool, make)

        @block.vector
        @when(c)
        def _(dve):
            def weigh(s, pair, e, step):
                for h in range(2):
                    dve.wait_ge(up_made.sem, step * 2 + (pb + h + 1))
                    dve.wait_ge(hidden_made.sem, step * 2 + (hb + h - 3))
                    m = mix[:, bass.ds(e, 1), :].rearrange("p o t -> p (o t)")
                    nc.vector.tensor_tensor(mixed[2 * s + h], ps[:, 2 * h + 1, 0:T], m, ALU.mult)\
                        .then_inc(weighed.sem, 1)

            def make(s, pair, e, step):
                for h in range(2):
                    dve.wait_ge(silu_made.sem, step * 2 + (sb + h + 1))
                    dve.wait_ge(up_made.sem, step * 2 + (pb + h + 1))
                    dve.wait_ge(hidden_used.sem, step * 2 + (hub + h - 3))
                    nc.vector.tensor_tensor(hidden[2 * s + h], silu[2 * s + h], ps[:, 2 * h + 1, 0:T], ALU.mult)\
                        .then_inc(hidden_made.sem, 1)
            each_step(dve, make if mix is None else weigh)
            dve.wait_ge(hidden_used.sem, hub + 2 * steps)
            dve.wait_ge(summed.sem, smb + 2)
            if keep != 1.0:
                for t in range(TT):
                    c.vchain(dve, nc.vector.tensor_scalar(x[:, t, :], x[:, t, :], keep, None, ALU.mult))
            for t in range(TT):
                for n in range(2):
                    xn = x[:, t, 512 * n:512 * n + 512]
                    c.vchain(dve, nc.vector.scalar_tensor_tensor(
                        out=xn, in0=ps[:, 4 + 2 * t + n, :], scalar=add, in1=xn, op0=ALU.mult, op1=ALU.add))

        @block.tensor
        @when(c)
        def _(pe):
            def down(s, h, start=False, stop=False):
                for t in range(TT):
                    for n in range(2):
                        last = nc.tensor.matmul(ps[:, 4 + 2 * t + n, :], hidden[2 * s + h][:, P * t:P * t + P],
                                                wd[s][:, h, 512 * n:512 * n + 512], start=start, stop=stop,
                                                skip_group_check=True)
                return last

            def clear(start, stop):
                for t in range(TT):
                    for n in range(2):
                        last = nc.tensor.matmul(ps[:, 4 + 2 * t + n, :], c.zeros[:, 0:P], c.zeros,
                                                start=start, stop=stop, skip_group_check=True)
                return last

            def products(s, pair, e, step):
                pe.wait_ge(loaded[s].sem, pair * 48 + (lb[s] + 48))
                for h in range(2):
                    pe.wait_ge(hidden_made.sem, step * 2 + (hb + h - 1))
                    for w, bank, made in ((wg, 2 * h, gate_made), (wu, 2 * h + 1, up_made)):
                        for k in range(KD):
                            last = nc.tensor.matmul(ps[:, bank, 0:T], w[s][:, k, P * h:P * h + P], hT[:, k, :],
                                                    start=(k == 0), stop=(k == KD - 1))
                        last.then_inc(made.sem, 1)
                for h in range(2):
                    pe.wait_ge(hidden_made.sem, step * 2 + (hb + h + 1))
                    last = down(s, h)
                    last.then_inc(hidden_used.sem, 1)
            clear(True, False).then_inc(summed.sem, 1)
            each_step(pe, products)
            clear(False, True).then_inc(summed.sem, 1)
    for s in range(2):
        n = (steps + 1 - s) // 2
        loaded[s].advance(48 * n)
    gate_made.advance(2 * steps)
    up_made.advance(2 * steps)
    silu_made.advance(2 * steps)
    if mix is not None:
        weighed.advance(2 * steps)
    hidden_made.advance(2 * steps)
    hidden_used.advance(2 * steps)
    summed.advance(2)


def split_ffn_stage(c, w_gate, w_up, w_down, keep=1.0, add=0.5):
    nc, x, ps = c.nc, c.x, c.ps
    G = w_gate.shape[0]
    assert G % 2 == 1
    UNITS = 3 * G
    loaded = signals(c, "unit_loaded0", "unit_loaded1", "unit_loaded2")
    high, low, low2, down_made, gate_made, up_made, silu_made, hidden_made, hidden_high, hidden_low, summed = signals(
        c, "unit_high", "unit_low_dve", "unit_low_pool", "s_down_made", "s_gate_made", "s_up_made", "s_silu_made",
        "s_hidden_made", "s_hidden_high", "s_hidden_low", "s_summed")
    lb = [s.base for s in loaded]
    hb, wb, vb, ub, gb, pb, sb, mb, ihb, ilb = (s.base for s in (high, low, low2, down_made, gate_made, up_made, silu_made,
                                                                hidden_made, hidden_high, hidden_low))
    acts = (c.act_high, c.act_low)
    silu = [c.work[:, T * h:T * h + T] for h in range(2)]
    hidden = [c.work[:, T * (2 + h):T * (3 + h)] for h in range(2)]
    HALF = KD * GW // 2

    class Step:

        def __init__(self, pair, odd):
            self.n, self.pair, self.odd = pair * 2 + odd, pair, odd

        def unit(self, j):
            at = 2 + 3 * self.odd + j
            return self.pair * 6 + at, at % 2, at % 3, self.pair * 2 + at // 3

    def stream(eng, start, body, end):
        start()
        with eng.Fori(0, G // 2) as i:
            for odd in range(2):
                body(Step(i, odd))
        end()

    after = Step(G // 2, 0)
    first = [(0, 0, 0, 0), (1, 1, 1, 0)]

    with nc.Block() as block:
        @block.sync
        def _(sp):
            def load(u, w, n):
                number, _, raw, _ = u
                sp.wait_ge(low.sem, number + (wb - 2))
                sp.wait_ge(low2.sem, number + (vb - 2))
                sp.dma_start(c.ring[:, raw, :], w[bass.ds(n, 1), :, :].rearrange("o p n -> p (o n)"))\
                    .then_inc(loaded[raw].sem, 16)

            def triple(t):
                load(t.unit(0), w_gate, t.n + 1)
                load(t.unit(1), w_down, t.n)
                load(t.unit(2), w_up, t.n + 1)

            stream(sp, lambda: (load(first[0], w_gate, 0), load(first[1], w_up, 0)), triple,
                   lambda: load(after.unit(0), w_down, G - 1))

        @block.scalar
        def _(act):
            def make_high(u, last_use=None, count=0):
                number, slot, raw, turn = u
                act.wait_ge(loaded[raw].sem, turn * 16 + (lb[raw] + 16))
                if last_use is not None:
                    act.wait_ge(last_use.sem, count + last_use.base)
                nc.scalar.activation(c.weight_high[:, slot, :], c.ring[:, raw, :], ACT.Copy).then_inc(high.sem, 1)

            def silus(n):
                for h in range(2):
                    act.wait_ge(gate_made.sem, n * 2 + (gb + h + 1))
                    act.wait_ge(hidden_made.sem, n * 2 + (mb + h - 1))
                    nc.scalar.activation(silu[h], ps[:, 2 * h, 0:T], ACT.Silu).then_inc(silu_made.sem, 1)

            def hiddens(n):
                for h in range(2):
                    act.wait_ge(hidden_made.sem, n * 2 + (mb + h + 1))
                    nc.scalar.activation(c.hidden_high[:, h, :], hidden[h], ACT.Copy).then_inc(hidden_high.sem, 1)

            def triple(t):
                make_high(t.unit(0), down_made, t.n)
                hiddens(t.n)
                make_high(t.unit(1), up_made, t.n * 2 + 2)
                silus(t.n + 1)
                make_high(t.unit(2), gate_made, t.n * 2 + 4)

            stream(act, lambda: (make_high(first[0]), make_high(first[1]), silus(0)), triple,
                   lambda: (hiddens(G - 1), make_high(after.unit(0), up_made, 2 * G)))

        def low_half(eng, engine, u, half, sem):
            number, slot, raw, _ = u
            eng.wait_ge(high.sem, number + (hb + 1))
            part = slice(HALF * half, HALF * half + HALF)
            engine.tensor_tensor(c.weight_low[:, slot, part], c.ring[:, raw, part],
                                 c.weight_high[:, slot, part].bitcast(F32), ALU.subtract).then_inc(sem, 1)

        @block.gpsimd
        def _(pool):
            half = lambda u: low_half(pool, nc.gpsimd, u, 1, low2.sem)
            stream(pool, lambda: (half(first[0]), half(first[1])), lambda t: [half(t.unit(j)) for j in range(3)],
                   lambda: half(after.unit(0)))

        @block.vector
        def _(dve):
            half = lambda u: low_half(dve, nc.vector, u, 0, low.sem)

            def hiddens(n):
                for h in range(2):
                    dve.wait_ge(silu_made.sem, n * 2 + (sb + h + 1))
                    dve.wait_ge(up_made.sem, n * 2 + (pb + h + 1))
                    nc.vector.tensor_tensor(hidden[h], silu[h], ps[:, 2 * h + 1, 0:T], ALU.mult).then_inc(hidden_made.sem, 1)
                for h in range(2):
                    dve.wait_ge(hidden_high.sem, n * 2 + (ihb + h + 1))
                    nc.vector.tensor_tensor(c.hidden_low[:, h, :], hidden[h], c.hidden_high[:, h, :].bitcast(F32),
                                            ALU.subtract).then_inc(hidden_low.sem, 1)

            def triple(t):
                half(t.unit(0))
                hiddens(t.n)
                half(t.unit(1))
                half(t.unit(2))

            stream(dve, lambda: (half(first[0]), half(first[1])), triple, lambda: (hiddens(G - 1), half(after.unit(0))))
            if keep != 1.0:
                for t in range(TT):
                    c.vchain(dve, nc.vector.tensor_scalar(x[:, t, :], x[:, t, :], keep, None, ALU.mult))
            dve.wait_ge(down_made.sem, down_made.base + G)
            dve.wait_ge(summed.sem, summed.base + 1)
            for t in range(TT):
                for n in range(2):
                    xn = x[:, t, 512 * n:512 * n + 512]
                    c.vchain(dve, nc.vector.scalar_tensor_tensor(
                        out=xn, in0=ps[:, 4 + 2 * t + n, :], scalar=add, in1=xn, op0=ALU.mult, op1=ALU.add))

        @block.tensor
        def _(pe):
            def clear(start, stop):
                for t in range(TT):
                    for n in range(2):
                        last = nc.tensor.matmul(ps[:, 4 + 2 * t + n, :], c.zeros[:, 0:P], c.zeros, start=start,
                                                stop=stop, skip_group_check=True)
                return last

            def split(u):
                number, slot, _, _ = u
                pe.wait_ge(low.sem, number + (wb + 1))
                pe.wait_ge(low2.sem, number + (vb + 1))
                return c.weight_high[:, slot, :], c.weight_low[:, slot, :]

            def across(u, n, bank, made):
                w = [m.rearrange("p (k f) -> p k f", k=KD) for m in split(u)]
                for h in range(2):
                    pe.wait_ge(hidden_made.sem, n * 2 + (mb + h - 1))
                    for k in range(KD):
                        last = three_passes(nc, ps[:, 2 * h + bank, 0:T], [m[:, k, P * h:P * h + P] for m in w],
                                            [m[:, k, :] for m in acts], k == 0, k == KD - 1)
                    last.then_inc(made.sem, 1)

            def down(u, n):
                w = [m.rearrange("p (h n) -> p h n", h=2) for m in split(u)]
                for h in range(2):
                    pe.wait_ge(hidden_low.sem, n * 2 + (ilb + h + 1))
                    for t in range(TT):
                        for q in range(2):
                            last = three_passes(nc, ps[:, 4 + 2 * t + q, :],
                                                [m[:, h, P * t:P * t + P] for m in (c.hidden_high, c.hidden_low)],
                                                [m[:, h, 512 * q:512 * q + 512] for m in w], False, False)
                last.then_inc(down_made.sem, 1)

            def triple(t):
                across(t.unit(0), t.n + 1, 0, gate_made)
                down(t.unit(1), t.n)
                across(t.unit(2), t.n + 1, 1, up_made)

            clear(True, False)
            stream(pe, lambda: (across(first[0], 0, 0, gate_made), across(first[1], 0, 1, up_made)), triple,
                   lambda: down(after.unit(0), G - 1))
            clear(False, True).then_inc(summed.sem, 1)
    for s in range(3):
        loaded[s].advance(16 * ((UNITS + 2 - s) // 3))
    for s in (high, low, low2):
        s.advance(UNITS)
    down_made.advance(G)
    for s in (gate_made, up_made, silu_made, hidden_made, hidden_high, hidden_low):
        s.advance(2 * G)
    summed.advance(1)


def product(c, w, groups, take, tm=False, src=None, cols=GW):
    return Product(w=w, groups=groups, take=take, tm=tm, src=c.hT if src is None else src, cols=cols,
                           kd=w.shape[2] // GW)


def three_passes(nc, out, still, moving, first, last):
    for n, (a, b) in enumerate(((0, 0), (0, 1), (1, 0))):
        ins = nc.tensor.matmul(out, still[a], moving[b], start=first and n == 0, stop=last and n == 2,
                               skip_group_check=True)
    return ins


def project_stage(c, runs, unloader="scalar"):
    nc, ps = c.nc, c.ps
    loaded = signals(c, "weights_loaded0", "weights_loaded1")
    made, taken, high, low, input_high, input_low = signals(
        c, "product_made", "product_taken", "weight_high_made", "weight_low_made", "input_high", "input_low")
    lb, mb, tb, hb, wb = [s.base for s in loaded], made.base, taken.base, high.base, low.base
    total = sum(r.groups for r in runs)
    src, kd = runs[0].src, runs[0].kd
    split = src is not c.hT or not c.parts_of_hT
    c.parts_of_hT = src is c.hT
    scalar_unloads = unloader == "scalar"

    def each_step(eng, body):
        n = 0
        for r in runs:
            if r.groups >= 4:
                with eng.Fori(0, r.groups // 2) as i:
                    for j in range(2):
                        body(r, (n + j) % 2, i * 2 + j, i * 2 + (n + j), i + (n + j) // 2)
                rest = range(r.groups - r.groups % 2, r.groups)
            else:
                rest = range(r.groups)
            for g in rest:
                body(r, (n + g) % 2, g, n + g, (n + g) // 2)
            n += r.groups

    def high_part(eng, copy):
        def one(r, s, g, step, uses):
            eng.wait_ge(loaded[s].sem, uses * 16 + (lb[s] + 16))
            eng.wait_ge(made.sem, step + (mb - 1))
            copy(c.weight_high[:, s, 0:kd * GW], c.ring[:, s, 0:kd * GW]).then_inc(high.sem, 1)
        if split:
            copy(c.act_high[:, 0:kd, :], src[:, 0:kd, :]).then_inc(input_high.sem, 1)
        each_step(eng, one)

    def low_part(eng, engine):
        def one(r, s, g, step, uses):
            eng.wait_ge(high.sem, step + (hb + 1))
            engine.tensor_tensor(c.weight_low[:, s, 0:kd * GW], c.ring[:, s, 0:kd * GW],
                                 c.weight_high[:, s, 0:kd * GW].bitcast(F32), ALU.subtract).then_inc(low.sem, 1)
        if split:
            eng.wait_ge(input_high.sem, input_high.base + 1)
            engine.tensor_tensor(c.act_low[:, 0:kd, :], src[:, 0:kd, :], c.act_high[:, 0:kd, :].bitcast(F32),
                                 ALU.subtract).then_inc(input_low.sem, 1)
        each_step(eng, one)

    def unload(eng):
        def one(r, s, g, step, uses):
            eng.wait_ge(made.sem, step + (mb + 1))
            r.take(g, ps[:, 2 * s:2 * s + 2, 0:r.cols]).then_inc(taken.sem, 1)
        each_step(eng, one)

    with nc.Block() as block:
        @block.sync
        def _(sp):
            def load(r, s, g, step, uses):
                sp.wait_ge(low.sem, step + (wb - 1))
                rows = r.w[bass.ds(g, 1), :, :].rearrange("o p n -> p (o n)")
                sp.dma_start(c.ring[:, s, 0:kd * GW], rows).then_inc(loaded[s].sem, 16)
            each_step(sp, load)

        @block.tensor
        def _(pe):
            def multiply(r, s, g, step, uses):
                pe.wait_ge(low.sem, step + (wb + 1))
                pe.wait_ge(taken.sem, step + (tb - 1))
                w = [m[:, s, 0:kd * GW].rearrange("p (k f) -> p k f", f=GW) for m in (c.weight_high, c.weight_low)]
                acts = (c.act_high, c.act_low)
                for a in range(2):
                    part = slice(P * a, P * a + P)
                    for k in range(kd):
                        if r.tm:
                            still, moving = [m[:, k, part] for m in acts], [m[:, k, 0:r.cols] for m in w]
                        else:
                            still, moving = [m[:, k, part] for m in w], [m[:, k, :] for m in acts]
                        last = three_passes(nc, ps[:, 2 * s + a, 0:r.cols], still, moving, k == 0, k == kd - 1)
                last.then_inc(made.sem, 1)
            if split:
                pe.wait_ge(input_low.sem, input_low.base + 1)
            each_step(pe, multiply)

        @block.scalar
        def _(act):
            if scalar_unloads:
                unload(act)
            else:
                high_part(act, lambda o, i: nc.scalar.activation(o, i, ACT.Copy))

        @block.vector
        def _(dve):
            if scalar_unloads:
                high_part(dve, nc.vector.tensor_copy)
            else:
                unload(dve)

        @block.gpsimd
        def _(pool):
            low_part(pool, nc.gpsimd)
    for s in range(2):
        loaded[s].advance(16 * ((total + 1 - s) // 2))
    for s in (made, taken, high, low):
        s.advance(total)
    if split:
        input_high.advance(1)
        input_low.advance(1)


def to_fm(c, dst, func=ACT.Copy):
    return lambda g, r: c.nc.scalar.activation(dst[:, bass.ds(g * 2, 2), :], r, func)


def to_tm(c, dst, func=ACT.Copy, cols=GW):
    return lambda g, r: c.nc.scalar.activation(dst[:, :, bass.ds(g * GW, cols)], r, func)


def add_to_x(c, keep=1.0):
    def take(g, r):
        xg = c.x[:, :, bass.ds(g * GW, GW)]
        return c.nc.vector.scalar_tensor_tensor(out=xg, in0=xg, scalar=keep, in1=r, op0=ALU.mult, op1=ALU.add)
    return take


def rope_stage(c, chunks, rotation, cos, sin):
    nc, ps = c.nc, c.ps
    turned, scaled, roped = signals(c, "rope_turned", "rope_scaled", "roped")
    tb, sb, rb = turned.base, scaled.base, roped.base
    n = chunks.shape[1] // 2
    prod = [c.work[:, 512 * k:512 * k + 512].rearrange("p (a t) -> p a t", a=2) for k in range(4)]

    with nc.Block() as block:
        @block.tensor
        def _(pe):
            for k in range(n):
                if k >= 4:
                    pe.wait_ge(roped.sem, rb + k - 3)
                nc.tensor.matmul(ps[:, k % 4, :], rotation, chunks[:, 2 * k:2 * k + 2, :].rearrange("p a t -> p (a t)"),
                                 start=True, stop=True).then_inc(turned.sem, 1)

        @block.gpsimd
        def _(pool):
            for k in range(n):
                if k >= 2:
                    pool.wait_ge(roped.sem, rb + k - 1)
                nc.gpsimd.tensor_tensor(prod[k % 2], chunks[:, 2 * k:2 * k + 2, :],
                                        cos.unsqueeze(1).to_broadcast([P, 2, T]), ALU.mult).then_inc(scaled.sem, 1)

        @block.vector
        def _(dve):
            for k in range(n):
                dve.wait_ge(turned.sem, tb + k + 1)
                c.vchain(dve, nc.vector.tensor_tensor(prod[2 + k % 2], ps[:, k % 4, :].rearrange("p (a t) -> p a t", a=2),
                                                      sin.unsqueeze(1).to_broadcast([P, 2, T]), ALU.mult))
                dve.wait_ge(scaled.sem, sb + k + 1)
                nc.vector.tensor_tensor(chunks[:, 2 * k:2 * k + 2, :], prod[k % 2], prod[2 + k % 2],
                                        ALU.add).then_inc(roped.sem, 1)
    for s in (turned, scaled, roped):
        s.advance(n)


def attention_stage(c, groups, scale):
    nc, ps = c.nc, c.ps
    scored, biased, exped, factored, weighted, turned, turned_taken, attended, output = signals(
        c, "scored", "biased", "exped", "factored", "weighted", "probs_turned", "turned_taken", "attended",
        "output_taken")
    zb, bb, eb, fb, wb, tb, kb, ab, ob = (s.base for s in (scored, biased, exped, factored, weighted, turned,
                                                           turned_taken, attended, output))
    passes = []
    for gi, (members, _) in enumerate(groups):
        slab = 0
        for m in members:
            passes.append((m, gi, slab, m is members[-1]))
            slab += len(m.v)
    N = len(passes)
    S = [c.work[:, 1024 * b:1024 * b + 1024].rearrange("p (a k) -> p a k", a=4) for b in range(2)]
    turned_sb = [c.ring[:, 2 * b:2 * b + 2, :].rearrange("p s n -> p (s n)")[:, 0:5 * 512]
                 .rearrange("p (l a q) -> p l a q", l=5, a=4) for b in range(2)]
    st = lambda b, n: c.small[:, 32 * b + 4 * n:32 * b + 4 * n + 4]

    with nc.Block() as block:
        @block.tensor
        def _(pe):
            def score(n):
                m, b = passes[n][0], n % 2
                if n >= 2:
                    pe.wait_ge(biased.sem, bb + n - 1)
                for p in range(2):
                    for j in range(2):
                        last = nc.tensor.matmul(ps[:, 2 * b + p, T * j:T * j + m.nk], m.q(p, j), m.k(p),
                                                start=True, stop=True)
                last.then_inc(scored.sem, 1)

            def turn(n):
                m, b = passes[n][0], n % 2
                pe.wait_ge(weighted.sem, wb + n + 1)
                if n:
                    pe.wait_ge(turned_taken.sem, kb + n)
                for l in range(len(m.v)):
                    w = min(P, m.nk - P * l)
                    for a in range(4):
                        last = nc.tensor.transpose(ps[0:w, 4 + l, P * a:P * a + P], S[b][:, a, P * l:P * l + w], c.ident)
                last.then_inc(turned.sem, 1)

            def attend(gi):
                members, _ = groups[gi]
                pe.wait_ge(turned_taken.sem, kb + sum(len(groups[g][0]) for g in range(gi + 1)))
                if gi >= 2:
                    pe.wait_ge(output.sem, ob + gi - 1)
                for p in range(2):
                    for j in range(2):
                        parts = [(m, l) for m in members for l in range(len(m.v))]
                        for n, (m, l) in enumerate(parts):
                            w = min(P, m.nk - P * l)
                            last = nc.tensor.matmul(ps[HD * p:HD * p + HD, 6 + gi % 2, P * j:P * j + P], m.v[l],
                                                    turned_sb[gi % 2][0:w, n, 2 * p + j, :],
                                                    start=(n == 0), stop=(n == len(parts) - 1))
                last.then_inc(attended.sem, 1)

            score(0)
            if N > 1:
                score(1)
            for n in range(N):
                turn(n)
                if n + 2 < N:
                    score(n + 2)
                if passes[n][3]:
                    attend(passes[n][1])

        @block.vector
        def _(dve):
            link = lambda ins: c.vchain(dve, ins)

            def bias(n):
                m, b = passes[n][0], n % 2
                dve.wait_ge(scored.sem, zb + n + 1)
                if n >= 2:
                    dve.wait_ge(turned.sem, tb + n - 1)
                src = ps[:, 2 * b:2 * b + 2, :].rearrange("p h (j k) -> p (h j) k", j=2)[:, :, 0:m.nk]
                link(nc.vector.tensor_tensor(S[b][:, :, 0:m.nk], src, m.mask.unsqueeze(1).to_broadcast([P, 4, m.nk]),
                                             ALU.add))
                link(nc.vector.tensor_reduce(st(b, 0), S[b][:, :, 0:m.nk], axis=AX.X, op=ALU.max))
                if m.sinks is None:
                    nc.vector.tensor_scalar(st(b, 1), st(b, 0), -scale, None, ALU.mult).then_inc(biased.sem, 1)
                else:
                    link(nc.vector.scalar_tensor_tensor(out=st(b, 0), in0=st(b, 0), scalar=scale, in1=m.sinks,
                                                        op0=ALU.mult, op1=ALU.max))
                    link(nc.vector.tensor_scalar(st(b, 1), st(b, 0), -1.0, None, ALU.mult))
                    nc.vector.tensor_tensor(st(b, 2), m.sinks, st(b, 0), ALU.subtract).then_inc(biased.sem, 1)

            def factor(n):
                m, b = passes[n][0], n % 2
                dve.wait_ge(exped.sem, eb + n + 1)
                if m.sinks is not None:
                    link(nc.vector.tensor_tensor(st(b, 4), st(b, 4), st(b, 3), ALU.add))
                ins = nc.vector.reciprocal(st(b, 5), st(b, 4))
                if m.gates is not None:
                    link(ins)
                    ins = nc.vector.tensor_tensor(st(b, 5).rearrange("p (h j) -> p h j", h=2),
                                                  st(b, 5).rearrange("p (h j) -> p h j", h=2), m.gates, ALU.mult)
                if m.valid is not None:
                    link(ins)
                    ins = nc.vector.tensor_scalar(st(b, 5), st(b, 5), m.valid, None, ALU.mult)
                ins.then_inc(factored.sem, 1)

            bias(0)
            for n in range(N):
                if n + 1 < N:
                    bias(n + 1)
                factor(n)

        @block.scalar
        def _(act):
            def exps(n):
                m, b = passes[n][0], n % 2
                act.wait_ge(biased.sem, bb + n + 1)
                if m.sinks is not None:
                    nc.scalar.activation(st(b, 3), st(b, 2), ACT.Exp)
                for a in range(4):
                    last = nc.scalar.activation(S[b][:, a, 0:m.nk], S[b][:, a, 0:m.nk], ACT.Exp, bias=st(b, 1)[:, a:a + 1],
                                                scale=scale, accum_out=st(b, 4)[:, a:a + 1])
                last.then_inc(exped.sem, 1)

            def take_turned(n):
                m, gi, slab, _ = passes[n]
                act.wait_ge(turned.sem, tb + n + 1)
                if gi >= 2:
                    act.wait_ge(attended.sem, ab + gi - 1)
                for l in range(len(m.v)):
                    w = min(P, m.nk - P * l)
                    last = nc.scalar.activation(turned_sb[gi % 2][0:w, slab + l, :, :].rearrange("p a q -> p (a q)"),
                                                ps[0:w, 4 + l, :], ACT.Copy)
                last.then_inc(turned_taken.sem, 1)

            def take_output(gi):
                act.wait_ge(attended.sem, ab + gi + 1)
                nc.scalar.activation(groups[gi][1], ps[:, 6 + gi % 2, 0:T].rearrange("p (j q) -> p j q", j=2),
                                     ACT.Copy).then_inc(output.sem, 1)

            exps(0)
            for n in range(N):
                if n + 1 < N:
                    exps(n + 1)
                take_turned(n)
                if passes[n][3]:
                    take_output(passes[n][1])

        @block.gpsimd
        def _(pool):
            for n in range(N):
                m, b = passes[n][0], n % 2
                pool.wait_ge(factored.sem, fb + n + 1)
                nc.gpsimd.tensor_tensor(S[b][:, :, 0:m.nk], S[b][:, :, 0:m.nk],
                                        st(b, 5).unsqueeze(2).to_broadcast([P, 4, m.nk]), ALU.mult)\
                    .then_inc(weighted.sem, 1)
    for s in (scored, biased, exped, factored, weighted, turned, turned_taken):
        s.advance(N)
    attended.advance(len(groups))
    output.advance(len(groups))


CMP_LEN, CMP_STRIDE = 32, 16
NCMP = (T - CMP_LEN) // CMP_STRIDE + 1


def load_stage(c, loads):
    nc = c.nc
    first, = signals(c, "tables_loaded")
    with nc.Block() as block:
        @block.sync
        def _(sp):
            for dst, src in loads:
                sp.dma_start(dst, src).then_inc(first.sem, 16)
            sp.wait_ge(first.sem, first.base + 16 * len(loads))
    first.advance(16 * len(loads))


def gmlp_stage(c, u, v, out, wT, bias, causal):
    nc, ps = c.nc, c.ps
    H = 8
    var_made, root_made, normed, mixed = signals(c, "gm_var_made", "gm_root_made", "gm_normed", "gm_mixed")
    vh = v.rearrange("p t (h d) -> p t h d", h=H)
    sq = c.work[:, 0:TT * H * HD].rearrange("p (t n) -> p t n", t=TT)
    sqh = sq.rearrange("p t (h d) -> p t h d", h=H)
    st = lambda n: c.small[:, 16 * n:16 * n + 16]
    with nc.Block() as block:
        @block.vector
        def _(dve):
            link = lambda ins: c.vchain(dve, ins)
            link(nc.vector.tensor_tensor(wT, wT, causal.unsqueeze(1).to_broadcast([P, H, P]), ALU.mult))
            link(nc.vector.tensor_reduce(st(0).rearrange("p (t h) -> p t h", t=TT), vh, axis=AX.X, op=ALU.add))
            link(nc.vector.tensor_scalar(st(0), st(0), 1.0 / HD, None, ALU.mult))
            for t in range(TT):
                link(nc.vector.tensor_tensor(vh[:, t], vh[:, t], st(0)[:, H * t:H * t + H].unsqueeze(2)
                                             .to_broadcast([P, H, HD]), ALU.subtract))
            link(nc.vector.tensor_tensor(sq, v, v, ALU.mult))
            link(nc.vector.tensor_reduce(st(1), sq.rearrange("p t (h d) -> p (t h) d", h=H), axis=AX.X, op=ALU.add))
            nc.vector.tensor_scalar(st(1), st(1), 1.0 / HD, LN_EPS, ALU.mult, ALU.add).then_inc(var_made.sem, 1)
            dve.wait_ge(root_made.sem, root_made.base + 1)
            link(nc.vector.reciprocal(st(3), st(2)))
            for t in range(TT):
                nc.vector.tensor_tensor(vh[:, t], vh[:, t], st(3)[:, H * t:H * t + H].unsqueeze(2)
                                        .to_broadcast([P, H, HD]), ALU.mult).then_inc(normed.sem, 1)
            for b in range(2):
                dve.wait_ge(mixed.sem, mixed.base + b + 1)
                spread = sq.rearrange("p t n -> p (t n)")[:, 512 * b:512 * b + 512].rearrange("p (j t) -> p j t", j=2)
                link(nc.vector.tensor_tensor(spread, ps[:, b, :].rearrange("p (j t) -> p j t", j=2),
                                             bias[:, 2 * b:2 * b + 2, :], ALU.add))
                link(nc.vector.tensor_tensor(out[:, 2 * b:2 * b + 2, :], spread, u[:, 2 * b:2 * b + 2, :], ALU.mult))

        @block.scalar
        def _(act):
            act.wait_ge(var_made.sem, var_made.base + 1)
            nc.scalar.activation(st(2), st(1), ACT.Sqrt).then_inc(root_made.sem, 1)

        @block.tensor
        def _(pe):
            pe.wait_ge(normed.sem, normed.base + TT)
            for b in range(2):
                for h in range(4 * b, 4 * b + 4):
                    for t in range(TT):
                        at = T * (h // 2 % 2) + P * t
                        last = nc.tensor.matmul(ps[HD * (h % 2):HD * (h % 2) + HD, b, at:at + P],
                                                v[:, t, HD * h:HD * h + HD], wT[:, h, :], start=True, stop=True)
                last.then_inc(mixed.sem, 1)
    var_made.advance(1)
    root_made.advance(1)
    normed.advance(TT)
    mixed.advance(2)


def compress_stage(c, kv, w1, w2, pe_cols, cos, sin, kT, vT):
    nc, ps = c.nc, c.ps
    hid_made, pe_made, pe_taken, gelued, second, ready, flipped = signals(
        c, "cmp_hidden", "cmp_pe_made", "cmp_pe_taken", "cmp_gelued", "cmp_second", "cmp_rotated", "cmp_flipped")
    h1 = c.work[0:HD, 0:4 * 16].rearrange("p (a n) -> p a n", a=4)
    peb = c.work[0:HD, 64:66]
    kc = c.work[0:NCMP, 128:256].rearrange("p (g h d) -> p g h d", g=2, h=2)
    rot = c.work[0:NCMP, 256:512].rearrange("p (g u h d) -> p g u h d", g=2, u=2, h=2)
    tmp = c.work[0:NCMP, 512:640].rearrange("p (n g d) -> p n g d", n=2, g=2)
    with nc.Block() as block:
        @block.tensor
        def _(pe):
            for m in range(2):
                for l in range(CMP_LEN):
                    last = nc.tensor.matmul(ps[0:HD, 4 + m, 0:1], w1[0:HD, m, l, :], pe_cols[0:HD, m, l:l + 1],
                                            start=(l == 0), stop=(l == CMP_LEN - 1))
            last.then_inc(pe_made.sem, 1)
            for m in range(2):
                for g in range(2):
                    at = slice(HD * g, HD * g + HD)
                    for l in range(CMP_LEN):
                        last = nc.tensor.matmul(ps[0:HD, 2 * m + g, 0:NCMP], w1[at, m, l, :],
                                                kv[at, m, l:l + CMP_STRIDE * (NCMP - 1) + 1:CMP_STRIDE],
                                                start=(l == 0), stop=(l == CMP_LEN - 1))
            last.then_inc(hid_made.sem, 1)
            pe.wait_ge(gelued.sem, gelued.base + 1)
            for m in range(2):
                for g in range(2):
                    last = nc.tensor.matmul(ps[0:NCMP, 6 + m, HD * g:HD * g + HD], h1[:, 2 * m + g, 0:NCMP],
                                            w2[0:HD, m, :], start=True, stop=True)
            last.then_inc(second.sem, 1)
            pe.wait_ge(ready.sem, ready.base + 1)
            for g in range(2):
                last = nc.tensor.transpose(ps[:, 4, 16 * g:16 * g + NCMP], rot[:, g].rearrange("p u h d -> p (u h d)"),
                                           c.ident[0:NCMP, 0:NCMP])
            last.then_inc(flipped.sem, 1)

        @block.scalar
        def _(act):
            act.wait_ge(pe_taken.sem, pe_taken.base + 1)
            act.wait_ge(hid_made.sem, hid_made.base + 1)
            for m in range(2):
                last = nc.scalar.activation(h1[:, 2 * m:2 * m + 2, 0:NCMP], ps[0:HD, 2 * m:2 * m + 2, 0:NCMP],
                                            ACT.Gelu_apprx_tanh, bias=peb[:, m:m + 1])
            last.then_inc(gelued.sem, 1)

        @block.vector
        def _(dve):
            link = lambda ins: c.vchain(dve, ins)
            dve.wait_ge(pe_made.sem, pe_made.base + 1)
            nc.vector.tensor_copy(peb, ps[0:HD, 4:6, 0:1].rearrange("p a o -> p (a o)")).then_inc(pe_taken.sem, 1)
            dve.wait_ge(second.sem, second.base + 1)
            link(nc.vector.tensor_copy(vT, ps[0:NCMP, 7, 0:128].rearrange("p (g d) -> p g d", g=2)))
            link(nc.vector.tensor_copy(kc, ps[0:NCMP, 6, 0:128].rearrange("p (g h d) -> p g h d", g=2, h=2)))
            cb = cos[0:NCMP].unsqueeze(1).to_broadcast([NCMP, 2, 32])
            sb = sin[0:NCMP].unsqueeze(1).to_broadcast([NCMP, 2, 32])
            for half, op in ((0, ALU.subtract), (1, ALU.add)):
                link(nc.vector.tensor_tensor(tmp[:, 0], kc[:, :, half, :], cb, ALU.mult))
                link(nc.vector.tensor_tensor(tmp[:, 1], kc[:, :, 1 - half, :], sb, ALU.mult))
                link(nc.vector.tensor_tensor(rot[:, :, 0, half, :], tmp[:, 0], tmp[:, 1], op))
            nc.vector.tensor_copy(rot[:, :, 1], rot[:, :, 0]).then_inc(ready.sem, 1)
            dve.wait_ge(flipped.sem, flipped.base + 1)
            link(nc.vector.tensor_copy(kT[:, :, 0:NCMP], ps[:, 4, 0:32].rearrange("p (g n) -> p g n", g=2)[:, :, 0:NCMP]))
    for s in (hid_made, pe_made, pe_taken, gelued, second, ready, flipped):
        s.advance(1)


def even_mixer(c):
    d = c.dram
    norm_stage(c, gain_fm=c.gains[:, KD:2 * KD])
    seg = c.seg
    vtm = c.vtm
    t = c.tables
    wT = t[:, 0:1024].rearrange("p (h t) -> p h t", h=8)
    bias = t[:, 1024:2048].rearrange("p (a t) -> p a t", a=4)
    causal = t[:, 2048:2176]
    w2 = t[:, 2176:2304].rearrange("p (m o) -> p m o", m=2)
    pe_cols = t[:, 2304:2368].rearrange("p (m l) -> p m l", m=2)
    rot64 = t[:, 2368:2496]
    cos, sin = t[:, 2496:2752], t[:, 2752:3008]
    ccos, csin = t[:, 3008:3040], t[:, 3040:3072]
    amask = t[:, 3072:3584].rearrange("p (t k) -> p t k", t=2)
    cmask = t[:, 3584:3616].rearrange("p (t k) -> p t k", t=2)
    valid = t[:, 3616:3618]
    kT = t[:, 3618:3650].rearrange("p (g n) -> p g n", g=2)
    vT = t[0:NCMP, 3650:3778].rearrange("p (g d) -> p g d", g=2)
    w1 = c.ring[:, 0:2, :].rearrange("p m (l o) -> p m l o", l=CMP_LEN)
    load_stage(c, [(t[:, 0:3618], d["l_even_tables"])])
    wi = d["l_ev_in"]
    project_stage(c, [
        product(c, wi[0:2], 2, to_fm(c, seg[:, 0:4], ACT.Gelu_apprx_tanh)),
        product(c, wi[7:9], 2, to_tm(c, vtm, ACT.Gelu_apprx_tanh), tm=True),
        product(c, wi[2:7], 5, to_fm(c, seg[:, 4:14])),
        product(c, wi[9:10], 1, to_tm(c, vtm[:, :, 512:768]), tm=True),
        product(c, wi[10:11], 1, to_tm(c, vtm[:, :, 768:792], ACT.Sigmoid, cols=24), tm=True, cols=24)])
    load_stage(c, [(c.ring[:, 0:2, :].rearrange("p m n -> p (m n)"), d["l_cmp_w1"])])
    gmlp_stage(c, seg[:, 0:4], vtm[:, :, 0:512], c.cat[:, 0:4], wT, bias, causal)
    compress_stage(c, seg[:, 12:14], w1, w2, pe_cols, ccos, csin, kT, vT)
    rope_stage(c, seg[:, 4:12], rot64, cos, sin)
    groups = []
    for g in range(2):
        for qt in range(TT):
            def q(p, j, g=g, qt=qt):
                return seg[HD * p:HD * p + HD, 4 + 2 * g + j, P * qt:P * qt + P]
            gates = vtm[:, qt, 768 + 12 * g:780 + 12 * g].rearrange("p (j h c) -> p c h j", j=2, h=2)
            nk = P * (qt + 1)
            members = [Pass(
                q=q, k=lambda p, g=g: kT[HD * p:HD * p + HD, g, 0:NCMP], nk=NCMP, v=[vT[:, g, :]],
                mask=cmask[:, qt, 0:NCMP], sinks=None, gates=gates[:, 0], valid=valid[:, qt:qt + 1])]
            for b in range(2):
                members.append(Pass(
                    q=q, k=lambda p, g=g, b=b, nk=nk: seg[HD * p:HD * p + HD, 8 + 2 * b + g, 0:nk], nk=nk,
                    v=[vtm[:, l, 512 + P * b + HD * g:512 + P * b + HD * g + HD] for l in range(qt + 1)],
                    mask=amask[:, qt, 0:nk], sinks=None, gates=gates[:, 1 + b], valid=None))
            groups.append((members, c.cat[:, 4 + 2 * g:6 + 2 * g, P * qt:P * qt + P]))
    attention_stage(c, groups, HD ** -0.5)
    project_stage(c, [product(c, d["l_ev_out"], 4, add_to_x(c), tm=True, src=c.cat)], "vector")


POOL_WINDOWS = (2, 4, 8, 16)
NT = 16
CH = 32


def pool_stage(c, z, operators, weights, scale, out):
    nc, ps = c.nc, c.ps
    pooled, taken, mixed = signals(c, "pooled", "pooled_taken", "pool_mixed")
    buf = c.work[:, 0:4 * T].rearrange("p (g t) -> p g t", g=4)
    with nc.Block() as block:
        @block.tensor
        def _(pe):
            for g in range(4):
                for t in range(TT):
                    last = nc.tensor.matmul(ps[:, g, 0:T], z[:, t, P * g:P * g + P], operators[:, g, t, :],
                                            start=(t == 0), stop=(t == TT - 1))
                last.then_inc(pooled.sem, 1)
            for g in range(4):
                pe.wait_ge(taken.sem, taken.base + g + 1)
                nc.tensor.matmul(ps[:, 4 + g, 0:T], weights[:, g, :], buf[:, g, :], start=True,
                                 stop=True).then_inc(mixed.sem, 1)

        @block.scalar
        def _(act):
            for g in range(4):
                act.wait_ge(pooled.sem, pooled.base + g + 1)
                nc.scalar.activation(buf[:, g, :], ps[:, g, 0:T], ACT.Copy).then_inc(taken.sem, 1)

        @block.vector
        def _(dve):
            for g in range(4):
                dve.wait_ge(mixed.sem, mixed.base + g + 1)
                c.vchain(dve, nc.vector.tensor_scalar(out[:, g, :], ps[:, 4 + g, 0:T], scale[:, g:g + 1], None, ALU.mult))
    for s in (pooled, taken, mixed):
        s.advance(4)


def s5_tables_stage(c, lam_re, lam_im, log_dt, c_re, c_im, decay, phases, readout):
    nc = c.nc
    V = nc.vector
    reduced, sines = signals(c, "s5_angle_reduced", "s5_sines")
    st = lambda n: c.rowbuf[:, 0, NT * n:NT * n + NT]
    dt, a, theta, k, half, sh, sn, m, cs, cm1, nr, ni, inv, cr, ci, t1, t2 = (st(n) for n in range(17))
    two_pi = 2 * np.pi
    parts = [6.28125, 0.0019340515136718750]
    parts.append(float(np.float32(two_pi - sum(parts))))
    ln2 = [0.693359375, float(np.float32(np.log(2.0) - 0.693359375))]
    big = 1.5 * 2.0 ** 23
    pi = 3.1415925
    with nc.Block() as block:
        @block.scalar
        def _(act):
            act.wait_ge(reduced.sem, reduced.base + 1)
            nc.scalar.activation(sh, half, ACT.Sin)
            nc.scalar.activation(sn, theta, ACT.Sin).then_inc(sines.sem, 1)

        @block.vector
        def _(dve):
            link = lambda ins: c.vchain(dve, ins)
            mul = lambda o, x, y: link(V.tensor_tensor(o, x, y, ALU.mult))
            add = lambda o, x, y: link(V.tensor_tensor(o, x, y, ALU.add))
            sub = lambda o, x, y: link(V.tensor_tensor(o, x, y, ALU.subtract))
            fma = lambda o, x, s, y: link(V.scalar_tensor_tensor(out=o, in0=x, scalar=s, in1=y, op0=ALU.mult, op1=ALU.add))

            def round_to(o, x, s):
                link(V.tensor_scalar(o, x, float(s), None, ALU.mult))
                link(V.tensor_scalar(o, o, big, None, ALU.add))
                link(V.tensor_scalar(o, o, -big, None, ALU.add))

            round_to(k, log_dt, 1 / np.log(2.0))
            link(V.tensor_scalar(a, log_dt, 1.0, None, ALU.mult))
            for part in ln2:
                fma(a, k, -part, a)
            link(V.memset(dt, 1.0))
            for n in range(9, 0, -1):
                mul(dt, dt, a)
                link(V.tensor_scalar(dt, dt, 1.0 / n, 1.0, ALU.mult, ALU.add))
            link(V.tensor_scalar(k, k, -127.0, 128.0, ALU.max, ALU.min))
            link(V.tensor_scalar(t1.bitcast(mybir.dt.int32), k, 127.0, 2.0 ** 23, ALU.add, ALU.mult))
            mul(dt, dt, t1)
            mul(theta, lam_im, dt)
            round_to(k, theta, 1 / two_pi)
            for part in parts:
                fma(theta, k, -part, theta)
            link(V.tensor_scalar(theta, theta, -pi, pi, ALU.max, ALU.min))
            V.tensor_scalar(half, theta, 0.5, None, ALU.mult).then_inc(reduced.sem, 1)
            mul(a, lam_re, dt)
            link(V.tensor_scalar(a, a, -104.0, 104.0, ALU.max, ALU.min))
            link(V.tensor_scalar(a, a, 1.0 / 128, None, ALU.mult))
            link(V.memset(m, 1.0))
            for n in range(9, 1, -1):
                mul(m, m, a)
                link(V.tensor_scalar(m, m, 1.0 / n, 1.0, ALU.mult, ALU.add))
            mul(m, m, a)
            for _ in range(7):
                link(V.scalar_tensor_tensor(out=m, in0=m, scalar=2.0, in1=m, op0=ALU.add, op1=ALU.mult))
            link(V.tensor_scalar(decay, m, 1.0, None, ALU.add))
            dve.wait_ge(sines.sem, sines.base + 1)
            mul(cm1, sh, sh)
            link(V.tensor_scalar(cm1, cm1, -2.0, None, ALU.mult))
            link(V.tensor_scalar(cs, cm1, 1.0, None, ALU.add))
            mul(nr, decay, cm1)
            add(nr, nr, m)
            mul(ni, decay, sn)
            mul(t1, lam_re, lam_re)
            mul(inv, lam_im, lam_im)
            add(inv, inv, t1)
            link(V.reciprocal(inv, inv))
            mul(cr, nr, lam_re)
            mul(t1, ni, lam_im)
            add(cr, cr, t1)
            mul(cr, cr, inv)
            mul(ci, ni, lam_re)
            mul(t1, nr, lam_im)
            sub(ci, ci, t1)
            mul(ci, ci, inv)
            out = [readout[:, n, :].rearrange("p (n c) -> p n c", n=NT) for n in range(3)]
            wide = lambda s: s.unsqueeze(2).to_broadcast([P, NT, CH])
            mul(out[0], c_re, wide(cr))
            mul(out[1], c_im, wide(ci))
            sub(out[0], out[0], out[1])
            mul(out[1], c_im, wide(cr))
            mul(out[2], c_re, wide(ci))
            link(V.scalar_tensor_tensor(out=readout[:, 2, :], in0=readout[:, 1, :], scalar=-1.0, in1=readout[:, 2, :],
                                        op0=ALU.mult, op1=ALU.subtract))
            link(V.tensor_scalar(readout[:, 1, :], readout[:, 0, :], -1.0, None, ALU.mult))
            mul(t1, cs, cs)
            mul(t2, sn, sn)
            add(t1, t1, t2)
            link(V.tensor_scalar(t1, t1, -0.5, 1.5, ALU.mult, ALU.add))
            mul(cs, cs, t1)
            mul(sn, sn, t1)
            pr, pi_ = phases[:, 0], phases[:, 1]
            link(V.memset(pr[:, :, 0:1], 1.0))
            link(V.memset(pi_[:, :, 0:1], 0.0))
            n = 1
            while n < T:
                wide = lambda s: s.unsqueeze(2).to_broadcast([P, NT, n])
                tmp = c.work[:, 0:NT * n].rearrange("p (a k) -> p a k", a=NT)
                new = slice(n, 2 * n)
                mul(pr[:, :, new], pr[:, :, 0:n], wide(cs))
                mul(tmp, pi_[:, :, 0:n], wide(sn))
                sub(pr[:, :, new], pr[:, :, new], tmp)
                mul(pi_[:, :, new], pi_[:, :, 0:n], wide(cs))
                mul(tmp, pr[:, :, 0:n], wide(sn))
                add(pi_[:, :, new], pi_[:, :, new], tmp)
                n *= 2
                mul(t1, cs, sn)
                mul(t2, sn, sn)
                mul(cs, cs, cs)
                sub(cs, cs, t2)
                link(V.tensor_scalar(sn, t1, 2.0, None, ALU.mult))
    for s in (reduced, sines):
        s.advance(1)


def s5_stage(c, u, b_in, decay, phases, readout, skip, y):
    nc, ps = c.nc, c.ps
    driven, rotated, scanned, unrotated, read, skipped = signals(
        c, "s5_driven", "s5_rotated", "s5_scanned", "s5_unrotated", "s5_read", "s5_skipped")
    two = lambda s: s.rearrange("p (r t) -> p r t", r=2)
    cosw = [two(c.work[:, 512 * b:512 * b + 512]) for b in range(2)]
    sinw = [two(c.work[:, 1024 + 512 * b:1536 + 512 * b]) for b in range(2)]
    w = [two(c.work[:, 2048 + 512 * b:2560 + 512 * b]) for b in range(2)]
    turned = [c.rowbuf[:, b, :].rearrange("p (e r t) -> p e r t", e=2, r=2) for b in range(2)]
    wide = lambda s, n: phases[:, s, n, :].unsqueeze(1).to_broadcast([P, 2, T])
    with nc.Block() as block:
        @block.tensor
        def _(pe):
            def drive(n):
                if n >= 2:
                    pe.wait_ge(rotated.sem, rotated.base + n - 1)
                at = slice(CH * (n % 4), CH * (n % 4) + CH)
                for r in range(2):
                    last = nc.tensor.matmul(ps[:, n % 2, T * r:T * r + T], b_in[at, r, n // 4, :], u[at, n // 4, :],
                                            start=True, stop=True)
                last.then_inc(driven.sem, 1)

            def readout_of(n):
                pe.wait_ge(unrotated.sem, unrotated.base + n + 1)
                cols = slice(CH * n, CH * n + CH)
                e = turned[n % 2]
                for k, (m, v) in enumerate(((0, e[:, 0, 0]), (1, e[:, 1, 1]), (2, e[:, 0, 1]), (2, e[:, 1, 0]))):
                    last = nc.tensor.matmul(ps[CH * (n % 4):CH * (n % 4) + CH, 4 + n // 4, 0:T], readout[:, m, cols], v,
                                            start=(k == 0), stop=(k == 3))
                last.then_inc(read.sem, 1)

            drive(0)
            drive(1)
            for n in range(NT):
                if n + 2 < NT:
                    drive(n + 2)
                readout_of(n)

        @block.vector
        def _(dve):
            link = lambda ins: c.vchain(dve, ins)
            for n in range(NT):
                b = n % 2
                dve.wait_ge(driven.sem, driven.base + n + 1)
                bu = two(ps[:, b, :])
                nc.vector.tensor_tensor(cosw[b], bu, wide(0, n), ALU.mult)
                ins = nc.vector.tensor_tensor(sinw[b], bu, wide(1, n), ALU.mult)
                ins.then_inc(rotated.sem, 1)
                dve.wait_ge(rotated.sem, rotated.base + n + 1)
                nc.vector.tensor_tensor(cosw[b][:, 0], cosw[b][:, 0], sinw[b][:, 1], ALU.add)
                link(nc.vector.tensor_tensor(cosw[b][:, 1], cosw[b][:, 1], sinw[b][:, 0], ALU.subtract))
                if n >= 2:
                    dve.wait_ge(unrotated.sem, unrotated.base + n - 1)
                rate = decay[:, n:n + 1].to_broadcast([P, T])
                for r in range(2):
                    last = nc.vector.tensor_tensor_scan(w[b][:, r], rate, cosw[b][:, r], 0.0, ALU.mult, ALU.add)
                last.then_inc(scanned.sem, 1)
            for m in range(4):
                dve.wait_ge(read.sem, read.base + 4 * m + 4)
                nc.vector.scalar_tensor_tensor(out=y[:, m, :], in0=u[:, m, :], scalar=skip[:, m:m + 1], in1=ps[:, 4 + m, 0:T],
                                               op0=ALU.mult, op1=ALU.add).then_inc(skipped.sem, 1)

        @block.gpsimd
        def _(pool):
            for n in range(NT):
                b = n % 2
                pool.wait_ge(scanned.sem, scanned.base + n + 1)
                if n >= 2:
                    pool.wait_ge(read.sem, read.base + n - 1)
                for e in range(2):
                    last = nc.gpsimd.tensor_tensor(turned[b][:, e], w[b], wide(e, n), ALU.mult)
                last.then_inc(unrotated.sem, 1)

        @block.scalar
        def _(act):
            act.wait_ge(skipped.sem, skipped.base + 4)
            c.achain(act, nc.scalar.activation(y, y, ACT.Gelu_apprx_tanh))
    for s in (driven, rotated, scanned, unrotated, read):
        s.advance(NT)
    skipped.advance(4)


def multiply_stage(c, out, a, b):
    with c.nc.Block() as block:
        @block.vector
        def _(dve):
            c.vchain(dve, c.nc.vector.tensor_tensor(out, a, b, ALU.mult))


def odd_mixer(c):
    d, seg, t = c.dram, c.seg, c.tables
    norm_stage(c, gain_fm=c.gains[:, 4 * KD:5 * KD])
    operators = t[:, 0:2048].rearrange("p (g t s) -> p g t s", g=4, t=TT)
    weights = t[:, 2048:2560].rearrange("p (g d) -> p g d", g=4)
    scale, skip = t[:, 2560:2564], t[:, 2564:2568]
    lam_re, lam_im, log_dt = (t[:, 2568 + NT * n:2568 + NT * n + NT] for n in range(3))
    b_in = t[:, 2616:3640].rearrange("p (r m s) -> p r m s", r=2, m=4)
    c_re, c_im = (t[:, 3640 + 512 * n:4152 + 512 * n].rearrange("p (n c) -> p n c", n=NT) for n in range(2))
    decay = t[:, 4664:4664 + NT]
    phases = c.ring.rearrange("p s n -> p (s n)").rearrange("p (r n t) -> p r n t", r=2, n=NT)
    readout = c.vtm.rearrange("p t n -> p (t n)")[:, 0:1536].rearrange("p (m n) -> p m n", m=3)
    load_stage(c, [(t[:, 0:4664], d["l_odd_tables"])])
    zc, u, y, ab = c.vtm[:, :, 0:512], seg[:, 0:4], seg[:, 4:8], seg[:, 8:16]
    wi = d["l_od_in"]
    project_stage(c, [product(c, wi[0:2], 2, to_tm(c, zc), tm=True), product(c, wi[2:4], 2, to_fm(c, u))])
    pool_stage(c, zc, operators, weights, scale, c.cat[:, 0:4])
    s5_tables_stage(c, lam_re, lam_im, log_dt, c_re, c_im, decay, phases, readout)
    s5_stage(c, u, b_in, decay, phases, readout, skip, y)
    wg = d["l_glu"]
    project_stage(c, [product(c, wg[0:2], 2, to_fm(c, ab[:, 0:4]), src=y),
                      product(c, wg[2:4], 2, to_fm(c, ab[:, 4:8], ACT.Sigmoid), src=y)])
    multiply_stage(c, c.cat[:, 4:8], ab[:, 0:4], ab[:, 4:8])
    project_stage(c, [product(c, d["l_od_out"], 4, add_to_x(c), tm=True, src=c.cat)], "vector")


RET_HEADS = 4


def retention_stage(c, q, k, v, decay, gate, out):
    nc, ps = c.nc, c.ps
    scored, decayed, summed, kept, square_made, square_summed, rooted, scaled, gated = signals(
        c, "ret_scored", "ret_decayed", "ret_summed", "ret_kept", "ret_squared", "ret_square_summed", "ret_rooted",
        "ret_scaled", "ret_gated")
    A = [c.work[:, 512 * h:512 * h + 512].rearrange("p (s t) -> p s t", s=TT) for h in range(RET_HEADS)]
    sq = [c.work[:, 2048 + 512 * b:2560 + 512 * b].rearrange("p (j t) -> p j t", j=2) for b in range(2)]
    root = [c.work[:, 3072 + T * b:3072 + T * b + T] for b in range(2)]
    two = lambda s: s.rearrange("p (j t) -> p j t", j=2)
    with nc.Block() as block:
        @block.tensor
        def _(pe):
            def score(h):
                if h >= 2:
                    pe.wait_ge(decayed.sem, decayed.base + h - 1)
                for s in range(TT):
                    last = nc.tensor.matmul(ps[:, h % 2, T * s:T * s + T], k[:, h, P * s:P * s + P], q[:, h, :],
                                            start=True, stop=True)
                last.then_inc(scored.sem, 1)

            def combine(h):
                pe.wait_ge(decayed.sem, decayed.base + h + 1)
                if h >= 2:
                    pe.wait_ge(square_made.sem, square_made.base + h - 1)
                for j in range(2):
                    for s in range(TT):
                        at = 2 * P * h + P * j
                        last = nc.tensor.matmul(ps[:, 2 + h % 2, T * j:T * j + T], v[:, s, at:at + P], A[h][:, s, :],
                                                start=(s == 0), stop=(s == TT - 1))
                last.then_inc(summed.sem, 1)

            def square_sum(h):
                pe.wait_ge(square_made.sem, square_made.base + h + 1)
                if h >= 2:
                    pe.wait_ge(rooted.sem, rooted.base + h - 1)
                for j in range(2):
                    last = nc.tensor.matmul(ps[:, 4 + h % 2, 0:T], c.ones, sq[h % 2][:, j, :], start=(j == 0), stop=(j == 1))
                last.then_inc(square_summed.sem, 1)

            score(0)
            for h in range(RET_HEADS):
                if h + 1 < RET_HEADS:
                    score(h + 1)
                combine(h)
                if h:
                    square_sum(h - 1)
            square_sum(RET_HEADS - 1)

        @block.scalar
        def _(act):
            def root_of(h):
                act.wait_ge(square_summed.sem, square_summed.base + h + 1)
                if h >= 2:
                    act.wait_ge(scaled.sem, scaled.base + h - 1)
                nc.scalar.activation(root[h % 2], ps[:, 4 + h % 2, 0:T], ACT.Sqrt, scale=1.0 / 256,
                                     bias=c.eps[:, 0:1]).then_inc(rooted.sem, 1)

            for h in range(RET_HEADS):
                act.wait_ge(summed.sem, summed.base + h + 1)
                nc.scalar.activation(out[:, 2 * h:2 * h + 2, :], two(ps[:, 2 + h % 2, :]), ACT.Copy).then_inc(kept.sem, 1)
                if h >= 2:
                    act.wait_ge(square_summed.sem, square_summed.base + h - 1)
                nc.scalar.activation(sq[h % 2], two(ps[:, 2 + h % 2, :]), ACT.Square).then_inc(square_made.sem, 1)
                if h:
                    root_of(h - 1)
            root_of(RET_HEADS - 1)

        @block.vector
        def _(dve):
            for h in range(RET_HEADS):
                dve.wait_ge(scored.sem, scored.base + h + 1)
                nc.vector.tensor_tensor(A[h], two(ps[:, h % 2, :]), decay[:, h], ALU.mult).then_inc(decayed.sem, 1)
            for h in range(RET_HEADS):
                dve.wait_ge(rooted.sem, rooted.base + h + 1)
                c.vchain(dve, nc.vector.reciprocal(root[h % 2], root[h % 2]))
                dve.wait_ge(kept.sem, kept.base + h + 1)
                o = out[:, 2 * h:2 * h + 2, :]
                nc.vector.tensor_tensor(o, o, root[h % 2].unsqueeze(1).to_broadcast([P, 2, T]), ALU.mult)\
                    .then_inc(scaled.sem, 1)

        @block.gpsimd
        def _(pool):
            for h in range(RET_HEADS):
                pool.wait_ge(scaled.sem, scaled.base + h + 1)
                o = out[:, 2 * h:2 * h + 2, :]
                nc.gpsimd.tensor_tensor(o, o, gate[:, 2 * h:2 * h + 2, :], ALU.mult).then_inc(gated.sem, 1)
    for s in (scored, decayed, summed, kept, square_made, square_summed, rooted, scaled, gated):
        s.advance(RET_HEADS)


HG = 8
L = 32
NB = T // L


def hgrn_stage(c, q, z, v, gate, bound, rest, first_layer, norm_gain, out):
    nc, ps = c.nc, c.ps
    names = ("hg_sigmoid", "hg_bounded", "hg_logged", "hg_summed", "hg_exped", "hg_queries", "hg_keys",
             "hg_scored", "hg_turned_taken", "hg_masked", "hg_driven", "hg_drive_taken", "hg_stated", "hg_made",
             "hg_kept", "hg_square_summed", "hg_sums_taken")
    (sigmoid, bounded, logged, bsummed, exped, queries, keys, scored, turned_taken, masked, driven, drive_taken, stated,
     made, kept, square_summed, sums_taken) = signals(c, *names)
    rooted, scaled = signals(c, "hg_rooted", "hg_scaled")
    R = [c.ring[:, n, :].rearrange("p (h t) -> p h t", h=HG) for n in range(4)]
    K, E1, E2, M = R
    lo = -43.0
    st = [c.work[:, 1024 * b:1024 * b + 1024].rearrange("p (n v) -> p n v", n=NB) for b in range(2)]
    mk = [c.work[:, 2048 + T * b:2048 + T * b + T].rearrange("p (t s) -> p t s", t=TT) for b in range(2)]
    kt = [c.work[:, 2560 + T * b:2560 + T * b + T].rearrange("p (t s) -> p t s", t=TT) for b in range(2)]
    sq = [c.work[:, 3072 + T * b:3072 + T * b + T] for b in range(2)]
    drive = [c.rowbuf[:, b, :].rearrange("p (n v) -> p n v", n=NB) for b in range(2)]
    sums = K
    blocks = lambda s: s.rearrange("p (n l) -> p n l", n=NB)
    with nc.Block() as block:
        @block.scalar
        def _(act):
            for h in range(HG):
                nc.scalar.activation(K[:, h, :], z[:, h, :], ACT.Sigmoid, scale=-1.0)
                if first_layer:
                    nc.scalar.activation(E1[:, h, :], z[:, h, :], ACT.Sigmoid).then_inc(sigmoid.sem, 1)
                else:
                    nc.scalar.activation(z[:, h, :], z[:, h, :], ACT.Sigmoid).then_inc(sigmoid.sem, 1)
            for h in range(HG):
                act.wait_ge(bounded.sem, bounded.base + h + 1)
                nc.scalar.activation(E1[:, h, :] if first_layer else z[:, h, :], E1[:, h, :] if first_layer else z[:, h, :],
                                     ACT.Ln).then_inc(logged.sem, 1)
            for h in range(HG):
                act.wait_ge(bsummed.sem, bsummed.base + h + 1)
                nc.scalar.activation(E1[:, h, :], M[:, h, :], ACT.Exp)
                nc.scalar.activation(E2[:, h, :], M[:, h, :], ACT.Exp, scale=-1.0)
                nc.scalar.activation(out[:, h, :], out[:, h, :], ACT.Exp)
                nc.scalar.activation(z[:, h, :], z[:, h, :], ACT.Exp).then_inc(exped.sem, 1)

            def take_turned(h):
                act.wait_ge(scored.sem, scored.base + h + 1)
                if h >= 2:
                    act.wait_ge(driven.sem, driven.base + h - 1)
                nc.scalar.activation(kt[h % 2].rearrange("p t s -> p (t s)"), ps[:, 5, 0:T], ACT.Copy)\
                    .then_inc(turned_taken.sem, 1)

            def take_drive(h):
                act.wait_ge(driven.sem, driven.base + h + 1)
                if h >= 2:
                    act.wait_ge(stated.sem, stated.base + h - 1)
                nc.scalar.activation(drive[h % 2].rearrange("p (t n) v -> p n t v", t=TT),
                                     ps[:, 0:4, 0:T].rearrange("p n (t v) -> p n t v", t=TT), ACT.Copy)\
                    .then_inc(drive_taken.sem, 1)

            def take_output(h):
                act.wait_ge(made.sem, made.base + h + 1)
                if h >= 2:
                    act.wait_ge(square_summed.sem, square_summed.base + h - 1)
                nc.scalar.activation(out[:, h, :], ps[:, 6, 0:T], ACT.Copy)
                nc.scalar.activation(sq[h % 2], ps[:, 6, 0:T], ACT.Square).then_inc(kept.sem, 1)

            take_turned(0)
            for h in range(HG):
                take_drive(h)
                if h + 1 < HG:
                    take_turned(h + 1)
                if h:
                    take_output(h - 1)
            take_output(HG - 1)
            act.wait_ge(sums_taken.sem, sums_taken.base + HG)
            nc.scalar.activation(sums, sums, ACT.Sqrt, scale=1.0 / P, bias=c.eps[:, 0:1]).then_inc(rooted.sem, 1)

        @block.vector
        def _(dve):
            link = lambda ins: c.vchain(dve, ins)
            for h in range(HG):
                dve.wait_ge(sigmoid.sem, sigmoid.base + h + 1)
                if first_layer:
                    link(nc.vector.tensor_scalar(z[:, h, :], z[:, h, :], -lo, 0.0, ALU.add, ALU.min))
                    nc.vector.tensor_scalar(E1[:, h, :], E1[:, h, :], float(np.exp(lo)), None, ALU.max).then_inc(bounded.sem, 1)
                else:
                    nc.vector.tensor_scalar(K[:, h, :], K[:, h, :], rest[:, h:h + 1], None, ALU.mult)
                    nc.vector.tensor_scalar(z[:, h, :], z[:, h, :], rest[:, h:h + 1], bound[:, h:h + 1], ALU.mult,
                                            ALU.add).then_inc(bounded.sem, 1)
            for h in range(HG):
                dve.wait_ge(logged.sem, logged.base + h + 1)
                if first_layer:
                    link(nc.vector.tensor_tensor(z[:, h, :], z[:, h, :], E1[:, h, :], ALU.add))
                link(nc.vector.tensor_tensor_scan(z[:, h, :], c.block_reset, z[:, h, :], 0.0, ALU.mult, ALU.add))
                B = blocks(z[:, h, :])
                nc.vector.tensor_tensor(blocks(M[:, h, :]), B, B[:, :, L // 2 - 1:L // 2].to_broadcast([P, NB, L]), ALU.subtract)
                nc.vector.tensor_tensor(blocks(out[:, h, :]), B[:, :, L - 1:L].to_broadcast([P, NB, L]), B, ALU.subtract)\
                    .then_inc(bsummed.sem, 1)
            for h in range(HG):
                dve.wait_ge(exped.sem, exped.base + h + 1)
                nc.vector.tensor_tensor(E1[:, h, :], E1[:, h, :], q[:, h, :], ALU.mult)
                nc.vector.tensor_tensor(q[:, h, :], q[:, h, :], z[:, h, :], ALU.mult).then_inc(queries.sem, 1)

            def mask(h):
                dve.wait_ge(scored.sem, scored.base + h + 1)
                if h >= 2:
                    dve.wait_ge(made.sem, made.base + h - 1)
                nc.vector.tensor_tensor(mk[h % 2], ps[:, 4, 0:T].rearrange("p (t s) -> p t s", t=TT),
                                        c.block_causal.unsqueeze(1).to_broadcast([P, TT, P]), ALU.mult).then_inc(masked.sem, 1)

            def states(h):
                dve.wait_ge(drive_taken.sem, drive_taken.base + h + 1)
                if h >= 2:
                    dve.wait_ge(made.sem, made.base + h - 1)
                ins = nc.vector.tensor_copy(st[h % 2][:, 0, :], drive[h % 2][:, 0, :])
                for n in range(1, NB - 1):
                    link(ins)
                    ins = nc.vector.scalar_tensor_tensor(
                        out=st[h % 2][:, n, :], in0=st[h % 2][:, n - 1, :], scalar=z[:, h, L * n + L - 1:L * n + L],
                        in1=drive[h % 2][:, n, :], op0=ALU.mult, op1=ALU.add)
                ins.then_inc(stated.sem, 1)

            def take_sums(h):
                dve.wait_ge(square_summed.sem, square_summed.base + h + 1)
                nc.vector.tensor_copy(sums[:, h, :], ps[:, 7, 0:T]).then_inc(sums_taken.sem, 1)

            mask(0)
            for h in range(HG):
                states(h)
                if h + 1 < HG:
                    mask(h + 1)
                if h >= 2:
                    take_sums(h - 2)
            take_sums(HG - 2)
            take_sums(HG - 1)
            dve.wait_ge(rooted.sem, rooted.base + 1)
            link(nc.vector.reciprocal(sums, sums))
            for h in range(HG):
                nc.vector.scalar_tensor_tensor(out=out[:, h, :], in0=out[:, h, :], scalar=norm_gain, in1=sums[:, h, :],
                                               op0=ALU.mult, op1=ALU.mult).then_inc(scaled.sem, 1)

        @block.gpsimd
        def _(pool):
            for h in range(HG):
                pool.wait_ge(exped.sem, exped.base + h + 1)
                nc.gpsimd.tensor_tensor(E2[:, h, :], E2[:, h, :], K[:, h, :], ALU.mult)
                nc.gpsimd.tensor_tensor(out[:, h, :], out[:, h, :], K[:, h, :], ALU.mult).then_inc(keys.sem, 1)
            for h in range(HG):
                pool.wait_ge(scaled.sem, scaled.base + h + 1)
                nc.gpsimd.tensor_tensor(out[:, h, :], out[:, h, :], gate[:, h, :], ALU.mult)

        @block.tensor
        def _(pe):
            def score(h):
                pe.wait_ge(queries.sem, queries.base + h + 1)
                pe.wait_ge(keys.sem, keys.base + h + 1)
                if h:
                    pe.wait_ge(turned_taken.sem, turned_taken.base + h)
                    pe.wait_ge(masked.sem, masked.base + h)
                for t in range(TT):
                    at = slice(P * t, P * t + P)
                    nc.tensor.matmul(ps[:, 4, at], E2[:, h, at], E1[:, h, at], start=True, stop=True)
                    last = nc.tensor.transpose(ps[:, 5, at], out[:, h, at], c.ident)
                last.then_inc(scored.sem, 1)

            def drives(h):
                pe.wait_ge(turned_taken.sem, turned_taken.base + h + 1)
                if h:
                    pe.wait_ge(drive_taken.sem, drive_taken.base + h)
                for t in range(TT):
                    for n in range(4):
                        rows = slice(L * n, L * n + L)
                        last = nc.tensor.matmul(ps[:, n, P * t:P * t + P], kt[h % 2][rows, t, :],
                                                v[rows, t, P * h:P * h + P], start=True, stop=True)
                last.then_inc(driven.sem, 1)

            def output(h):
                pe.wait_ge(masked.sem, masked.base + h + 1)
                pe.wait_ge(stated.sem, stated.base + h + 1)
                if h:
                    pe.wait_ge(kept.sem, kept.base + h)
                for t in range(TT):
                    nc.tensor.matmul(ps[:, 6, P * t:P * t + P], v[:, t, P * h:P * h + P], mk[h % 2][:, t, :],
                                     start=(t == 0), stop=False, skip_group_check=True)
                for n in range(1, NB):
                    last = nc.tensor.matmul(ps[:, 6, L * n:L * n + L], st[h % 2][:, n - 1, :], q[:, h, L * n:L * n + L],
                                            start=False, stop=(n == NB - 1), skip_group_check=True)
                last.then_inc(made.sem, 1)

            def square_sum(h):
                pe.wait_ge(kept.sem, kept.base + h + 1)
                if h:
                    pe.wait_ge(sums_taken.sem, sums_taken.base + h)
                nc.tensor.matmul(ps[:, 7, 0:T], c.ones, sq[h % 2], start=True, stop=True).then_inc(square_summed.sem, 1)

            score(0)
            for h in range(HG):
                drives(h)
                if h + 1 < HG:
                    score(h + 1)
                if h:
                    output(h - 1)
                if h >= 2:
                    square_sum(h - 2)
            output(HG - 1)
            square_sum(HG - 2)
            square_sum(HG - 1)
    for s in signals(c, *names):
        s.advance(HG)
    rooted.advance(1)
    scaled.advance(HG)


ALPHA = (2.0 * 2) ** 0.25
EXPERTS = 8


def bounds_stage(c, raw, bound, rest):
    nc = c.nc
    diff_made, = signals(c, "bound_diff_made")
    with nc.Block() as block:
        @block.vector
        def _(dve):
            nc.vector.tensor_tensor(bound, raw[:, HG:2 * HG], raw[:, 0:HG], ALU.subtract).then_inc(diff_made.sem, 1)

        @block.scalar
        def _(act):
            act.wait_ge(diff_made.sem, diff_made.base + 1)
            nc.scalar.activation(rest, bound, ACT.Sigmoid, scale=-1.0).then_inc(c.achain.sem, 1)
            c.achain.n += 1
            act.wait_ge(c.achain.sem, c.achain.n)
            c.achain(act, nc.scalar.activation(bound, bound, ACT.Sigmoid))
    diff_made.advance(1)


def weigh_add_stage(c, total, part):
    with c.nc.Block() as block:
        @block.vector
        def _(dve):
            c.vchain(dve, c.nc.vector.tensor_tensor(total, total, part, ALU.add))


def gated_fm(c, dst, gate):
    return lambda g, r: c.nc.vector.tensor_tensor(dst[:, bass.ds(g * 2, 2), :], r, gate[:, bass.ds(g * 2, 2), :], ALU.mult)


def route_stage(c, router, lower, earlier, r):
    nc, ps = c.nc, c.ps
    E = EXPERTS
    logits_made, diff_made, exp_made, chosen_made, placed = signals(
        c, "logits_made", "logit_diff_made", "logit_exp_made", "chosen_made", "placed")
    w = c.work
    lg = w[:, 0:2 * E].rearrange("p (t e) -> p t e", t=TT)
    gt = w[:, 64:64 + 2 * E * E].rearrange("p (t e f) -> p t e f", t=TT, e=E)
    eq = w[:, 256:256 + 2 * E * E].rearrange("p (t e f) -> p t e f", t=TT, e=E)
    rank, one, two_, tmp = (w[:, 400 + 16 * n:416 + 16 * n].rearrange("p (t e) -> p t e", t=TT) for n in range(4))
    s = lambda n: w[:, 500 + 2 * n:502 + 2 * n]
    with nc.Block() as block:
        @block.tensor
        def _(pe):
            for t in range(TT):
                for k in range(KD):
                    last = nc.tensor.matmul(ps[:, t, 0:E], c.hT[:, k, P * t:P * t + P], router[:, k, :], start=(k == 0),
                                            stop=(k == KD - 1))
            last.then_inc(logits_made.sem, 1)
            pe.wait_ge(chosen_made.sem, chosen_made.base + 1)
            nc.tensor.matmul(ps[:, 2, 0:E], earlier, r.chosen[:, 0], start=True, stop=True)
            nc.tensor.matmul(ps[:, 2, E:2 * E], earlier, r.chosen[:, 1], start=True, stop=False)
            nc.tensor.matmul(ps[:, 2, E:2 * E], c.ones, r.chosen[:, 0], start=False, stop=True)
            for t in range(TT):
                last = nc.tensor.matmul(ps[:, 2, 2 * E:3 * E], c.ones, r.chosen[:, t], start=(t == 0), stop=(t == TT - 1))
            last.then_inc(placed.sem, 1)

        @block.vector
        def _(dve):
            link = lambda ins: c.vchain(dve, ins)
            V = nc.vector
            dve.wait_ge(logits_made.sem, logits_made.base + 1)
            link(V.tensor_copy(lg, ps[:, 0:TT, 0:E]))
            for t in range(TT):
                other = lg[:, t].unsqueeze(1).to_broadcast([P, E, E])
                own = lg[:, t].unsqueeze(2).to_broadcast([P, E, E])
                link(V.tensor_tensor(gt[:, t], other, own, ALU.is_gt))
                link(V.tensor_tensor(eq[:, t], other, own, ALU.is_equal))
                link(V.tensor_tensor(eq[:, t], eq[:, t], lower, ALU.mult))
                link(V.tensor_tensor(gt[:, t], gt[:, t], eq[:, t], ALU.add))
            link(V.tensor_reduce(rank, gt, axis=AX.X, op=ALU.add))
            link(V.tensor_scalar(one, rank, 0.0, None, ALU.is_equal))
            link(V.tensor_scalar(two_, rank, 1.0, None, ALU.is_equal))
            V.tensor_tensor(r.chosen, one, two_, ALU.add).then_inc(chosen_made.sem, 1)
            link(V.tensor_tensor(tmp, one, two_, ALU.subtract))
            link(V.tensor_tensor(tmp, tmp, lg, ALU.mult))
            link(V.tensor_reduce(s(0), tmp, axis=AX.X, op=ALU.add))
            V.tensor_scalar(s(1), s(0), -1.0, None, ALU.mult).then_inc(diff_made.sem, 1)
            dve.wait_ge(exp_made.sem, exp_made.base + 1)
            link(V.tensor_scalar(s(3), s(2), 1.0, None, ALU.add))
            link(V.reciprocal(s(4), s(3)))
            link(V.tensor_tensor(s(5), s(2), s(4), ALU.mult))
            for t in range(TT):
                link(V.tensor_scalar(tmp[:, t], two_[:, t], s(5)[:, t:t + 1], None, ALU.mult))
                link(V.scalar_tensor_tensor(out=r.weight[:, t], in0=one[:, t], scalar=s(4)[:, t:t + 1], in1=tmp[:, t],
                                            op0=ALU.mult, op1=ALU.add))
            dve.wait_ge(placed.sem, placed.base + 1)
            link(V.tensor_copy(r.place, ps[:, 2, 0:2 * E].rearrange("p (t e) -> p t e", t=TT)))
            link(V.tensor_reduce(s(0)[:, 0:1], ps[:, 2, 2 * E:3 * E], axis=AX.X, op=ALU.max))
            link(V.tensor_copy(r.most, s(0)[0:1, 0:1]))

        @block.scalar
        def _(act):
            act.wait_ge(diff_made.sem, diff_made.base + 1)
            nc.scalar.activation(s(2), s(1), ACT.Exp).then_inc(exp_made.sem, 1)
    for sig in (logits_made, diff_made, exp_made, chosen_made, placed):
        sig.advance(1)


def spread_stage(c, weight, mix):
    nc, ps = c.nc, c.ps
    spread, = signals(c, "mix_spread")
    with nc.Block() as block:
        @block.tensor
        @when(c)
        def _(pe):
            for e in range(EXPERTS):
                for t in range(TT):
                    at = T * (e % 2) + P * t
                    last = nc.tensor.matmul(ps[:, 4 + e // 2, at:at + P], weight[:, t, e:e + 1].to_broadcast([P, P]),
                                            c.ident, start=True, stop=True)
                if e % 2:
                    last.then_inc(spread.sem, 1)

        @block.vector
        @when(c)
        def _(dve):
            for b in range(4):
                dve.wait_ge(spread.sem, spread.base + b + 1)
                c.vchain(dve, nc.vector.tensor_copy(mix[:, 2 * b:2 * b + 2, :],
                                                    ps[:, 4 + b, :].rearrange("p (e t) -> p e t", e=2)))
    spread.advance(4)


SLOTS = 128


def gather_stage(c, r, iota, taken_from, given_to, picks, weighed):
    nc, ps, E = c.nc, c.ps, EXPERTS
    picked, weighed_made, turned, turned_taken, gathered, taken = signals(
        c, "moe_picked", "moe_weighed", "moe_turned", "moe_turned_taken", "moe_gathered", "moe_taken")
    with nc.Block() as block:
        @block.vector
        @when(c)
        def _(dve):
            for scale, dst, made in ((r.chosen, picks, picked), (r.weight, weighed, weighed_made)):
                for e in range(E):
                    for t in range(TT):
                        last = nc.vector.tensor_scalar(dst[:, t, e, :], iota, r.place[:, t, e:e + 1], scale[:, t, e:e + 1],
                                                       ALU.is_equal, ALU.mult)
                    last.then_inc(made.sem, 1)

        @block.tensor
        @when(c)
        def _(pe):
            n = 0
            for half in range(2):
                pe.wait_ge(picked.sem, picked.base + 4 * half + 4)
                for k in range(KD):
                    if n >= 4:
                        pe.wait_ge(taken.sem, taken.base + n - 3)
                    for t in range(TT):
                        last = nc.tensor.matmul(ps[:, n % 4, :], c.x[:, t, P * k:P * k + P],
                                                picks[:, t, 4 * half:4 * half + 4, :].rearrange("p e s -> p (e s)"),
                                                start=(t == 0), stop=(t == TT - 1))
                    last.then_inc(gathered.sem, 1)
                    n += 1
            for b in range(4):
                pe.wait_ge(weighed_made.sem, weighed_made.base + 2 * b + 2)
                for e in range(2):
                    for t in range(TT):
                        at = T * e + P * t
                        last = nc.tensor.transpose(ps[:, 4 + b, at:at + P], weighed[:, t, 2 * b + e, :], c.ident)
                last.then_inc(turned.sem, 1)

        @block.scalar
        @when(c)
        def _(act):
            for n in range(2 * KD):
                act.wait_ge(gathered.sem, gathered.base + n + 1)
                half, k = n // KD, n % KD
                nc.scalar.activation(taken_from[:, 4 * half:4 * half + 4, k, :],
                                     ps[:, n % 4, :].rearrange("p (e s) -> p e s", e=4), ACT.Copy).then_inc(taken.sem, 1)
            for b in range(4):
                act.wait_ge(turned.sem, turned.base + b + 1)
                nc.scalar.activation(given_to[:, 2 * b:2 * b + 2, :], ps[:, 4 + b, :].rearrange("p (e t) -> p e t", e=2),
                                     ACT.Copy).then_inc(turned_taken.sem, 1)


def experts_stage(c, w_gate, w_up, w_down, G, inputs, outputs):
    nc, ps, E = c.nc, c.ps, EXPERTS
    assert G % 2 == 0
    loaded = signals(c, "moe_loaded0", "moe_loaded1")
    gate_made, up_made, silu_made, hidden_made, hidden_used, output_taken = signals(
        c, "moe_gate_made", "moe_up_made", "moe_silu_made", "moe_hidden_made", "moe_hidden_used", "moe_output_taken")
    lb = [s.base for s in loaded]
    gb, pb, sb, hb, hub, ob = (s.base for s in (gate_made, up_made, silu_made, hidden_made, hidden_used, output_taken))
    wg = [c.slots[3 * s].rearrange("p (k f) -> p k f", k=KD) for s in range(2)]
    wu = [c.slots[3 * s + 1].rearrange("p (k f) -> p k f", k=KD) for s in range(2)]
    wd = [c.slots[3 * s + 2].rearrange("p (h n) -> p h n", h=2) for s in range(2)]
    silu = [c.work[:, P * n:P * n + P] for n in range(4)]
    hidden = [c.work[:, P * (4 + n):P * (5 + n)] for n in range(4)]

    def each_step(eng, e, body):
        with eng.Fori(0, G // 2) as i:
            for s in range(2):
                body(s, i + e * (G // 2), i * 2 + (e * G + s))

    with nc.Block() as block:
        @block.sync
        @when(c)
        def _(sp):
            def load(s, pair, step):
                sp.wait_ge(hidden_used.sem, step * 2 + (hub - 2))
                for w, dst in ((w_gate, 3 * s), (w_up, 3 * s + 1), (w_down, 3 * s + 2)):
                    src = w[bass.ds(step, 1), :, :].rearrange("o p n -> p (o n)")
                    sp.dma_start(c.slots[dst], src).then_inc(loaded[s].sem, 16)
            with sp.Fori(0, E * G // 2) as i:
                for s in range(2):
                    load(s, i, i * 2 + s)

        @block.scalar
        @when(c)
        def _(act):
            def gate(s, pair, step):
                for h in range(2):
                    act.wait_ge(gate_made.sem, step * 2 + (gb + h + 1))
                    act.wait_ge(hidden_made.sem, step * 2 + (hb + h - 3))
                    nc.scalar.activation(silu[2 * s + h], ps[:, 2 * h, 0:SLOTS], ACT.Silu).then_inc(silu_made.sem, 1)
            for e in range(E):
                each_step(act, e, gate)
                act.wait_ge(hidden_used.sem, hub + 2 * G * (e + 1))
                y = 4 + 2 * (e % 2)
                nc.scalar.activation(outputs[:, e, :].rearrange("p (a n) -> p a n", a=2), ps[:, y:y + 2, :],
                                     ACT.Copy).then_inc(output_taken.sem, 1)

        @block.vector
        @when(c)
        def _(dve):
            def make(s, pair, step):
                for h in range(2):
                    dve.wait_ge(silu_made.sem, step * 2 + (sb + h + 1))
                    dve.wait_ge(up_made.sem, step * 2 + (pb + h + 1))
                    dve.wait_ge(hidden_used.sem, step * 2 + (hub + h - 3))
                    nc.vector.tensor_tensor(hidden[2 * s + h], silu[2 * s + h], ps[:, 2 * h + 1, 0:SLOTS], ALU.mult)\
                        .then_inc(hidden_made.sem, 1)
            with dve.Fori(0, E * G // 2) as i:
                for s in range(2):
                    make(s, i, i * 2 + s)

        @block.tensor
        @when(c)
        def _(pe):
            for e in range(E):
                y = 4 + 2 * (e % 2)

                def edge(start, stop):
                    for n in range(2):
                        nc.tensor.matmul(ps[:, y + n, :], c.zeros[:, 0:P], c.zeros, start=start, stop=stop,
                                         skip_group_check=True)

                def products(s, pair, step):
                    pe.wait_ge(loaded[s].sem, pair * 48 + (lb[s] + 48))
                    for h in range(2):
                        pe.wait_ge(hidden_made.sem, step * 2 + (hb + h - 1))
                        for w, bank, made in ((wg, 2 * h, gate_made), (wu, 2 * h + 1, up_made)):
                            for k in range(KD):
                                last = nc.tensor.matmul(ps[:, bank, 0:SLOTS], w[s][:, k, P * h:P * h + P],
                                                        inputs[:, e, k, :], start=(k == 0), stop=(k == KD - 1))
                            last.then_inc(made.sem, 1)
                    for h in range(2):
                        pe.wait_ge(hidden_made.sem, step * 2 + (hb + h + 1))
                        for n in range(2):
                            last = nc.tensor.matmul(ps[:, y + n, :], hidden[2 * s + h], wd[s][:, h, 512 * n:512 * n + 512],
                                                    start=False, stop=False, skip_group_check=True)
                        last.then_inc(hidden_used.sem, 1)

                if e >= 2:
                    pe.wait_ge(output_taken.sem, ob + e - 1)
                edge(True, False)
                each_step(pe, e, products)


def combine_stage(c, given_to, outputs, keep):
    nc, ps, x = c.nc, c.ps, c.x
    combined, = signals(c, "moe_combined")
    with nc.Block() as block:
        @block.tensor
        @when(c)
        def _(pe):
            for t in range(TT):
                for n in range(2):
                    for e in range(EXPERTS):
                        last = nc.tensor.matmul(ps[:, 2 * t + n, :], given_to[:, e, P * t:P * t + P],
                                                outputs[:, e, 512 * n:512 * n + 512], start=(e == 0), stop=(e == EXPERTS - 1))
                    last.then_inc(combined.sem, 1)

        @block.vector
        @when(c)
        def _(dve):
            for t in range(TT):
                for n in range(2):
                    dve.wait_ge(combined.sem, combined.base + 2 * t + n + 1)
                    xn = x[:, t, 512 * n:512 * n + 512]
                    c.vchain(dve, nc.vector.scalar_tensor_tensor(out=xn, in0=xn, scalar=keep, in1=ps[:, 2 * t + n, :],
                                                                 op0=ALU.mult, op1=ALU.add))


class Routing:

    def __init__(self, chosen, weight, place, most):
        self.chosen, self.weight, self.place, self.most = chosen, weight, place, most


def moe_stage(c, router, lower, earlier, iota):
    nc, d, t = c.nc, c.dram, c.tables
    c.parts.close()
    more = c.stack.enter_context(nc.sbuf_tensor("more_slots", [P, 2, KD * GW], F32))[...]
    c.slots = [c.ring[:, n, :] for n in range(4)] + [more[:, n, :] for n in range(2)]
    te = lambda o: t[:, o:o + 16].rearrange("p (t e) -> p t e", t=TT)
    r = Routing(te(4400), te(4416), te(4432), c.most)
    route_stage(c, router, lower, earlier, r)
    G = d["l_moe_gate"].shape[0] // EXPERTS
    weights = (d["l_moe_gate"], d["l_moe_up"], d["l_moe_down"])
    flat = lambda s: s.rearrange("p a b -> p (a b)")
    xg = flat(c.seg).rearrange("p (e k s) -> p e k s", e=EXPERTS, k=KD)
    out = flat(c.seg).rearrange("p (e n) -> p e n", e=EXPERTS)
    picks = flat(c.merged).rearrange("p (t e s) -> p t e s", t=TT, e=EXPERTS)
    weighed = c.work[:, 0:2048].rearrange("p (t e s) -> p t e s", t=TT, e=EXPERTS)
    chain, mix = c.vchain, c.seg[:, 0:8]
    c.condition, c.vchain = lambda most: most > SLOTS, c.dense_chain
    spread_stage(c, r.weight, mix)
    ffn_stage(c, *weights, G, EXPERTS, mix, keep=ALPHA, add=1.0)
    c.condition, c.vchain = lambda most: most <= SLOTS, c.gathered_chain
    gather_stage(c, r, iota, xg, c.cat, picks, weighed)
    experts_stage(c, *weights, G, xg, out)
    combine_stage(c, c.cat, out, ALPHA)
    c.condition, c.vchain = None, chain


def second_start(c):
    d, t = c.dram, c.tables
    norm_stage(c, gain_tm=d["final_norm_w"])
    norm_stage(c, layer=(d["ln_in_g"], d["ln_in_b"]))
    second_tables(c)


def second_tables(c):
    load_stage(c, [(c.tables[:, 0:4392], c.dram["l_second_tables"])])
    bounds_stage(c, c.tables[:, 4224:4240], c.bound[:, 0:HG], c.bound[:, HG:2 * HG])


def second_layer(c, layer):
    d, seg, vtm, t = c.dram, c.seg, c.vtm, c.tables
    decay = t[:, 0:2048].rearrange("p (h s t) -> p h s t", h=RET_HEADS, s=TT)
    rot, cos, sin = t[:, 2048:2176], t[:, 2176:2432], t[:, 2432:2688]
    c.block_causal, c.block_reset = t[:, 2688:2816], t[:, 2816:3072]
    mask = t[:, 3072:3584].rearrange("p (t k) -> p t k", t=TT)
    router = t[:, 3584:3648].rearrange("p (k e) -> p k e", k=KD)
    lower = t[:, 3648:3712].rearrange("p (e f) -> p e f", e=EXPERTS)
    sinks = t[:, 3712 + 16 * layer:3728 + 16 * layer]
    hg_gain = t[:, 3744 + layer:3745 + layer]
    w, wo = d["l_w_in"][46 * layer:46 * layer + 46], d["l_outs"][16 * layer:16 * layer + 16]

    def gated(n, gate, first):
        dst = c.merged if first else seg[:, 8:16]
        project_stage(c, [product(c, wo[4 * n:4 * n + 4], 4, gated_fm(c, dst, gate), src=c.cat)], "vector")
        if not first:
            weigh_add_stage(c, c.merged, dst)

    project_stage(c, [product(c, w[0:4], 4, to_fm(c, seg[:, 0:8])), product(c, w[4:8], 4, to_tm(c, vtm), tm=True),
                      product(c, w[8:12], 4, to_fm(c, seg[:, 8:16], ACT.Silu)),
                      product(c, w[34:38], 4, to_fm(c, seg[:, 16:24], ACT.Sigmoid))])
    rope_stage(c, seg[:, 0:8], rot, cos, sin)
    retention_stage(c, seg[:, 0:4], seg[:, 4:8], vtm, decay, seg[:, 8:16], c.cat)
    gated(0, seg[:, 16:24], True)
    project_stage(c, [product(c, w[12:20], 8, to_fm(c, seg[:, 0:16])), product(c, w[20:24], 4, to_tm(c, vtm), tm=True),
                      product(c, w[24:28], 4, to_fm(c, seg[:, 16:24], ACT.Silu)),
                      product(c, w[38:42], 4, to_fm(c, seg[:, 24:32], ACT.Sigmoid))])
    hgrn_stage(c, seg[:, 0:8], seg[:, 8:16], vtm, seg[:, 16:24], c.bound[:, 0:HG], c.bound[:, HG:2 * HG], layer == 0,
               hg_gain, c.cat)
    gated(1, seg[:, 24:32], False)
    project_stage(c, [product(c, w[28:32], 4, to_fm(c, seg[:, 0:8])),
                      product(c, d["l_twice_sk"][2 * layer:2 * layer + 2], 2, to_fm(c, seg[:, 16:20])),
                      product(c, w[33:34], 1, to_tm(c, vtm), tm=True),
                      product(c, w[42:46], 4, to_fm(c, seg[:, 24:32], ACT.Sigmoid))])
    groups = []
    for g in range(4):
        for qt in range(TT):
            nk = P * (qt + 1)
            groups.append(([Pass(
                q=lambda p, j, g=g, qt=qt: seg[HD * p:HD * p + HD, 2 * g + j, P * qt:P * qt + P],
                k=lambda p, g=g, nk=nk: seg[HD * p:HD * p + HD, 16 + g, 0:nk], nk=nk,
                v=[vtm[:, l, HD * g:HD * g + HD] for l in range(qt + 1)], mask=mask[:, qt, 0:nk],
                sinks=sinks[:, 4 * g:4 * g + 4], gates=None, valid=None)],
                c.cat[:, 2 * g:2 * g + 2, P * qt:P * qt + P]))
    attention_stage(c, groups, HD ** -0.5)
    gated(2, seg[:, 24:32], False)
    project_stage(c, [product(c, wo[12:16], 4, add_to_x(c, ALPHA), tm=True, src=c.merged)], "vector")
    norm_stage(c, layer=(d["ln_mix_g"][layer], d["ln_mix_b"][layer]))
    if layer == 0:
        split_ffn_stage(c, d["l_ffn2_gate"], d["l_ffn2_up"], d["l_ffn2_down"], keep=ALPHA, add=1.0)
    else:
        moe_stage(c, router, lower, t[:, 3760:3888], t[:, 3888:4016])
    norm_stage(c, layer=(d["ln_ffn_g"][layer], d["ln_ffn_b"][layer]))


def start_stage(c):
    nc = c.nc
    loads = [(c.x, c.dram["x"].rearrange("o (t p) d -> p (o t) d", p=P)), (c.ident, c.dram["c_ident"]),
             (c.gains, c.dram["l_gains"])]
    first, = signals(c, "first_loaded")
    with nc.Block() as block:
        @block.sync
        def _(sp):
            for dst, src in loads:
                sp.dma_start(dst, src).then_inc(first.sem, 16)
            sp.wait_ge(first.sem, START + 16 * len(loads))

        @block.vector
        def _(dve):
            nc.vector.memset(c.zeros, 0.0)
            nc.vector.memset(c.ones, 1.0)
            nc.vector.memset(c.eps, RMS_EPS)


def end_stage(c):
    nc = c.nc
    stored, = signals(c, "stored")
    with nc.Block() as block:
        @block.sync
        def _(sp):
            sp.dma_start(c.dram["out"].rearrange("o (t p) d -> p (o t) d", p=P), c.x).then_inc(stored.sem, 16)
            sp.wait_ge(stored.sem, START + 16)


SIGNALS = ("stat_ready root_ready normed packed unloaded gains_loaded ffn_loaded0 ffn_loaded1 gate_made up_made "
           "silu_made weighed hidden_made hidden_used summed first_loaded stored vector_chain scalar_chain dense_chain gathered_chain "
           "weights_loaded0 weights_loaded1 product_made product_taken rope_turned rope_scaled roped scored biased "
           "exped factored weighted probs_turned turned_taken attended output_taken tables_loaded gm_var_made "
           "gm_root_made gm_normed gm_mixed cmp_hidden cmp_pe_made cmp_pe_taken cmp_gelued cmp_second cmp_rotated "
           "cmp_flipped pooled pooled_taken pool_mixed s5_angle_reduced s5_sines s5_driven s5_rotated "
           "s5_scanned s5_unrotated s5_read s5_skipped ret_scored ret_decayed ret_summed ret_kept ret_squared "
           "ret_square_summed ret_rooted ret_scaled ret_gated hg_sigmoid hg_bounded hg_logged hg_summed hg_exped "
           "hg_queries hg_keys hg_scored hg_turned_taken hg_masked hg_driven hg_drive_taken hg_stated hg_made hg_kept "
           "hg_square_summed hg_sums_taken hg_rooted hg_scaled bound_diff_made logits_made logit_diff_made "
           "logit_exp_made mix_spread chosen_made placed moe_picked moe_weighed moe_turned moe_turned_taken moe_gathered "
           "moe_taken moe_loaded0 moe_loaded1 moe_gate_made moe_up_made moe_silu_made moe_hidden_made moe_hidden_used "
           "moe_output_taken moe_combined input_high input_low weight_high_made weight_low_made unit_loaded0 unit_loaded1 "
           "unit_loaded2 unit_high unit_low_dve unit_low_pool s_down_made s_gate_made s_up_made s_silu_made "
           "s_hidden_made s_hidden_high s_hidden_low s_summed").split()


def allocate(c):
    nc = c.nc

    def sb(name, *shape):
        c.bytes = c.bytes + int(np.prod(shape)) * 4
        return c.stack.enter_context(nc.sbuf_tensor(name, [P, *shape], F32))[...]

    c.bytes = 0
    c.x = sb("x", TT, D)
    c.hT = sb("hT", KD, T)
    c.ring = sb("ring", 4, KD * GW)
    c.work = sb("work", 4096)
    c.rowbuf = sb("rowbuf", 2, D)
    c.small = sb("small", 64)
    c.ident = sb("ident", P)
    c.gains = sb("gains_fm", 6 * KD)
    c.zeros = c.stack.enter_context(nc.sbuf_tensor("zeros", [32, 512], mybir.dt.bfloat16))[...]
    c.ones = sb("ones", P)
    c.seg = sb("seg", 32, T)
    c.merged = sb("merged", KD, T)
    c.bound = sb("bound", 2 * HG)
    c.eps = sb("eps", 1)
    c.vtm = sb("vtm", TT, D)
    c.cat = sb("cat", KD, T)
    c.tables = sb("tables", 4800)
    c.most = c.stack.enter_context(nc.sbuf_tensor("most", [1, 1], mybir.dt.int32))[...]
    c.parts = c.stack.enter_context(ExitStack())
    part = lambda n, *shape: c.parts.enter_context(nc.sbuf_tensor(n, [P, *shape], mybir.dt.float32r))[...]
    c.act_high, c.act_low = part("act_high", KD, T), part("act_low", KD, T)
    c.weight_high, c.weight_low = part("weight_high", 2, KD * GW), part("weight_low", 2, KD * GW)
    c.hidden_high, c.hidden_low = part("hidden_high", 2, T), part("hidden_low", 2, T)
    c.ps = c.stack.enter_context(nc.psum_tensor("ps", [P, 8, 512], F32))[...]


def program(nc, dram, stages):
    with ExitStack() as stack:
        c = Core(nc, dram, stack)
        allocate(c)
        signals(c, *SIGNALS)
        c.vchain = Chain(c.sig["vector_chain"].sem)
        c.dense_chain, c.gathered_chain = (Chain(c.sig[n].sem) for n in ("dense_chain", "gathered_chain"))
        c.achain = Chain(c.sig["scalar_chain"].sem)
        with nc.Block() as block:
            @block.gpsimd
            def _(pool):
                for s in c.sig.values():
                    nc.gpsimd.sem_inc(s.sem, START)
        start_stage(c)
        for s in stages:
            run_stage(c, s)
        end_stage(c)


def run_stage(c, s):
    d = c.dram
    kind, *a = s
    if kind == "ffn1":
        layer, half = a
        n = 3 * layer + 2 * half
        norm_stage(c, gain_fm=c.gains[:, KD * n:KD * n + KD])
        i = 2 * layer + half
        g = d["l_ffn_gate"].shape[0] // 4
        split_ffn_stage(c, *(d[w][i * g:(i + 1) * g] for w in ("l_ffn_gate", "l_ffn_up", "l_ffn_down")))
    if kind == "even":
        even_mixer(c)
    if kind == "odd":
        odd_mixer(c)
    if kind == "second":
        second_start(c)
    if kind == "tables":
        second_tables(c)
    if kind == "moe":
        t = c.tables
        moe_stage(c, t[:, 3584:3648].rearrange("p (k e) -> p k e", k=KD),
                  t[:, 3648:3712].rearrange("p (e f) -> p e f", e=EXPERTS), t[:, 3760:3888], t[:, 3888:4016])
    if kind == "ln":
        norm_stage(c, layer=(d["ln_in_g"], d["ln_in_b"]))
    if kind == "layer":
        second_layer(c, *a)


def pack_in(w):
    k, n = w.shape
    return np.ascontiguousarray(w.reshape(k // P, P, n // GW, GW).transpose(2, 1, 0, 3)).reshape(n // GW, P, -1)


def pack_down(w):
    f, n = w.shape
    return np.ascontiguousarray(w.reshape(f // GW, 2, P, n).transpose(0, 2, 1, 3)).reshape(f // GW, P, -1)


def columns(v):
    return np.ascontiguousarray(v.reshape(-1, P).T)


def layout(i):
    i = {k: np.asarray(v) for k, v in i.items()}
    a = {"x": i["x"]}
    a["c_ident"] = np.eye(P, dtype=np.float32)
    a["l_gains"] = columns(i["norm_w"])
    a["l_ffn_gate"] = np.concatenate([pack_in(w) for l in i["ffn_w_gate"] for w in l])
    a["l_ffn_up"] = np.concatenate([pack_in(w) for l in i["ffn_w_up"] for w in l])
    a["l_ffn_down"] = np.concatenate([pack_down(w) for l in i["ffn_w_down"] for w in l])
    even_layout(i, a)
    odd_layout(i, a)
    second_layout(i, a)
    return a


def rope_tables(pos, half, steps):
    inv = (np.float32(10000.0) ** -steps).astype(np.float32)
    ang = (pos.astype(np.float32)[:, None] * inv[None, :]).astype(np.float32)
    return np.cos(ang).astype(np.float32), np.sin(ang).astype(np.float32)


def rotation(width):
    r, h = np.zeros((P, P), np.float32), width // 2
    for o in range(0, P, width):
        for n in range(h):
            r[o + h + n, o + n] = -1.0
            r[o + n, o + h + n] = 1.0
    return r


def even_layout(i, a):
    w = i["ev_w_in"][0]
    cut = np.cumsum([0, 512, 512, 512, 128, 128, 128, 128, 128, 128, 24])
    u, v, q, kc, vc, ks, vs, kw, vw, gl = (w[:, cut[n]:cut[n + 1]] for n in range(10))
    twice = lambda k: [k[:, 0:64], k[:, 0:64], k[:, 64:128], k[:, 64:128]]
    a["l_ev_in"] = pack_in(np.concatenate(
        [u, q, *twice(ks), *twice(kw), kc, vc, v, vs, vw, gl, np.zeros((D, GW - 24), np.float32)], axis=1))
    a["l_ev_out"] = pack_in(i["ev_w_out"][0])
    t = np.arange(T)
    qt = t.reshape(TT, P).T
    wT = i["gm_w_s"][0].transpose(2, 0, 1).reshape(P, -1)
    b = i["gm_b"][0]
    bias = np.repeat(np.tile(b, (1, TT)).reshape(4, 2, T), HD, axis=1).transpose(1, 0, 2).reshape(P, -1)
    causal = (np.arange(P)[:, None] <= np.arange(P)[None, :]).astype(np.float32)
    w2 = np.tile(i["nsa_cmp_w2"][0].transpose(1, 0, 2).reshape(HD, -1), (2, 1))
    pe = np.tile(i["nsa_cmp_pe"][0].transpose(2, 0, 1).reshape(HD, -1), (2, 1))
    steps = np.arange(32, dtype=np.float32) / 32
    cos, sin = rope_tables(t, 32, steps)
    fm = lambda m: np.tile(m.T, (4, 1))
    end = np.arange(NCMP) * CMP_STRIDE + CMP_LEN - 1
    cc, cs = rope_tables(end, 32, steps)
    pad = lambda m: np.concatenate([m, np.zeros((P - NCMP, 32), np.float32)])
    amask = np.where(t[None, None, :] <= qt[:, :, None], 0.0, NEG).astype(np.float32)
    cm = np.where(end[None, None, :] <= qt[:, :, None], 0.0, NEG).astype(np.float32)
    cmask = np.concatenate([cm, np.full((P, TT, 1), NEG, np.float32)], axis=2)
    valid = (qt >= end[0]).astype(np.float32)
    a["l_even_tables"] = np.concatenate(
        [wT, bias, causal, w2, pe, rotation(64), fm(cos), fm(sin), pad(cc), pad(cs), amask.reshape(P, -1),
         cmask.reshape(P, -1), valid], axis=1).astype(np.float32)
    a["l_cmp_w1"] = np.tile(i["nsa_cmp_w1"][0].reshape(2, CMP_LEN, HD, HD).transpose(2, 0, 1, 3).reshape(HD, -1), (2, 1))


def odd_layout(i, a):
    a["l_od_in"], a["l_od_out"], a["l_glu"] = (pack_in(i[n][0]) for n in ("od_w_in", "od_w_out", "s5_w_glu"))
    t = np.arange(T)
    ops = []
    for w in POOL_WINDOWS:
        seen = (t[:, None] <= t[None, :]) & (t[:, None] > t[None, :] - w)
        ops.append(seen / np.minimum(t + 1, w)[None, :] - np.eye(T))
    ops = np.stack(ops).astype(np.float32).reshape(4, TT, P, T).transpose(2, 0, 1, 3).reshape(P, -1)
    pw = i["pool_w"][0].transpose(1, 0, 2).reshape(P, -1)
    dt = np.repeat(i["s5_log_dt"][0], 64)
    b_in = np.zeros((2, 4, 4, 2, 16, 2, 64), np.float32)
    c_out = np.zeros((2, NT, 2, 64, 2, 16), np.float32)
    for n, (b, o) in enumerate(((i["s5_b_re"][0], i["s5_c_re"][0]), (i["s5_b_im"][0], i["s5_c_im"][0]))):
        for g in range(2):
            b_in[n, :, :, g, :, g, :] = b.reshape(4, 4, 2, 64, 16)[:, :, g].transpose(0, 1, 3, 2)
            c_out[n, :, g, :, g, :] = o.reshape(NT, 2, 16, 64)[:, g].transpose(0, 2, 1)
    b_in = b_in.reshape(2, 4, P, P).transpose(2, 0, 1, 3).reshape(P, -1)
    c_out = c_out.reshape(2, NT, P, CH).transpose(2, 0, 1, 3).reshape(P, -1)
    a["l_odd_tables"] = np.concatenate(
        [ops, pw, columns(i["pool_scale"]), columns(i["s5_d"]), columns(i["s5_lam_re"]), columns(i["s5_lam_im"]),
         columns(dt), b_in, c_out], axis=1)


def second_layout(i, a):
    for n in ("ln_in_g", "ln_in_b", "ln_mix_g", "ln_mix_b", "ln_ffn_g", "ln_ffn_b"):
        a[n] = i[n + "_2"]
    a["final_norm_w"] = i["final_norm_w"]
    w = i["w_in_2"]
    a["l_w_in"] = np.concatenate([pack_in(m) for m in w])
    sk = w[:, :, 8192:8448]
    a["l_twice_sk"] = np.concatenate([pack_in(np.repeat(m.reshape(D, 4, 1, HD), 2, axis=2).reshape(D, -1)) for m in sk])
    a["l_outs"] = np.concatenate([pack_in(i[n][l]) for l in range(2)
                                  for n in ("ret_w_out_2", "hgrn_w_out_2", "swa_w_out_2", "w_o_2")])
    a["l_ffn2_gate"], a["l_ffn2_up"] = pack_in(i["ffn_w_gate_2"][0]), pack_in(i["ffn_w_up_2"][0])
    a["l_ffn2_down"] = pack_down(i["ffn_w_down_2"][0])
    if "moe_w_gate_2" in i:
        a["l_moe_gate"] = np.concatenate([pack_in(m) for m in i["moe_w_gate_2"][0]])
        a["l_moe_up"] = np.concatenate([pack_in(m) for m in i["moe_w_up_2"][0]])
        a["l_moe_down"] = np.concatenate([pack_down(m) for m in i["moe_w_down_2"][0]])
    t = np.arange(T)
    gap = t[None, :] - t[:, None]
    gamma = 1.0 - 2.0 ** (-5.0 - np.arange(RET_HEADS))
    dec = np.where(gap >= 0, gamma[:, None, None] ** np.maximum(gap, 0), 0.0) * P ** -0.5
    dec = dec.reshape(RET_HEADS, TT, P, T).transpose(2, 0, 1, 3).reshape(P, -1)
    cos, sin = rope_tables(t, 64, np.linspace(0.0, 1.0, 64, dtype=np.float32))
    fm = lambda m: np.tile(m.T, (2, 1))
    p = np.arange(P)
    causal = (p[:, None] <= p[None, :]) & (p[:, None] // L == p[None, :] // L)
    reset = np.broadcast_to(t % L != 0, (P, T))
    chunk = np.arange(T) // 64
    qc = chunk.reshape(TT, P).T[:, :, None]
    mask = np.where((chunk <= qc) & (chunk >= qc - 2), 0.0, NEG).reshape(P, -1)
    router = i["moe_router_2"][0].reshape(KD, P, EXPERTS).transpose(1, 0, 2).reshape(P, -1)
    e = np.arange(EXPERTS)
    lower = np.broadcast_to((e[None, :] < e[:, None]).reshape(1, -1), (P, EXPERTS ** 2))
    sinks = np.broadcast_to(i["swa_sinks_2"].reshape(2, 4, 2, 2).transpose(0, 1, 3, 2).reshape(1, -1), (P, 32))
    gain = i["hgrn_norm_g_2"].T
    earlier = p[:, None] < p[None, :]
    iota = np.broadcast_to(p[None, :], (P, P))
    raw = columns(i["hgrn_lower_bounds_2"])
    a["l_second_tables"] = np.concatenate(
        [dec, rotation(P), fm(cos), fm(sin), causal, reset, mask, router, lower, sinks, gain,
         np.zeros((P, 14)), earlier, iota, np.zeros((P, 4224 - 4016)), raw,
         np.zeros((P, 4392 - 4240))], axis=1).astype(np.float32)


STAGES = [("ffn1", 0, 0), ("even",), ("ffn1", 0, 1), ("ffn1", 1, 0), ("odd",), ("ffn1", 1, 1), ("second",),
          ("layer", 0), ("layer", 1)]


def build(nc, arrays):
    dram = {n: nc.dram_tensor("in_" + n, v.shape, F32, kind="ExternalInput").ap() for n, v in arrays.items()}
    dram["out"] = nc.dram_tensor("out", (1, T, D), F32, kind="ExternalOutput").ap()
    program(nc, dram, STAGES)


def kernel(**inputs):
    import concourse.bacc as bacc
    from concourse.bass_utils import run_bass_kernel_spmd as run

    arrays = layout(inputs)
    nc = bacc.Bacc("TRN2", target_bir_lowering=False, num_devices=1)
    build(nc, arrays)
    r = run(nc, [{"in_" + n: v for n, v in arrays.items()}], core_ids=[0])
    return r.results[0]["out"]
```

```python
from contextlib import ExitStack

import numpy as np
import concourse.bass as bass
from concourse import mybir

F32 = mybir.dt.float32
ALU = mybir.AluOpType
ACT = mybir.ActivationFunctionType
AX = mybir.AxisListType

P = 128
T = 256
D = 1024
TT = T // P
KD = D // P
GW = 256
HD = 64
START = 8
RMS_EPS = 1e-6
LN_EPS = 1e-5
NEG = -1e30


class Core:

    def __init__(self, nc, dram, stack):
        self.nc, self.dram, self.stack, self.sig = nc, dram, stack, {}
        self.condition = None


class Product:

    def __init__(self, w, groups, take, tm, src, cols, kd):
        self.w, self.groups, self.take, self.tm, self.src, self.cols, self.kd = w, groups, take, tm, src, cols, kd


class Pass:

    def __init__(self, q, k, nk, v, mask, sinks, gates, valid):
        self.q, self.k, self.nk, self.v = q, k, nk, v
        self.mask, self.sinks, self.gates, self.valid = mask, sinks, gates, valid


class Signal:

    def __init__(self, sem):
        self.sem, self.base = sem, START

    def advance(self, n):
        self.base += n


class Chain:

    def __init__(self, sem):
        self.sem, self.n = sem, START

    def __call__(self, eng, ins):
        self.n += 1
        ins.then_inc(self.sem, 1)
        eng.wait_ge(self.sem, self.n)


def when(c):
    def wrap(body):
        if c.condition is None:
            return body

        def guarded(eng):
            with eng.If(c.condition(eng.value_load(c.most, min_val=0, max_val=T))):
                body(eng)
        return guarded
    return wrap


def signals(c, *names):
    for n in names:
        if n not in c.sig:
            c.sig[n] = Signal(c.stack.enter_context(c.nc.semaphore(n)))
    return [c.sig[n] for n in names]


def norm_stage(c, gain_fm=None, gain_tm=None, layer=None):
    nc, x, hT, ps = c.nc, c.x, c.hT, c.ps
    stat_ready, root_ready, normed, packed, unloaded, gains = signals(
        c, "stat_ready", "root_ready", "normed", "packed", "unloaded", "gains_loaded")
    high, = signals(c, "input_high")
    b0, r0, n0, p0, u0, g0 = (s.base for s in (stat_ready, root_ready, normed, packed, unloaded, gains))
    inplace = gain_fm is None
    c.parts_of_hT = True
    xs = x if inplace else c.work.rearrange("p (t d) -> p t d", t=TT)[:, :, 0:D]
    rows = [gain_tm] if gain_tm is not None else (list(layer) if layer else [])

    with nc.Block() as block:
        @block.sync
        def _(sp):
            for n, row in enumerate(rows):
                sp.dma_start(c.rowbuf[:, n, :], row.partition_broadcast(P)).then_inc(gains.sem, 16)

        @block.scalar
        def _(act):
            act.wait_ge(stat_ready.sem, b0 + 1)
            nc.scalar.activation(c.small[:, 2:4], c.small[:, 0:2], ACT.Sqrt).then_inc(root_ready.sem, 1)
            for n in range(4):
                act.wait_ge(unloaded.sem, u0 + n + 1)
                part = (slice(None), slice(4 * (n % 2), 4 * (n % 2) + 4), slice(P * (n // 2), P * (n // 2) + P))
                nc.scalar.activation(c.act_high[part], hT[part], ACT.Copy).then_inc(high.sem, 1)

        @block.vector
        def _(dve):
            link = lambda ins: c.vchain(dve, ins)
            if layer:
                for t in range(TT):
                    for h in range(2):
                        link(nc.vector.bn_stats(c.small[:, 32 + 16 * t + 6 * h:38 + 16 * t + 6 * h],
                                                x[:, t, 512 * h:512 * h + 512]))
                for t in range(TT):
                    link(nc.vector.bn_aggr(c.small[:, 16 + 2 * t:18 + 2 * t], c.small[:, 32 + 16 * t:44 + 16 * t]))
                var = c.small[:, 16:20].rearrange("p (t two) -> p t two", two=2)[:, :, 1]
                nc.vector.tensor_scalar(c.small[:, 0:2], var, LN_EPS, None, ALU.add).then_inc(stat_ready.sem, 1)
            else:
                for t in range(TT):
                    link(nc.vector.tensor_tensor_reduce(
                        out=c.work[:, 0:D], in0=x[:, t, :], in1=x[:, t, :], scale=1.0, scalar=0.0,
                        op0=ALU.mult, op1=ALU.add, accum_out=c.small[:, 4 + t:5 + t]))
                nc.vector.tensor_scalar(c.small[:, 0:2], c.small[:, 4:6], 1.0 / D, RMS_EPS,
                                        ALU.mult, ALU.add).then_inc(stat_ready.sem, 1)
            dve.wait_ge(root_ready.sem, r0 + 1)
            link(nc.vector.reciprocal(c.small[:, 6:8], c.small[:, 2:4]))
            if rows:
                dve.wait_ge(gains.sem, g0 + 16 * len(rows))
            for t in range(TT):
                if layer:
                    link(nc.vector.tensor_scalar(xs[:, t, :], x[:, t, :], c.small[:, 16 + 2 * t:17 + 2 * t],
                                                 c.small[:, 6 + t:7 + t], ALU.subtract, ALU.mult))
                    link(nc.vector.tensor_tensor(xs[:, t, :], xs[:, t, :], c.rowbuf[:, 0, :], ALU.mult))
                    nc.vector.tensor_tensor(xs[:, t, :], xs[:, t, :], c.rowbuf[:, 1, :],
                                            ALU.add).then_inc(normed.sem, 1)
                elif gain_tm is not None:
                    nc.vector.scalar_tensor_tensor(
                        out=xs[:, t, :], in0=x[:, t, :], scalar=c.small[:, 6 + t:7 + t], in1=c.rowbuf[:, 0, :],
                        op0=ALU.mult, op1=ALU.mult).then_inc(normed.sem, 1)
                else:
                    nc.vector.tensor_scalar(xs[:, t, :], x[:, t, :], c.small[:, 6 + t:7 + t], None,
                                            ALU.mult).then_inc(normed.sem, 1)
            for n in range(4):
                t, q = n // 2, n % 2
                dve.wait_ge(packed.sem, p0 + n + 1)
                src = ps[:, n, :].rearrange("p (k f) -> p k f", k=4)
                dst = hT[:, 4 * q:4 * q + 4, P * t:P * t + P]
                if gain_fm is not None:
                    g = gain_fm[:, 4 * q:4 * q + 4].unsqueeze(2).to_broadcast([P, 4, P])
                    nc.vector.tensor_tensor(dst, src, g, ALU.mult).then_inc(unloaded.sem, 1)
                else:
                    nc.vector.tensor_copy(dst, src).then_inc(unloaded.sem, 1)
            for n in range(4):
                part = (slice(None), slice(4 * (n % 2), 4 * (n % 2) + 4), slice(P * (n // 2), P * (n // 2) + P))
                dve.wait_ge(high.sem, high.base + n + 1)
                nc.vector.tensor_tensor(c.act_low[part], hT[part], c.act_high[part].bitcast(F32), ALU.subtract)

        @block.tensor
        def _(pe):
            for t in range(TT):
                pe.wait_ge(normed.sem, n0 + t + 1)
                for q in range(2):
                    for k in range(4):
                        last = nc.tensor.transpose(ps[:, 2 * t + q, P * k:P * k + P],
                                                   xs[:, t, P * (4 * q + k):P * (4 * q + k) + P], c.ident)
                    last.then_inc(packed.sem, 1)
    stat_ready.advance(1)
    root_ready.advance(1)
    normed.advance(2)
    packed.advance(4)
    unloaded.advance(4)
    high.advance(4)
    gains.advance(16 * len(rows))


def ffn_stage(c, w_gate, w_up, w_down, per_expert, experts=1, mix=None, keep=1.0, add=0.5):
    nc, x, hT, ps = c.nc, c.x, c.hT, c.ps
    G = per_expert
    loaded = signals(c, "ffn_loaded0", "ffn_loaded1")
    gate_made, up_made, silu_made, weighed, hidden_made, hidden_used, summed = signals(
        c, "gate_made", "up_made", "silu_made", "weighed", "hidden_made", "hidden_used", "summed")
    steps = experts * G
    lb = [s.base for s in loaded]
    gb, pb, sb, wb, hb, hub, smb = (s.base for s in (gate_made, up_made, silu_made, weighed, hidden_made,
                                                    hidden_used, summed))
    wg = [c.slots[3 * s].rearrange("p (k f) -> p k f", k=KD) for s in range(2)]
    wu = [c.slots[3 * s + 1].rearrange("p (k f) -> p k f", k=KD) for s in range(2)]
    wd = [c.slots[3 * s + 2].rearrange("p (h n) -> p h n", h=2) for s in range(2)]
    silu = [c.work[:, T * n:T * n + T] for n in range(4)]
    mixed = [c.work[:, T * (4 + n):T * (5 + n)] for n in range(4)]
    hidden = [c.work[:, T * (8 + n):T * (9 + n)] for n in range(4)]

    def each_step(eng, body):
        if experts > 1:
            assert G % 2 == 0
            with eng.Fori(0, experts) as e:
                with eng.Fori(0, G // 2) as i:
                    for s in range(2):
                        body(s, e * (G // 2) + i, e, e * G + i * 2 + s)
        else:
            with eng.Fori(0, G // 2) as i:
                for s in range(2):
                    body(s, i, 0, i * 2 + s)
            if G % 2:
                body(0, G // 2, 0, G - 1)

    with nc.Block() as block:
        @block.sync
        @when(c)
        def _(sp):
            def load(s, pair, e, step):
                sp.wait_ge(hidden_used.sem, step * 2 + (hub - 2))
                for w, dst in ((w_gate, 3 * s), (w_up, 3 * s + 1), (w_down, 3 * s + 2)):
                    src = w[bass.ds(step, 1), :, :].rearrange("o p n -> p (o n)")
                    sp.dma_start(c.slots[dst], src).then_inc(loaded[s].sem, 16)
            each_step(sp, load)

        @block.scalar
        @when(c)
        def _(act):
            def gate(s, pair, e, step):
                for h in range(2):
                    act.wait_ge(gate_made.sem, step * 2 + (gb + h + 1))
                    act.wait_ge(hidden_made.sem, step * 2 + (hb + h - 3))
                    nc.scalar.activation(silu[2 * s + h], ps[:, 2 * h, 0:T], ACT.Silu).then_inc(silu_made.sem, 1)
            each_step(act, gate)

        @block.gpsimd
        @when(c)
        def _(pool):
            def make(s, pair, e, step):
                for h in range(2):
                    pool.wait_ge(silu_made.sem, step * 2 + (sb + h + 1))
                    pool.wait_ge(weighed.sem, step * 2 + (wb + h + 1))
                    pool.wait_ge(hidden_used.sem, step * 2 + (hub + h - 3))
                    nc.gpsimd.tensor_tensor(hidden[2 * s + h], mixed[2 * s + h], silu[2 * s + h], ALU.mult)\
                        .then_inc(hidden_made.sem, 1)
            if mix is not None:
                each_step(pool, make)

        @block.vector
        @when(c)
        def _(dve):
            def weigh(s, pair, e, step):
                for h in range(2):
                    dve.wait_ge(up_made.sem, step * 2 + (pb + h + 1))
                    dve.wait_ge(hidden_made.sem, step * 2 + (hb + h - 3))
                    m = mix[:, bass.ds(e, 1), :].rearrange("p o t -> p (o t)")
                    nc.vector.tensor_tensor(mixed[2 * s + h], ps[:, 2 * h + 1, 0:T], m, ALU.mult)\
                        .then_inc(weighed.sem, 1)

            def make(s, pair, e, step):
                for h in range(2):
                    dve.wait_ge(silu_made.sem, step * 2 + (sb + h + 1))
                    dve.wait_ge(up_made.sem, step * 2 + (pb + h + 1))
                    dve.wait_ge(hidden_used.sem, step * 2 + (hub + h - 3))
                    nc.vector.tensor_tensor(hidden[2 * s + h], silu[2 * s + h], ps[:, 2 * h + 1, 0:T], ALU.mult)\
                        .then_inc(hidden_made.sem, 1)
            each_step(dve, make if mix is None else weigh)
            dve.wait_ge(hidden_used.sem, hub + 2 * steps)
            dve.wait_ge(summed.sem, smb + 2)
            if keep != 1.0:
                for t in range(TT):
                    c.vchain(dve, nc.vector.tensor_scalar(x[:, t, :], x[:, t, :], keep, None, ALU.mult))
            for t in range(TT):
                for n in range(2):
                    xn = x[:, t, 512 * n:512 * n + 512]
                    c.vchain(dve, nc.vector.scalar_tensor_tensor(
                        out=xn, in0=ps[:, 4 + 2 * t + n, :], scalar=add, in1=xn, op0=ALU.mult, op1=ALU.add))

        @block.tensor
        @when(c)
        def _(pe):
            def down(s, h, start=False, stop=False):
                for t in range(TT):
                    for n in range(2):
                        last = nc.tensor.matmul(ps[:, 4 + 2 * t + n, :], hidden[2 * s + h][:, P * t:P * t + P],
                                                wd[s][:, h, 512 * n:512 * n + 512], start=start, stop=stop,
                                                skip_group_check=True)
                return last

            def clear(start, stop):
                for t in range(TT):
                    for n in range(2):
                        last = nc.tensor.matmul(ps[:, 4 + 2 * t + n, :], c.zeros[:, 0:P], c.zeros,
                                                start=start, stop=stop, skip_group_check=True)
                return last

            def products(s, pair, e, step):
                pe.wait_ge(loaded[s].sem, pair * 48 + (lb[s] + 48))
                for h in range(2):
                    pe.wait_ge(hidden_made.sem, step * 2 + (hb + h - 1))
                    for w, bank, made in ((wg, 2 * h, gate_made), (wu, 2 * h + 1, up_made)):
                        for k in range(KD):
                            last = nc.tensor.matmul(ps[:, bank, 0:T], w[s][:, k, P * h:P * h + P], hT[:, k, :],
                                                    start=(k == 0), stop=(k == KD - 1))
                        last.then_inc(made.sem, 1)
                for h in range(2):
                    pe.wait_ge(hidden_made.sem, step * 2 + (hb + h + 1))
                    last = down(s, h)
                    last.then_inc(hidden_used.sem, 1)
            clear(True, False).then_inc(summed.sem, 1)
            each_step(pe, products)
            clear(False, True).then_inc(summed.sem, 1)
    for s in range(2):
        n = (steps + 1 - s) // 2
        loaded[s].advance(48 * n)
    gate_made.advance(2 * steps)
    up_made.advance(2 * steps)
    silu_made.advance(2 * steps)
    if mix is not None:
        weighed.advance(2 * steps)
    hidden_made.advance(2 * steps)
    hidden_used.advance(2 * steps)
    summed.advance(2)


def split_ffn_stage(c, w_gate, w_up, w_down, keep=1.0, add=0.5, then=None):
    nc, x, ps = c.nc, c.x, c.ps
    G = w_gate.shape[0]
    assert G % 2 == 1
    loaded_ahead, c.ahead = c.ahead, then is not None
    UNITS = 3 * G
    loaded = signals(c, "unit_loaded0", "unit_loaded1", "unit_loaded2")
    high, low, low2, down_made, gate_made, up_made, silu_made, hidden_made, hidden_high, hidden_low, summed = signals(
        c, "unit_high", "unit_low_dve", "unit_low_pool", "s_down_made", "s_gate_made", "s_up_made", "s_silu_made",
        "s_hidden_made", "s_hidden_high", "s_hidden_low", "s_summed")
    lb = [s.base for s in loaded]
    hb, wb, vb, ub, gb, pb, sb, mb, ihb, ilb = (s.base for s in (high, low, low2, down_made, gate_made, up_made, silu_made,
                                                                hidden_made, hidden_high, hidden_low))
    acts = (c.act_high, c.act_low)
    silu = [c.work[:, T * h:T * h + T] for h in range(2)]
    hidden = [c.work[:, T * (2 + h):T * (3 + h)] for h in range(2)]
    HALF = KD * GW // 2

    class Step:

        def __init__(self, pair, odd):
            self.n, self.pair, self.odd = pair * 2 + odd, pair, odd

        def unit(self, j):
            at = 2 + 3 * self.odd + j
            return self.pair * 6 + at, at % 2, at % 3, self.pair * 2 + at // 3

    def stream(eng, start, body, end):
        start()
        with eng.Fori(0, G // 2) as i:
            for odd in range(2):
                body(Step(i, odd))
        end()

    after = Step(G // 2, 0)
    first = [(0, 0, 0, 0), (1, 1, 1, 0)]

    with nc.Block() as block:
        @block.sync
        def _(sp):
            def load(u, w, n):
                number, _, raw, _ = u
                sp.wait_ge(low.sem, number + (wb - 2))
                sp.wait_ge(low2.sem, number + (vb - 2))
                sp.dma_start(c.ring[:, raw, :], w[bass.ds(n, 1), :, :].rearrange("o p n -> p (o n)"))\
                    .then_inc(loaded[raw].sem, 16)

            def triple(t):
                load(t.unit(0), w_gate, t.n + 1)
                load(t.unit(1), w_down, t.n)
                load(t.unit(2), w_up, t.n + 1)

            stream(sp, lambda: None if loaded_ahead else (load(first[0], w_gate, 0), load(first[1], w_up, 0)), triple,
                   lambda: load(after.unit(0), w_down, G - 1))
            if then is not None:
                load_ahead(c, sp, then, [(low.sem, wb + UNITS), (low2.sem, vb + UNITS)])

        @block.scalar
        def _(act):
            def make_high(u, last_use=None, count=0):
                number, slot, raw, turn = u
                act.wait_ge(loaded[raw].sem, turn * 16 + (lb[raw] + 16))
                if last_use is not None:
                    act.wait_ge(last_use.sem, count + last_use.base)
                nc.scalar.activation(c.weight_high[:, slot, :], c.ring[:, raw, :], ACT.Copy).then_inc(high.sem, 1)

            def silus(n):
                for h in range(2):
                    act.wait_ge(gate_made.sem, n * 2 + (gb + h + 1))
                    act.wait_ge(hidden_made.sem, n * 2 + (mb + h - 1))
                    nc.scalar.activation(silu[h], ps[:, 2 * h, 0:T], ACT.Silu).then_inc(silu_made.sem, 1)

            def hiddens(n):
                for h in range(2):
                    act.wait_ge(hidden_made.sem, n * 2 + (mb + h + 1))
                    nc.scalar.activation(c.hidden_high[:, h, :], hidden[h], ACT.Copy).then_inc(hidden_high.sem, 1)

            def triple(t):
                make_high(t.unit(0), down_made, t.n)
                hiddens(t.n)
                make_high(t.unit(1), up_made, t.n * 2 + 2)
                silus(t.n + 1)
                make_high(t.unit(2), gate_made, t.n * 2 + 4)

            stream(act, lambda: (make_high(first[0]), make_high(first[1]), silus(0)), triple,
                   lambda: (make_high(after.unit(0), down_made, G - 1), hiddens(G - 1)))

        def low_half(eng, engine, u, half, sem):
            number, slot, raw, _ = u
            eng.wait_ge(high.sem, number + (hb + 1))
            part = slice(HALF * half, HALF * half + HALF)
            engine.tensor_tensor(c.weight_low[:, slot, part], c.ring[:, raw, part],
                                 c.weight_high[:, slot, part].bitcast(F32), ALU.subtract).then_inc(sem, 1)

        @block.gpsimd
        def _(pool):
            half = lambda u: low_half(pool, nc.gpsimd, u, 1, low2.sem)
            stream(pool, lambda: (half(first[0]), half(first[1])), lambda t: [half(t.unit(j)) for j in range(3)],
                   lambda: half(after.unit(0)))

        @block.vector
        def _(dve):
            half = lambda u: low_half(dve, nc.vector, u, 0, low.sem)

            def hiddens(n):
                for h in range(2):
                    dve.wait_ge(silu_made.sem, n * 2 + (sb + h + 1))
                    dve.wait_ge(up_made.sem, n * 2 + (pb + h + 1))
                    nc.vector.tensor_tensor(hidden[h], silu[h], ps[:, 2 * h + 1, 0:T], ALU.mult).then_inc(hidden_made.sem, 1)
                for h in range(2):
                    dve.wait_ge(hidden_high.sem, n * 2 + (ihb + h + 1))
                    nc.vector.tensor_tensor(c.hidden_low[:, h, :], hidden[h], c.hidden_high[:, h, :].bitcast(F32),
                                            ALU.subtract).then_inc(hidden_low.sem, 1)

            def triple(t):
                half(t.unit(0))
                hiddens(t.n)
                half(t.unit(1))
                half(t.unit(2))

            stream(dve, lambda: (half(first[0]), half(first[1])), triple, lambda: (half(after.unit(0)), hiddens(G - 1)))
            if keep != 1.0:
                for t in range(TT):
                    c.vchain(dve, nc.vector.tensor_scalar(x[:, t, :], x[:, t, :], keep, None, ALU.mult))
            dve.wait_ge(down_made.sem, down_made.base + G)
            dve.wait_ge(summed.sem, summed.base + 1)
            for t in range(TT):
                for n in range(2):
                    xn = x[:, t, 512 * n:512 * n + 512]
                    c.vchain(dve, nc.vector.scalar_tensor_tensor(
                        out=xn, in0=ps[:, 4 + 2 * t + n, :], scalar=add, in1=xn, op0=ALU.mult, op1=ALU.add))

        @block.tensor
        def _(pe):
            def clear(start, stop):
                for t in range(TT):
                    for n in range(2):
                        last = nc.tensor.matmul(ps[:, 4 + 2 * t + n, :], c.zeros[:, 0:P], c.zeros, start=start,
                                                stop=stop, skip_group_check=True)
                return last

            def split(u):
                number, slot, _, _ = u
                pe.wait_ge(low.sem, number + (wb + 1))
                pe.wait_ge(low2.sem, number + (vb + 1))
                return c.weight_high[:, slot, :], c.weight_low[:, slot, :]

            def across(u, n, bank, made):
                freed, count = (silu_made, sb) if bank == 0 else (hidden_made, mb)
                w = [m.rearrange("p (k f) -> p k f", k=KD) for m in split(u)]
                for h in range(2):
                    pe.wait_ge(freed.sem, n * 2 + (count + h - 1))
                    for k in range(KD):
                        last = three_passes(nc, ps[:, 2 * h + bank, 0:T], [m[:, k, P * h:P * h + P] for m in w],
                                            [m[:, k, :] for m in acts], k == 0, k == KD - 1)
                    last.then_inc(made.sem, 1)

            def down(u, n):
                w = [m.rearrange("p (h n) -> p h n", h=2) for m in split(u)]
                for h in range(2):
                    pe.wait_ge(hidden_low.sem, n * 2 + (ilb + h + 1))
                    for t in range(TT):
                        for q in range(2):
                            last = three_passes(nc, ps[:, 4 + 2 * t + q, :],
                                                [m[:, h, P * t:P * t + P] for m in (c.hidden_high, c.hidden_low)],
                                                [m[:, h, 512 * q:512 * q + 512] for m in w], False, False)
                last.then_inc(down_made.sem, 1)

            def triple(t):
                across(t.unit(0), t.n + 1, 0, gate_made)
                down(t.unit(1), t.n)
                across(t.unit(2), t.n + 1, 1, up_made)

            clear(True, False)
            stream(pe, lambda: (across(first[0], 0, 0, gate_made), across(first[1], 0, 1, up_made)), triple,
                   lambda: down(after.unit(0), G - 1))
            clear(False, True).then_inc(summed.sem, 1)
    for s in range(3):
        loaded[s].advance(16 * ((UNITS + 2 - s) // 3))
    for s in (high, low, low2):
        s.advance(UNITS)
    down_made.advance(G)
    for s in (gate_made, up_made, silu_made, hidden_made, hidden_high, hidden_low):
        s.advance(2 * G)
    summed.advance(1)


def product(c, w, groups, take, tm=False, src=None, cols=GW):
    return Product(w=w, groups=groups, take=take, tm=tm, src=c.hT if src is None else src, cols=cols,
                           kd=w.shape[2] // GW)


def three_passes(nc, out, still, moving, first, last):
    for n, (a, b) in enumerate(((0, 0), (0, 1), (1, 0))):
        ins = nc.tensor.matmul(out, still[a], moving[b], start=first and n == 0, stop=last and n == 2,
                               skip_group_check=True)
    return ins


def first_groups(weights):
    return [(n, weights[n], "weights_loaded%d" % n) for n in range(2)]


def first_units(w_gate, w_up):
    return [(n, w[0], "unit_loaded%d" % n) for n, w in enumerate((w_gate, w_up))]


def load_ahead(c, sp, sources, slots_free):
    for sem, count in slots_free:
        sp.wait_ge(sem, count)
    for slot, source, name in sources:
        loaded, = signals(c, name)
        sp.dma_start(c.ring[:, slot, 0:source.shape[1]], source).then_inc(loaded.sem, 16)


def project_stage(c, runs, unloader="scalar", then=None, aside=None):
    nc, ps = c.nc, c.ps
    loaded = signals(c, "weights_loaded0", "weights_loaded1")
    made, taken, high, low, low2, input_high, input_low = signals(
        c, "product_made", "product_taken", "weight_high_made", "weight_low_dve", "weight_low_pool", "input_high",
        "input_low")
    lb = [s.base for s in loaded]
    mb, tb, hb, wb, vb = (s.base for s in (made, taken, high, low, low2))
    total = sum(r.groups for r in runs)
    src, kd = runs[0].src, runs[0].kd
    split = src is not c.hT or not c.parts_of_hT
    c.parts_of_hT = src is c.hT
    scalar_unloads = unloader == "scalar"

    assert runs[0].groups >= 2
    loaded_ahead, c.ahead = c.ahead, then is not None

    def each_step(eng, body, skip=0):
        n = 0
        for r in runs:
            if r.groups >= 4:
                with eng.Fori(skip // 2, r.groups // 2) as i:
                    for j in range(2):
                        body(r, (n + j) % 2, i * 2 + j, i * 2 + (n + j), i + (n + j) // 2)
                rest = range(r.groups - r.groups % 2, r.groups)
            else:
                rest = range(skip, r.groups)
            skip = 0
            for g in rest:
                body(r, (n + g) % 2, g, n + g, (n + g) // 2)
            n += r.groups

    def high_part(eng, copy, after=None, between=None, only=None):
        def one(r, s, g, step, uses):
            eng.wait_ge(loaded[s].sem, uses * 16 + (lb[s] + 16))
            eng.wait_ge(made.sem, step + (mb - 1))
            copy(c.weight_high[:, s, 0:kd * GW], c.ring[:, s, 0:kd * GW]).then_inc(high.sem, 1)
            if after is not None:
                after(r, s, g, step, uses)
        if only is not None:
            for group in only:
                one(*group)
        elif between is not None:
            one(runs[0], 0, 0, 0, 0)
            between()
            one(runs[0], 1, 1, 1, 0)
            each_step(eng, one, skip=2)
        else:
            each_step(eng, one)

    def split_high(copy):
        copy(c.act_high[:, 0:kd, :], src[:, 0:kd, :]).then_inc(input_high.sem, 1)

    def split_low(dve):
        dve.wait_ge(input_high.sem, input_high.base + 1)
        nc.vector.tensor_tensor(c.act_low[:, 0:kd, :], src[:, 0:kd, :], c.act_high[:, 0:kd, :].bitcast(F32),
                                ALU.subtract).then_inc(input_low.sem, 1)

    def low_part(eng, engine, part, sem):
        def one(r, s, g, step, uses):
            eng.wait_ge(high.sem, step + (hb + 1))
            engine.tensor_tensor(c.weight_low[:, s, part], c.ring[:, s, part], c.weight_high[:, s, part].bitcast(F32),
                                 ALU.subtract).then_inc(sem.sem, 1)
        return one

    def unload_one(eng):
        def one(r, s, g, step, uses):
            eng.wait_ge(made.sem, step + (mb + 1))
            r.take(g, ps[:, 2 * s:2 * s + 2, 0:r.cols]).then_inc(taken.sem, 1)
        return one

    groups, step = [], 0
    for r in runs:
        for g in range(r.groups):
            groups.append((r, step % 2, g, step, step // 2))
            step += 1
    on_dve = kd * GW * 5 // 8
    dve_low = lambda dve: low_part(dve, nc.vector, slice(0, on_dve), low)

    with nc.Block() as block:
        @block.sync
        def _(sp):
            def load(r, s, g, step, uses):
                sp.wait_ge(low.sem, step + (wb - 1))
                sp.wait_ge(low2.sem, step + (vb - 1))
                rows = r.w[bass.ds(g, 1), :, :].rearrange("o p n -> p (o n)")
                sp.dma_start(c.ring[:, s, 0:kd * GW], rows).then_inc(loaded[s].sem, 16)
            each_step(sp, load, skip=2 if loaded_ahead else 0)
            if then is not None:
                load_ahead(c, sp, then, [(low.sem, wb + total), (low2.sem, vb + total)])

        @block.tensor
        def _(pe):
            def multiply(r, s, g, step, uses):
                pe.wait_ge(low.sem, step + (wb + 1))
                pe.wait_ge(low2.sem, step + (vb + 1))
                pe.wait_ge(taken.sem, step + (tb - 1))
                w = [m[:, s, 0:kd * GW].rearrange("p (k f) -> p k f", f=GW) for m in (c.weight_high, c.weight_low)]
                acts = (c.act_high, c.act_low)
                for a in range(2):
                    part = slice(P * a, P * a + P)
                    for k in range(kd):
                        if r.tm:
                            still, moving = [m[:, k, part] for m in acts], [m[:, k, 0:r.cols] for m in w]
                        else:
                            still, moving = [m[:, k, part] for m in w], [m[:, k, :] for m in acts]
                        last = three_passes(nc, ps[:, 2 * s + a, 0:r.cols], still, moving, k == 0, k == kd - 1)
                last.then_inc(made.sem, 1)
            if split:
                pe.wait_ge(input_low.sem, input_low.base + 1)
            each_step(pe, multiply)

        @block.scalar
        def _(act):
            high_of = lambda o, i: nc.scalar.activation(o, i, ACT.Copy)
            if aside is not None:
                high_part(act, high_of, only=groups[0:2])
                for n, group in enumerate(groups):
                    unload_one(act)(*group)
                    high_part(act, high_of, only=groups[n + 2:n + 3])
                    if n + 3 == total:
                        aside.scalar(act)
            elif scalar_unloads:
                if split:
                    split_high(high_of)
                each_step(act, unload_one(act))
            else:
                high_part(act, high_of)

        @block.vector
        def _(dve):
            if aside is not None:
                aside.vector(dve)
            elif scalar_unloads:
                high_part(dve, nc.vector.tensor_copy, dve_low(dve), (lambda: split_low(dve)) if split else None)
            else:
                if split:
                    split_high(nc.vector.tensor_copy)
                    split_low(dve)
                make_low, take = dve_low(dve), unload_one(dve)
                for group in groups[0:2]:
                    make_low(*group)
                for n, group in enumerate(groups):
                    take(*group)
                    for ahead in groups[n + 2:n + 3]:
                        make_low(*ahead)

        @block.gpsimd
        def _(pool):
            if aside is not None:
                for group in groups:
                    low_part(pool, nc.gpsimd, slice(0, on_dve), low)(*group)
                    low_part(pool, nc.gpsimd, slice(on_dve, kd * GW), low2)(*group)
            else:
                each_step(pool, low_part(pool, nc.gpsimd, slice(on_dve, kd * GW), low2))
    for s in range(2):
        loaded[s].advance(16 * ((total + 1 - s) // 2))
    for s in (made, taken, high, low, low2):
        s.advance(total)
    if split:
        input_high.advance(1)
        input_low.advance(1)


def to_fm(c, dst, func=ACT.Copy):
    return lambda g, r: c.nc.scalar.activation(dst[:, bass.ds(g * 2, 2), :], r, func)


def to_tm(c, dst, func=ACT.Copy, cols=GW):
    return lambda g, r: c.nc.scalar.activation(dst[:, :, bass.ds(g * GW, cols)], r, func)


def add_to_x(c, keep=1.0):
    def take(g, r):
        xg = c.x[:, :, bass.ds(g * GW, GW)]
        return c.nc.vector.scalar_tensor_tensor(out=xg, in0=xg, scalar=keep, in1=r, op0=ALU.mult, op1=ALU.add)
    return take


def rope_stage(c, chunks, rotation, cos, sin):
    nc, ps = c.nc, c.ps
    turned, scaled, roped = signals(c, "rope_turned", "rope_scaled", "roped")
    tb, sb, rb = turned.base, scaled.base, roped.base
    n = chunks.shape[1] // 2
    prod = [c.work[:, 512 * k:512 * k + 512].rearrange("p (a t) -> p a t", a=2) for k in range(4)]

    with nc.Block() as block:
        @block.tensor
        def _(pe):
            for k in range(n):
                if k >= 4:
                    pe.wait_ge(roped.sem, rb + k - 3)
                nc.tensor.matmul(ps[:, k % 4, :], rotation, chunks[:, 2 * k:2 * k + 2, :].rearrange("p a t -> p (a t)"),
                                 start=True, stop=True).then_inc(turned.sem, 1)

        @block.gpsimd
        def _(pool):
            for k in range(n):
                if k >= 2:
                    pool.wait_ge(roped.sem, rb + k - 1)
                nc.gpsimd.tensor_tensor(prod[k % 2], chunks[:, 2 * k:2 * k + 2, :],
                                        cos.unsqueeze(1).to_broadcast([P, 2, T]), ALU.mult).then_inc(scaled.sem, 1)

        @block.vector
        def _(dve):
            for k in range(n):
                dve.wait_ge(turned.sem, tb + k + 1)
                c.vchain(dve, nc.vector.tensor_tensor(prod[2 + k % 2], ps[:, k % 4, :].rearrange("p (a t) -> p a t", a=2),
                                                      sin.unsqueeze(1).to_broadcast([P, 2, T]), ALU.mult))
                dve.wait_ge(scaled.sem, sb + k + 1)
                nc.vector.tensor_tensor(chunks[:, 2 * k:2 * k + 2, :], prod[k % 2], prod[2 + k % 2],
                                        ALU.add).then_inc(roped.sem, 1)
    for s in (turned, scaled, roped):
        s.advance(n)


def attention_stage(c, groups, scale):
    nc, ps = c.nc, c.ps
    scored, biased, exped, factored, weighted, turned, turned_taken, attended, output = signals(
        c, "scored", "biased", "exped", "factored", "weighted", "probs_turned", "turned_taken", "attended",
        "output_taken")
    zb, bb, eb, fb, wb, tb, kb, ab, ob = (s.base for s in (scored, biased, exped, factored, weighted, turned,
                                                           turned_taken, attended, output))
    passes = []
    for gi, (members, _) in enumerate(groups):
        slab = 0
        for m in members:
            passes.append((m, gi, slab, m is members[-1]))
            slab += len(m.v)
    N = len(passes)
    S = [c.work[:, 1024 * b:1024 * b + 1024].rearrange("p (a k) -> p a k", a=4) for b in range(2)]
    turned_sb = [c.ring[:, 2 * b:2 * b + 2, :].rearrange("p s n -> p (s n)")[:, 0:5 * 512]
                 .rearrange("p (l a q) -> p l a q", l=5, a=4) for b in range(2)]
    st = lambda b, n: c.small[:, 32 * b + 4 * n:32 * b + 4 * n + 4]

    with nc.Block() as block:
        @block.tensor
        def _(pe):
            def score(n):
                m, b = passes[n][0], n % 2
                if n >= 2:
                    pe.wait_ge(biased.sem, bb + n - 1)
                for p in range(2):
                    for j in range(2):
                        last = nc.tensor.matmul(ps[:, 2 * b + p, T * j:T * j + m.nk], m.q(p, j), m.k(p),
                                                start=True, stop=True)
                last.then_inc(scored.sem, 1)

            def turn(n):
                m, b = passes[n][0], n % 2
                pe.wait_ge(weighted.sem, wb + n + 1)
                if n:
                    pe.wait_ge(turned_taken.sem, kb + n)
                for l in range(len(m.v)):
                    w = min(P, m.nk - P * l)
                    for a in range(4):
                        last = nc.tensor.transpose(ps[0:w, 4 + l, P * a:P * a + P], S[b][:, a, P * l:P * l + w], c.ident)
                last.then_inc(turned.sem, 1)

            def attend(gi):
                members, _ = groups[gi]
                pe.wait_ge(turned_taken.sem, kb + sum(len(groups[g][0]) for g in range(gi + 1)))
                if gi >= 2:
                    pe.wait_ge(output.sem, ob + gi - 1)
                for p in range(2):
                    for j in range(2):
                        parts = [(m, l) for m in members for l in range(len(m.v))]
                        for n, (m, l) in enumerate(parts):
                            w = min(P, m.nk - P * l)
                            last = nc.tensor.matmul(ps[HD * p:HD * p + HD, 6 + gi % 2, P * j:P * j + P], m.v[l],
                                                    turned_sb[gi % 2][0:w, n, 2 * p + j, :],
                                                    start=(n == 0), stop=(n == len(parts) - 1))
                last.then_inc(attended.sem, 1)

            score(0)
            if N > 1:
                score(1)
            for n in range(N):
                turn(n)
                if n + 2 < N:
                    score(n + 2)
                if passes[n][3]:
                    attend(passes[n][1])

        @block.vector
        def _(dve):
            link = lambda ins: c.vchain(dve, ins)

            def bias(n):
                m, b = passes[n][0], n % 2
                dve.wait_ge(scored.sem, zb + n + 1)
                if n >= 2:
                    dve.wait_ge(turned.sem, tb + n - 1)
                src = ps[:, 2 * b:2 * b + 2, :].rearrange("p h (j k) -> p (h j) k", j=2)[:, :, 0:m.nk]
                link(nc.vector.tensor_tensor(S[b][:, :, 0:m.nk], src, m.mask.unsqueeze(1).to_broadcast([P, 4, m.nk]),
                                             ALU.add))
                link(nc.vector.tensor_reduce(st(b, 0), S[b][:, :, 0:m.nk], axis=AX.X, op=ALU.max))
                if m.sinks is None:
                    nc.vector.tensor_scalar(st(b, 1), st(b, 0), -scale, None, ALU.mult).then_inc(biased.sem, 1)
                else:
                    link(nc.vector.scalar_tensor_tensor(out=st(b, 0), in0=st(b, 0), scalar=scale, in1=m.sinks,
                                                        op0=ALU.mult, op1=ALU.max))
                    link(nc.vector.tensor_scalar(st(b, 1), st(b, 0), -1.0, None, ALU.mult))
                    nc.vector.tensor_tensor(st(b, 2), m.sinks, st(b, 0), ALU.subtract).then_inc(biased.sem, 1)

            def factor(n):
                m, b = passes[n][0], n % 2
                dve.wait_ge(exped.sem, eb + n + 1)
                if m.sinks is not None:
                    link(nc.vector.tensor_tensor(st(b, 4), st(b, 4), st(b, 3), ALU.add))
                ins = nc.vector.reciprocal(st(b, 5), st(b, 4))
                if m.gates is not None:
                    link(ins)
                    ins = nc.vector.tensor_tensor(st(b, 5).rearrange("p (h j) -> p h j", h=2),
                                                  st(b, 5).rearrange("p (h j) -> p h j", h=2), m.gates, ALU.mult)
                if m.valid is not None:
                    link(ins)
                    ins = nc.vector.tensor_scalar(st(b, 5), st(b, 5), m.valid, None, ALU.mult)
                ins.then_inc(factored.sem, 1)

            bias(0)
            for n in range(N):
                if n + 1 < N:
                    bias(n + 1)
                factor(n)

        @block.scalar
        def _(act):
            def exps(n):
                m, b = passes[n][0], n % 2
                act.wait_ge(biased.sem, bb + n + 1)
                if m.sinks is not None:
                    nc.scalar.activation(st(b, 3), st(b, 2), ACT.Exp)
                for a in range(4):
                    last = nc.scalar.activation(S[b][:, a, 0:m.nk], S[b][:, a, 0:m.nk], ACT.Exp, bias=st(b, 1)[:, a:a + 1],
                                                scale=scale, accum_out=st(b, 4)[:, a:a + 1])
                last.then_inc(exped.sem, 1)

            def take_turned(n):
                m, gi, slab, _ = passes[n]
                act.wait_ge(turned.sem, tb + n + 1)
                if gi >= 2:
                    act.wait_ge(attended.sem, ab + gi - 1)
                for l in range(len(m.v)):
                    w = min(P, m.nk - P * l)
                    last = nc.scalar.activation(turned_sb[gi % 2][0:w, slab + l, :, :].rearrange("p a q -> p (a q)"),
                                                ps[0:w, 4 + l, :], ACT.Copy)
                last.then_inc(turned_taken.sem, 1)

            def take_output(gi):
                act.wait_ge(attended.sem, ab + gi + 1)
                nc.scalar.activation(groups[gi][1], ps[:, 6 + gi % 2, 0:T].rearrange("p (j q) -> p j q", j=2),
                                     ACT.Copy).then_inc(output.sem, 1)

            exps(0)
            for n in range(N):
                if n + 1 < N:
                    exps(n + 1)
                take_turned(n)
                if passes[n][3]:
                    take_output(passes[n][1])

        @block.gpsimd
        def _(pool):
            for n in range(N):
                m, b = passes[n][0], n % 2
                pool.wait_ge(factored.sem, fb + n + 1)
                nc.gpsimd.tensor_tensor(S[b][:, :, 0:m.nk], S[b][:, :, 0:m.nk],
                                        st(b, 5).unsqueeze(2).to_broadcast([P, 4, m.nk]), ALU.mult)\
                    .then_inc(weighted.sem, 1)
    for s in (scored, biased, exped, factored, weighted, turned, turned_taken):
        s.advance(N)
    attended.advance(len(groups))
    output.advance(len(groups))


CMP_LEN, CMP_STRIDE = 32, 16
NCMP = (T - CMP_LEN) // CMP_STRIDE + 1


def load_stage(c, loads):
    nc = c.nc
    first, = signals(c, "tables_loaded")
    with nc.Block() as block:
        @block.sync
        def _(sp):
            for dst, src in loads:
                sp.dma_start(dst, src).then_inc(first.sem, 16)
            sp.wait_ge(first.sem, first.base + 16 * len(loads))
    first.advance(16 * len(loads))


def gmlp_stage(c, u, v, out, wT, bias, causal):
    nc, ps = c.nc, c.ps
    H = 8
    var_made, root_made, normed, mixed = signals(c, "gm_var_made", "gm_root_made", "gm_normed", "gm_mixed")
    vh = v.rearrange("p t (h d) -> p t h d", h=H)
    sq = c.work[:, 0:TT * H * HD].rearrange("p (t n) -> p t n", t=TT)
    sqh = sq.rearrange("p t (h d) -> p t h d", h=H)
    st = lambda n: c.small[:, 16 * n:16 * n + 16]
    with nc.Block() as block:
        @block.vector
        def _(dve):
            link = lambda ins: c.vchain(dve, ins)
            link(nc.vector.tensor_tensor(wT, wT, causal.unsqueeze(1).to_broadcast([P, H, P]), ALU.mult))
            link(nc.vector.tensor_reduce(st(0).rearrange("p (t h) -> p t h", t=TT), vh, axis=AX.X, op=ALU.add))
            link(nc.vector.tensor_scalar(st(0), st(0), 1.0 / HD, None, ALU.mult))
            for t in range(TT):
                link(nc.vector.tensor_tensor(vh[:, t], vh[:, t], st(0)[:, H * t:H * t + H].unsqueeze(2)
                                             .to_broadcast([P, H, HD]), ALU.subtract))
            link(nc.vector.tensor_tensor(sq, v, v, ALU.mult))
            link(nc.vector.tensor_reduce(st(1), sq.rearrange("p t (h d) -> p (t h) d", h=H), axis=AX.X, op=ALU.add))
            nc.vector.tensor_scalar(st(1), st(1), 1.0 / HD, LN_EPS, ALU.mult, ALU.add).then_inc(var_made.sem, 1)
            dve.wait_ge(root_made.sem, root_made.base + 1)
            link(nc.vector.reciprocal(st(3), st(2)))
            for t in range(TT):
                nc.vector.tensor_tensor(vh[:, t], vh[:, t], st(3)[:, H * t:H * t + H].unsqueeze(2)
                                        .to_broadcast([P, H, HD]), ALU.mult).then_inc(normed.sem, 1)
            for b in range(2):
                dve.wait_ge(mixed.sem, mixed.base + b + 1)
                spread = sq.rearrange("p t n -> p (t n)")[:, 512 * b:512 * b + 512].rearrange("p (j t) -> p j t", j=2)
                link(nc.vector.tensor_tensor(spread, ps[:, b, :].rearrange("p (j t) -> p j t", j=2),
                                             bias[:, 2 * b:2 * b + 2, :], ALU.add))
                link(nc.vector.tensor_tensor(out[:, 2 * b:2 * b + 2, :], spread, u[:, 2 * b:2 * b + 2, :], ALU.mult))

        @block.scalar
        def _(act):
            act.wait_ge(var_made.sem, var_made.base + 1)
            nc.scalar.activation(st(2), st(1), ACT.Sqrt).then_inc(root_made.sem, 1)

        @block.tensor
        def _(pe):
            pe.wait_ge(normed.sem, normed.base + TT)
            for b in range(2):
                for h in range(4 * b, 4 * b + 4):
                    for t in range(TT):
                        at = T * (h // 2 % 2) + P * t
                        last = nc.tensor.matmul(ps[HD * (h % 2):HD * (h % 2) + HD, b, at:at + P],
                                                v[:, t, HD * h:HD * h + HD], wT[:, h, :], start=True, stop=True)
                last.then_inc(mixed.sem, 1)
    var_made.advance(1)
    root_made.advance(1)
    normed.advance(TT)
    mixed.advance(2)


def compress_stage(c, kv, w1, w2, pe_cols, cos, sin, kT, vT):
    nc, ps = c.nc, c.ps
    hid_made, pe_made, pe_taken, gelued, second, ready, flipped = signals(
        c, "cmp_hidden", "cmp_pe_made", "cmp_pe_taken", "cmp_gelued", "cmp_second", "cmp_rotated", "cmp_flipped")
    h1 = c.work[0:HD, 0:4 * 16].rearrange("p (a n) -> p a n", a=4)
    peb = c.work[0:HD, 64:66]
    kc = c.work[0:NCMP, 128:256].rearrange("p (g h d) -> p g h d", g=2, h=2)
    rot = c.work[0:NCMP, 256:512].rearrange("p (g u h d) -> p g u h d", g=2, u=2, h=2)
    tmp = c.work[0:NCMP, 512:640].rearrange("p (n g d) -> p n g d", n=2, g=2)
    with nc.Block() as block:
        @block.tensor
        def _(pe):
            for m in range(2):
                for l in range(CMP_LEN):
                    last = nc.tensor.matmul(ps[0:HD, 4 + m, 0:1], w1[0:HD, m, l, :], pe_cols[0:HD, m, l:l + 1],
                                            start=(l == 0), stop=(l == CMP_LEN - 1))
            last.then_inc(pe_made.sem, 1)
            for m in range(2):
                for g in range(2):
                    at = slice(HD * g, HD * g + HD)
                    for l in range(CMP_LEN):
                        last = nc.tensor.matmul(ps[0:HD, 2 * m + g, 0:NCMP], w1[at, m, l, :],
                                                kv[at, m, l:l + CMP_STRIDE * (NCMP - 1) + 1:CMP_STRIDE],
                                                start=(l == 0), stop=(l == CMP_LEN - 1))
            last.then_inc(hid_made.sem, 1)
            pe.wait_ge(gelued.sem, gelued.base + 1)
            for m in range(2):
                for g in range(2):
                    last = nc.tensor.matmul(ps[0:NCMP, 6 + m, HD * g:HD * g + HD], h1[:, 2 * m + g, 0:NCMP],
                                            w2[0:HD, m, :], start=True, stop=True)
            last.then_inc(second.sem, 1)
            pe.wait_ge(ready.sem, ready.base + 1)
            for g in range(2):
                last = nc.tensor.transpose(ps[:, 4, 16 * g:16 * g + NCMP], rot[:, g].rearrange("p u h d -> p (u h d)"),
                                           c.ident[0:NCMP, 0:NCMP])
            last.then_inc(flipped.sem, 1)

        @block.scalar
        def _(act):
            act.wait_ge(pe_taken.sem, pe_taken.base + 1)
            act.wait_ge(hid_made.sem, hid_made.base + 1)
            for m in range(2):
                last = nc.scalar.activation(h1[:, 2 * m:2 * m + 2, 0:NCMP], ps[0:HD, 2 * m:2 * m + 2, 0:NCMP],
                                            ACT.Gelu_apprx_tanh, bias=peb[:, m:m + 1])
            last.then_inc(gelued.sem, 1)

        @block.vector
        def _(dve):
            link = lambda ins: c.vchain(dve, ins)
            dve.wait_ge(pe_made.sem, pe_made.base + 1)
            nc.vector.tensor_copy(peb, ps[0:HD, 4:6, 0:1].rearrange("p a o -> p (a o)")).then_inc(pe_taken.sem, 1)
            dve.wait_ge(second.sem, second.base + 1)
            link(nc.vector.tensor_copy(vT, ps[0:NCMP, 7, 0:128].rearrange("p (g d) -> p g d", g=2)))
            link(nc.vector.tensor_copy(kc, ps[0:NCMP, 6, 0:128].rearrange("p (g h d) -> p g h d", g=2, h=2)))
            cb = cos[0:NCMP].unsqueeze(1).to_broadcast([NCMP, 2, 32])
            sb = sin[0:NCMP].unsqueeze(1).to_broadcast([NCMP, 2, 32])
            for half, op in ((0, ALU.subtract), (1, ALU.add)):
                link(nc.vector.tensor_tensor(tmp[:, 0], kc[:, :, half, :], cb, ALU.mult))
                link(nc.vector.tensor_tensor(tmp[:, 1], kc[:, :, 1 - half, :], sb, ALU.mult))
                link(nc.vector.tensor_tensor(rot[:, :, 0, half, :], tmp[:, 0], tmp[:, 1], op))
            nc.vector.tensor_copy(rot[:, :, 1], rot[:, :, 0]).then_inc(ready.sem, 1)
            dve.wait_ge(flipped.sem, flipped.base + 1)
            link(nc.vector.tensor_copy(kT[:, :, 0:NCMP], ps[:, 4, 0:32].rearrange("p (g n) -> p g n", g=2)[:, :, 0:NCMP]))
    for s in (hid_made, pe_made, pe_taken, gelued, second, ready, flipped):
        s.advance(1)


def even_mixer(c):
    d = c.dram
    norm_stage(c, gain_fm=c.gains[:, KD:2 * KD])
    seg = c.seg
    vtm = c.vtm
    t = c.tables
    wT = t[:, 0:1024].rearrange("p (h t) -> p h t", h=8)
    bias = t[:, 1024:2048].rearrange("p (a t) -> p a t", a=4)
    causal = t[:, 2048:2176]
    w2 = t[:, 2176:2304].rearrange("p (m o) -> p m o", m=2)
    pe_cols = t[:, 2304:2368].rearrange("p (m l) -> p m l", m=2)
    rot64 = t[:, 2368:2496]
    cos, sin = t[:, 2496:2752], t[:, 2752:3008]
    ccos, csin = t[:, 3008:3040], t[:, 3040:3072]
    amask = t[:, 3072:3584].rearrange("p (t k) -> p t k", t=2)
    cmask = t[:, 3584:3616].rearrange("p (t k) -> p t k", t=2)
    valid = t[:, 3616:3618]
    kT = t[:, 3618:3650].rearrange("p (g n) -> p g n", g=2)
    vT = t[0:NCMP, 3650:3778].rearrange("p (g d) -> p g d", g=2)
    w1 = c.ring[:, 0:2, :].rearrange("p m (l o) -> p m l o", l=CMP_LEN)
    load_stage(c, [(t[:, 0:3618], d["l_even_tables"])])
    wi = d["l_ev_in"]
    project_stage(c, [
        product(c, wi[0:2], 2, to_fm(c, seg[:, 0:4], ACT.Gelu_apprx_tanh)),
        product(c, wi[7:9], 2, to_tm(c, vtm, ACT.Gelu_apprx_tanh), tm=True),
        product(c, wi[2:7], 5, to_fm(c, seg[:, 4:14])),
        product(c, wi[9:10], 1, to_tm(c, vtm[:, :, 512:768]), tm=True),
        product(c, wi[10:11], 1, to_tm(c, vtm[:, :, 768:792], ACT.Sigmoid, cols=24), tm=True, cols=24)])
    load_stage(c, [(c.ring[:, 0:2, :].rearrange("p m n -> p (m n)"), d["l_cmp_w1"])])
    gmlp_stage(c, seg[:, 0:4], vtm[:, :, 0:512], c.cat[:, 0:4], wT, bias, causal)
    compress_stage(c, seg[:, 12:14], w1, w2, pe_cols, ccos, csin, kT, vT)
    rope_stage(c, seg[:, 4:12], rot64, cos, sin)
    groups = []
    for g in range(2):
        for qt in range(TT):
            def q(p, j, g=g, qt=qt):
                return seg[HD * p:HD * p + HD, 4 + 2 * g + j, P * qt:P * qt + P]
            gates = vtm[:, qt, 768 + 12 * g:780 + 12 * g].rearrange("p (j h c) -> p c h j", j=2, h=2)
            nk = P * (qt + 1)
            members = [Pass(
                q=q, k=lambda p, g=g: kT[HD * p:HD * p + HD, g, 0:NCMP], nk=NCMP, v=[vT[:, g, :]],
                mask=cmask[:, qt, 0:NCMP], sinks=None, gates=gates[:, 0], valid=valid[:, qt:qt + 1])]
            for b in range(2):
                members.append(Pass(
                    q=q, k=lambda p, g=g, b=b, nk=nk: seg[HD * p:HD * p + HD, 8 + 2 * b + g, 0:nk], nk=nk,
                    v=[vtm[:, l, 512 + P * b + HD * g:512 + P * b + HD * g + HD] for l in range(qt + 1)],
                    mask=amask[:, qt, 0:nk], sinks=None, gates=gates[:, 1 + b], valid=None))
            groups.append((members, c.cat[:, 4 + 2 * g:6 + 2 * g, P * qt:P * qt + P]))
    attention_stage(c, groups, HD ** -0.5)
    project_stage(c, [product(c, d["l_ev_out"], 4, add_to_x(c), tm=True, src=c.cat)], "vector",
                  then=first_units(*(d[n][d[n].shape[0] // 4:] for n in ("l_ffn_gate", "l_ffn_up"))))


POOL_WINDOWS = (2, 4, 8, 16)
NT = 16
CH = 32


def pool_stage(c, z, operators, weights, scale, out):
    nc, ps = c.nc, c.ps
    pooled, taken, mixed = signals(c, "pooled", "pooled_taken", "pool_mixed")
    buf = c.work[:, 0:4 * T].rearrange("p (g t) -> p g t", g=4)
    with nc.Block() as block:
        @block.tensor
        def _(pe):
            for g in range(4):
                for t in range(TT):
                    last = nc.tensor.matmul(ps[:, g, 0:T], z[:, t, P * g:P * g + P], operators[:, g, t, :],
                                            start=(t == 0), stop=(t == TT - 1))
                last.then_inc(pooled.sem, 1)
            for g in range(4):
                pe.wait_ge(taken.sem, taken.base + g + 1)
                nc.tensor.matmul(ps[:, 4 + g, 0:T], weights[:, g, :], buf[:, g, :], start=True,
                                 stop=True).then_inc(mixed.sem, 1)

        @block.scalar
        def _(act):
            for g in range(4):
                act.wait_ge(pooled.sem, pooled.base + g + 1)
                nc.scalar.activation(buf[:, g, :], ps[:, g, 0:T], ACT.Copy).then_inc(taken.sem, 1)

        @block.vector
        def _(dve):
            for g in range(4):
                dve.wait_ge(mixed.sem, mixed.base + g + 1)
                c.vchain(dve, nc.vector.tensor_scalar(out[:, g, :], ps[:, 4 + g, 0:T], scale[:, g:g + 1], None, ALU.mult))
    for s in (pooled, taken, mixed):
        s.advance(4)


class Aside:

    def __init__(self, scalar, vector):
        self.scalar, self.vector = scalar, vector


def s5_tables(c, lam_re, lam_im, log_dt, c_re, c_im, decay, phases, readout):
    nc = c.nc
    V = nc.vector
    reduced, sines = signals(c, "s5_angle_reduced", "s5_sines")
    reduced_count, sines_count = reduced.base + 1, sines.base + 1
    st = lambda n: c.rowbuf[:, 0, NT * n:NT * n + NT]
    dt, a, theta, k, half, sh, sn, m, cs, cm1, nr, ni, inv, cr, ci, t1, t2 = (st(n) for n in range(17))
    two_pi = 2 * np.pi
    parts = [6.28125, 0.0019340515136718750]
    parts.append(float(np.float32(two_pi - sum(parts))))
    ln2 = [0.693359375, float(np.float32(np.log(2.0) - 0.693359375))]
    big = 1.5 * 2.0 ** 23
    pi = 3.1415925

    def scalar(act):
        act.wait_ge(reduced.sem, reduced_count)
        nc.scalar.activation(sh, half, ACT.Sin)
        nc.scalar.activation(sn, theta, ACT.Sin).then_inc(sines.sem, 1)

    def vector(dve):
        link = lambda ins: c.vchain(dve, ins)
        mul = lambda o, x, y: link(V.tensor_tensor(o, x, y, ALU.mult))
        add = lambda o, x, y: link(V.tensor_tensor(o, x, y, ALU.add))
        sub = lambda o, x, y: link(V.tensor_tensor(o, x, y, ALU.subtract))
        fma = lambda o, x, s, y: link(V.scalar_tensor_tensor(out=o, in0=x, scalar=s, in1=y, op0=ALU.mult, op1=ALU.add))

        def round_to(o, x, s):
            link(V.tensor_scalar(o, x, float(s), None, ALU.mult))
            link(V.tensor_scalar(o, o, big, None, ALU.add))
            link(V.tensor_scalar(o, o, -big, None, ALU.add))

        round_to(k, log_dt, 1 / np.log(2.0))
        link(V.tensor_scalar(a, log_dt, 1.0, None, ALU.mult))
        for part in ln2:
            fma(a, k, -part, a)
        link(V.memset(dt, 1.0))
        for n in range(9, 0, -1):
            mul(dt, dt, a)
            link(V.tensor_scalar(dt, dt, 1.0 / n, 1.0, ALU.mult, ALU.add))
        link(V.tensor_scalar(k, k, -127.0, 128.0, ALU.max, ALU.min))
        link(V.tensor_scalar(t1.bitcast(mybir.dt.int32), k, 127.0, 2.0 ** 23, ALU.add, ALU.mult))
        mul(dt, dt, t1)
        mul(theta, lam_im, dt)
        round_to(k, theta, 1 / two_pi)
        for part in parts:
            fma(theta, k, -part, theta)
        link(V.tensor_scalar(theta, theta, -pi, pi, ALU.max, ALU.min))
        V.tensor_scalar(half, theta, 0.5, None, ALU.mult).then_inc(reduced.sem, 1)
        mul(a, lam_re, dt)
        link(V.tensor_scalar(a, a, -104.0, 104.0, ALU.max, ALU.min))
        link(V.tensor_scalar(a, a, 1.0 / 128, None, ALU.mult))
        link(V.memset(m, 1.0))
        for n in range(9, 1, -1):
            mul(m, m, a)
            link(V.tensor_scalar(m, m, 1.0 / n, 1.0, ALU.mult, ALU.add))
        mul(m, m, a)
        for _ in range(7):
            link(V.scalar_tensor_tensor(out=m, in0=m, scalar=2.0, in1=m, op0=ALU.add, op1=ALU.mult))
        link(V.tensor_scalar(decay, m, 1.0, None, ALU.add))
        dve.wait_ge(sines.sem, sines_count)
        mul(cm1, sh, sh)
        link(V.tensor_scalar(cm1, cm1, -2.0, None, ALU.mult))
        link(V.tensor_scalar(cs, cm1, 1.0, None, ALU.add))
        mul(nr, decay, cm1)
        add(nr, nr, m)
        mul(ni, decay, sn)
        mul(t1, lam_re, lam_re)
        mul(inv, lam_im, lam_im)
        add(inv, inv, t1)
        link(V.reciprocal(inv, inv))
        mul(cr, nr, lam_re)
        mul(t1, ni, lam_im)
        add(cr, cr, t1)
        mul(cr, cr, inv)
        mul(ci, ni, lam_re)
        mul(t1, nr, lam_im)
        sub(ci, ci, t1)
        mul(ci, ci, inv)
        out = [readout[:, n, :].rearrange("p (n c) -> p n c", n=NT) for n in range(3)]
        wide = lambda s: s.unsqueeze(2).to_broadcast([P, NT, CH])
        mul(out[0], c_re, wide(cr))
        mul(out[1], c_im, wide(ci))
        sub(out[0], out[0], out[1])
        mul(out[1], c_im, wide(cr))
        mul(out[2], c_re, wide(ci))
        link(V.scalar_tensor_tensor(out=readout[:, 2, :], in0=readout[:, 1, :], scalar=-1.0, in1=readout[:, 2, :],
                                    op0=ALU.mult, op1=ALU.subtract))
        link(V.tensor_scalar(readout[:, 1, :], readout[:, 0, :], -1.0, None, ALU.mult))
        mul(t1, cs, cs)
        mul(t2, sn, sn)
        add(t1, t1, t2)
        link(V.tensor_scalar(t1, t1, -0.5, 1.5, ALU.mult, ALU.add))
        mul(cs, cs, t1)
        mul(sn, sn, t1)
        pr, pi_ = phases
        link(V.memset(pr[:, :, 0:1], 1.0))
        link(V.memset(pi_[:, :, 0:1], 0.0))
        n = 1
        while n < T:
            wide = lambda s: s.unsqueeze(2).to_broadcast([P, NT, n])
            tmp = c.work[:, 0:NT * n].rearrange("p (a k) -> p a k", a=NT)
            new = slice(n, 2 * n)
            mul(pr[:, :, new], pr[:, :, 0:n], wide(cs))
            mul(tmp, pi_[:, :, 0:n], wide(sn))
            sub(pr[:, :, new], pr[:, :, new], tmp)
            mul(pi_[:, :, new], pi_[:, :, 0:n], wide(cs))
            mul(tmp, pr[:, :, 0:n], wide(sn))
            add(pi_[:, :, new], pi_[:, :, new], tmp)
            n *= 2
            mul(t1, cs, sn)
            mul(t2, sn, sn)
            mul(cs, cs, cs)
            sub(cs, cs, t2)
            link(V.tensor_scalar(sn, t1, 2.0, None, ALU.mult))
    for s in (reduced, sines):
        s.advance(1)
    return Aside(scalar, vector)


def s5_stage(c, u, b_in, decay, phases, readout, skip, y):
    nc, ps = c.nc, c.ps
    driven, rotated, scanned, unrotated, read, skipped = signals(
        c, "s5_driven", "s5_rotated", "s5_scanned", "s5_unrotated", "s5_read", "s5_skipped")
    two = lambda s: s.rearrange("p (r t) -> p r t", r=2)
    cosw = [two(c.work[:, 512 * b:512 * b + 512]) for b in range(2)]
    sinw = [two(c.work[:, 1024 + 512 * b:1536 + 512 * b]) for b in range(2)]
    w = [two(c.work[:, 2048 + 512 * b:2560 + 512 * b]) for b in range(2)]
    turned = [c.rowbuf[:, b, :].rearrange("p (e r t) -> p e r t", e=2, r=2) for b in range(2)]
    wide = lambda s, n: phases[s][:, n, :].unsqueeze(1).to_broadcast([P, 2, T])
    with nc.Block() as block:
        @block.tensor
        def _(pe):
            def drive(n):
                if n >= 2:
                    pe.wait_ge(rotated.sem, rotated.base + n - 1)
                at = slice(CH * (n % 4), CH * (n % 4) + CH)
                for r in range(2):
                    last = nc.tensor.matmul(ps[:, n % 2, T * r:T * r + T], b_in[at, r, n // 4, :], u[at, n // 4, :],
                                            start=True, stop=True)
                last.then_inc(driven.sem, 1)

            def readout_of(n):
                pe.wait_ge(unrotated.sem, unrotated.base + n + 1)
                cols = slice(CH * n, CH * n + CH)
                e = turned[n % 2]
                for k, (m, v) in enumerate(((0, e[:, 0, 0]), (1, e[:, 1, 1]), (2, e[:, 0, 1]), (2, e[:, 1, 0]))):
                    last = nc.tensor.matmul(ps[CH * (n % 4):CH * (n % 4) + CH, 4 + n // 4, 0:T], readout[:, m, cols], v,
                                            start=(k == 0), stop=(k == 3))
                last.then_inc(read.sem, 1)

            drive(0)
            drive(1)
            for n in range(NT):
                if n + 2 < NT:
                    drive(n + 2)
                readout_of(n)

        @block.vector
        def _(dve):
            link = lambda ins: c.vchain(dve, ins)
            for n in range(NT):
                b = n % 2
                dve.wait_ge(driven.sem, driven.base + n + 1)
                bu = two(ps[:, b, :])
                nc.vector.tensor_tensor(cosw[b], bu, wide(0, n), ALU.mult)
                ins = nc.vector.tensor_tensor(sinw[b], bu, wide(1, n), ALU.mult)
                ins.then_inc(rotated.sem, 1)
                dve.wait_ge(rotated.sem, rotated.base + n + 1)
                nc.vector.tensor_tensor(cosw[b][:, 0], cosw[b][:, 0], sinw[b][:, 1], ALU.add)
                link(nc.vector.tensor_tensor(cosw[b][:, 1], cosw[b][:, 1], sinw[b][:, 0], ALU.subtract))
                if n >= 2:
                    dve.wait_ge(unrotated.sem, unrotated.base + n - 1)
                rate = decay[:, n:n + 1].to_broadcast([P, T])
                for r in range(2):
                    last = nc.vector.tensor_tensor_scan(w[b][:, r], rate, cosw[b][:, r], 0.0, ALU.mult, ALU.add)
                last.then_inc(scanned.sem, 1)
            for m in range(4):
                dve.wait_ge(read.sem, read.base + 4 * m + 4)
                nc.vector.scalar_tensor_tensor(out=y[:, m, :], in0=u[:, m, :], scalar=skip[:, m:m + 1], in1=ps[:, 4 + m, 0:T],
                                               op0=ALU.mult, op1=ALU.add).then_inc(skipped.sem, 1)

        @block.gpsimd
        def _(pool):
            for n in range(NT):
                b = n % 2
                pool.wait_ge(scanned.sem, scanned.base + n + 1)
                if n >= 2:
                    pool.wait_ge(read.sem, read.base + n - 1)
                for e in range(2):
                    last = nc.gpsimd.tensor_tensor(turned[b][:, e], w[b], wide(e, n), ALU.mult)
                last.then_inc(unrotated.sem, 1)

        @block.scalar
        def _(act):
            act.wait_ge(skipped.sem, skipped.base + 4)
            c.achain(act, nc.scalar.activation(y, y, ACT.Gelu_apprx_tanh))
    for s in (driven, rotated, scanned, unrotated, read):
        s.advance(NT)
    skipped.advance(4)


def multiply_stage(c, out, a, b):
    with c.nc.Block() as block:
        @block.vector
        def _(dve):
            c.vchain(dve, c.nc.vector.tensor_tensor(out, a, b, ALU.mult))


def odd_mixer(c):
    d, seg, t = c.dram, c.seg, c.tables
    norm_stage(c, gain_fm=c.gains[:, 4 * KD:5 * KD])
    operators = t[:, 0:2048].rearrange("p (g t s) -> p g t s", g=4, t=TT)
    weights = t[:, 2048:2560].rearrange("p (g d) -> p g d", g=4)
    scale, skip = t[:, 2560:2564], t[:, 2564:2568]
    lam_re, lam_im, log_dt = (t[:, 2568 + NT * n:2568 + NT * n + NT] for n in range(3))
    b_in = t[:, 2616:3640].rearrange("p (r m s) -> p r m s", r=2, m=4)
    c_re, c_im = (t[:, 3640 + 512 * n:4152 + 512 * n].rearrange("p (n c) -> p n c", n=NT) for n in range(2))
    decay = t[:, 4664:4664 + NT]
    phases = [m.rearrange("p a b -> p (a b)").rearrange("p (n t) -> p n t", n=NT) for m in (c.ring[:, 2:4], seg[:, 8:24])]
    readout = seg[:, 24:30].rearrange("p a b -> p (a b)").rearrange("p (m n) -> p m n", m=3)
    load_stage(c, [(t[:, 0:4664], d["l_odd_tables"])])
    zc, u, y, ab = c.vtm[:, :, 0:512], seg[:, 0:4], seg[:, 4:8], seg[:, 8:16]
    wi = d["l_od_in"]
    tables = s5_tables(c, lam_re, lam_im, log_dt, c_re, c_im, decay, phases, readout)
    project_stage(c, [product(c, wi[0:2], 2, to_tm(c, zc), tm=True), product(c, wi[2:4], 2, to_fm(c, u))], aside=tables,
                  then=first_groups(d["l_glu"]))
    pool_stage(c, zc, operators, weights, scale, c.cat[:, 0:4])
    s5_stage(c, u, b_in, decay, phases, readout, skip, y)
    wg = d["l_glu"]
    project_stage(c, [product(c, wg[0:2], 2, to_fm(c, ab[:, 0:4]), src=y),
                      product(c, wg[2:4], 2, to_fm(c, ab[:, 4:8], ACT.Sigmoid), src=y)],
                  then=first_groups(d["l_od_out"]))
    multiply_stage(c, c.cat[:, 4:8], ab[:, 0:4], ab[:, 4:8])
    project_stage(c, [product(c, d["l_od_out"], 4, add_to_x(c), tm=True, src=c.cat)], "vector",
                  then=first_units(*(d[n][d[n].shape[0] // 4 * 3:] for n in ("l_ffn_gate", "l_ffn_up"))))


RET_HEADS = 4


def retention_stage(c, q, k, v, decay, gate, out):
    nc, ps = c.nc, c.ps
    scored, decayed, summed, kept, square_made, square_summed, rooted, scaled, gated = signals(
        c, "ret_scored", "ret_decayed", "ret_summed", "ret_kept", "ret_squared", "ret_square_summed", "ret_rooted",
        "ret_scaled", "ret_gated")
    A = [c.work[:, 512 * h:512 * h + 512].rearrange("p (s t) -> p s t", s=TT) for h in range(RET_HEADS)]
    sq = [c.work[:, 2048 + 512 * b:2560 + 512 * b].rearrange("p (j t) -> p j t", j=2) for b in range(2)]
    root = [c.work[:, 3072 + T * b:3072 + T * b + T] for b in range(2)]
    two = lambda s: s.rearrange("p (j t) -> p j t", j=2)
    with nc.Block() as block:
        @block.tensor
        def _(pe):
            def score(h):
                if h >= 2:
                    pe.wait_ge(decayed.sem, decayed.base + h - 1)
                for s in range(TT):
                    last = nc.tensor.matmul(ps[:, h % 2, T * s:T * s + T], k[:, h, P * s:P * s + P], q[:, h, :],
                                            start=True, stop=True)
                last.then_inc(scored.sem, 1)

            def combine(h):
                pe.wait_ge(decayed.sem, decayed.base + h + 1)
                if h >= 2:
                    pe.wait_ge(square_made.sem, square_made.base + h - 1)
                for j in range(2):
                    for s in range(TT):
                        at = 2 * P * h + P * j
                        last = nc.tensor.matmul(ps[:, 2 + h % 2, T * j:T * j + T], v[:, s, at:at + P], A[h][:, s, :],
                                                start=(s == 0), stop=(s == TT - 1))
                last.then_inc(summed.sem, 1)

            def square_sum(h):
                pe.wait_ge(square_made.sem, square_made.base + h + 1)
                if h >= 2:
                    pe.wait_ge(rooted.sem, rooted.base + h - 1)
                for j in range(2):
                    last = nc.tensor.matmul(ps[:, 4 + h % 2, 0:T], c.ones, sq[h % 2][:, j, :], start=(j == 0), stop=(j == 1))
                last.then_inc(square_summed.sem, 1)

            score(0)
            for h in range(RET_HEADS):
                if h + 1 < RET_HEADS:
                    score(h + 1)
                combine(h)
                if h:
                    square_sum(h - 1)
            square_sum(RET_HEADS - 1)

        @block.scalar
        def _(act):
            def root_of(h):
                act.wait_ge(square_summed.sem, square_summed.base + h + 1)
                if h >= 2:
                    act.wait_ge(scaled.sem, scaled.base + h - 1)
                nc.scalar.activation(root[h % 2], ps[:, 4 + h % 2, 0:T], ACT.Sqrt, scale=1.0 / 256,
                                     bias=c.eps[:, 0:1]).then_inc(rooted.sem, 1)

            for h in range(RET_HEADS):
                act.wait_ge(summed.sem, summed.base + h + 1)
                nc.scalar.activation(out[:, 2 * h:2 * h + 2, :], two(ps[:, 2 + h % 2, :]), ACT.Copy).then_inc(kept.sem, 1)
                if h >= 2:
                    act.wait_ge(square_summed.sem, square_summed.base + h - 1)
                nc.scalar.activation(sq[h % 2], two(ps[:, 2 + h % 2, :]), ACT.Square).then_inc(square_made.sem, 1)
                if h:
                    root_of(h - 1)
            root_of(RET_HEADS - 1)

        @block.vector
        def _(dve):
            for h in range(RET_HEADS):
                dve.wait_ge(scored.sem, scored.base + h + 1)
                nc.vector.tensor_tensor(A[h], two(ps[:, h % 2, :]), decay[:, h], ALU.mult).then_inc(decayed.sem, 1)
            for h in range(RET_HEADS):
                dve.wait_ge(rooted.sem, rooted.base + h + 1)
                c.vchain(dve, nc.vector.reciprocal(root[h % 2], root[h % 2]))
                dve.wait_ge(kept.sem, kept.base + h + 1)
                o = out[:, 2 * h:2 * h + 2, :]
                nc.vector.tensor_tensor(o, o, root[h % 2].unsqueeze(1).to_broadcast([P, 2, T]), ALU.mult)\
                    .then_inc(scaled.sem, 1)

        @block.gpsimd
        def _(pool):
            for h in range(RET_HEADS):
                pool.wait_ge(scaled.sem, scaled.base + h + 1)
                o = out[:, 2 * h:2 * h + 2, :]
                nc.gpsimd.tensor_tensor(o, o, gate[:, 2 * h:2 * h + 2, :], ALU.mult).then_inc(gated.sem, 1)
    for s in (scored, decayed, summed, kept, square_made, square_summed, rooted, scaled, gated):
        s.advance(RET_HEADS)


HG = 8
L = 32
NB = T // L


def hgrn_stage(c, q, z, v, gate, bound, rest, first_layer, norm_gain, out):
    nc, ps = c.nc, c.ps
    names = ("hg_sigmoid", "hg_bounded", "hg_logged", "hg_summed", "hg_exped", "hg_queries", "hg_keys",
             "hg_scored", "hg_turned_taken", "hg_masked", "hg_driven", "hg_drive_taken", "hg_stated", "hg_made",
             "hg_kept", "hg_square_summed", "hg_sums_taken")
    (sigmoid, bounded, logged, bsummed, exped, queries, keys, scored, turned_taken, masked, driven, drive_taken, stated,
     made, kept, square_summed, sums_taken) = signals(c, *names)
    rooted, scaled = signals(c, "hg_rooted", "hg_scaled")
    R = [c.ring[:, n, :].rearrange("p (h t) -> p h t", h=HG) for n in range(4)]
    K, E1, E2, M = R
    lo = -43.0
    st = [c.work[:, 1024 * b:1024 * b + 1024].rearrange("p (n v) -> p n v", n=NB) for b in range(2)]
    mk = [c.work[:, 2048 + T * b:2048 + T * b + T].rearrange("p (t s) -> p t s", t=TT) for b in range(2)]
    kt = [c.work[:, 2560 + T * b:2560 + T * b + T].rearrange("p (t s) -> p t s", t=TT) for b in range(2)]
    sq = [c.work[:, 3072 + T * b:3072 + T * b + T] for b in range(2)]
    drive = [c.rowbuf[:, b, :].rearrange("p (n v) -> p n v", n=NB) for b in range(2)]
    sums = K
    blocks = lambda s: s.rearrange("p (n l) -> p n l", n=NB)
    with nc.Block() as block:
        @block.scalar
        def _(act):
            for h in range(HG):
                nc.scalar.activation(K[:, h, :], z[:, h, :], ACT.Sigmoid, scale=-1.0)
                if first_layer:
                    nc.scalar.activation(E1[:, h, :], z[:, h, :], ACT.Sigmoid).then_inc(sigmoid.sem, 1)
                else:
                    nc.scalar.activation(z[:, h, :], z[:, h, :], ACT.Sigmoid).then_inc(sigmoid.sem, 1)
            for h in range(HG):
                act.wait_ge(bounded.sem, bounded.base + h + 1)
                nc.scalar.activation(E1[:, h, :] if first_layer else z[:, h, :], E1[:, h, :] if first_layer else z[:, h, :],
                                     ACT.Ln).then_inc(logged.sem, 1)
            for h in range(HG):
                act.wait_ge(bsummed.sem, bsummed.base + h + 1)
                nc.scalar.activation(E1[:, h, :], M[:, h, :], ACT.Exp)
                nc.scalar.activation(E2[:, h, :], M[:, h, :], ACT.Exp, scale=-1.0)
                nc.scalar.activation(out[:, h, :], out[:, h, :], ACT.Exp)
                nc.scalar.activation(z[:, h, :], z[:, h, :], ACT.Exp).then_inc(exped.sem, 1)

            def take_turned(h):
                act.wait_ge(scored.sem, scored.base + h + 1)
                if h >= 2:
                    act.wait_ge(driven.sem, driven.base + h - 1)
                nc.scalar.activation(kt[h % 2].rearrange("p t s -> p (t s)"), ps[:, 5, 0:T], ACT.Copy)\
                    .then_inc(turned_taken.sem, 1)

            def take_drive(h):
                act.wait_ge(driven.sem, driven.base + h + 1)
                if h >= 2:
                    act.wait_ge(stated.sem, stated.base + h - 1)
                nc.scalar.activation(drive[h % 2].rearrange("p (t n) v -> p n t v", t=TT),
                                     ps[:, 0:4, 0:T].rearrange("p n (t v) -> p n t v", t=TT), ACT.Copy)\
                    .then_inc(drive_taken.sem, 1)

            def take_output(h):
                act.wait_ge(made.sem, made.base + h + 1)
                if h >= 2:
                    act.wait_ge(square_summed.sem, square_summed.base + h - 1)
                nc.scalar.activation(out[:, h, :], ps[:, 6, 0:T], ACT.Copy)
                nc.scalar.activation(sq[h % 2], ps[:, 6, 0:T], ACT.Square).then_inc(kept.sem, 1)

            take_turned(0)
            for h in range(HG):
                take_drive(h)
                if h + 1 < HG:
                    take_turned(h + 1)
                if h:
                    take_output(h - 1)
            take_output(HG - 1)
            act.wait_ge(sums_taken.sem, sums_taken.base + HG)
            nc.scalar.activation(sums, sums, ACT.Sqrt, scale=1.0 / P, bias=c.eps[:, 0:1]).then_inc(rooted.sem, 1)

        @block.vector
        def _(dve):
            link = lambda ins: c.vchain(dve, ins)
            for h in range(HG):
                dve.wait_ge(sigmoid.sem, sigmoid.base + h + 1)
                if first_layer:
                    link(nc.vector.tensor_scalar(z[:, h, :], z[:, h, :], -lo, 0.0, ALU.add, ALU.min))
                    nc.vector.tensor_scalar(E1[:, h, :], E1[:, h, :], float(np.exp(lo)), None, ALU.max).then_inc(bounded.sem, 1)
                else:
                    nc.vector.tensor_scalar(K[:, h, :], K[:, h, :], rest[:, h:h + 1], None, ALU.mult)
                    nc.vector.tensor_scalar(z[:, h, :], z[:, h, :], rest[:, h:h + 1], bound[:, h:h + 1], ALU.mult,
                                            ALU.add).then_inc(bounded.sem, 1)
            for h in range(HG):
                dve.wait_ge(logged.sem, logged.base + h + 1)
                if first_layer:
                    link(nc.vector.tensor_tensor(z[:, h, :], z[:, h, :], E1[:, h, :], ALU.add))
                link(nc.vector.tensor_tensor_scan(z[:, h, :], c.block_reset, z[:, h, :], 0.0, ALU.mult, ALU.add))
                B = blocks(z[:, h, :])
                nc.vector.tensor_tensor(blocks(M[:, h, :]), B, B[:, :, L // 2 - 1:L // 2].to_broadcast([P, NB, L]), ALU.subtract)
                nc.vector.tensor_tensor(blocks(out[:, h, :]), B[:, :, L - 1:L].to_broadcast([P, NB, L]), B, ALU.subtract)\
                    .then_inc(bsummed.sem, 1)
            for h in range(HG):
                dve.wait_ge(exped.sem, exped.base + h + 1)
                nc.vector.tensor_tensor(E1[:, h, :], E1[:, h, :], q[:, h, :], ALU.mult)
                nc.vector.tensor_tensor(q[:, h, :], q[:, h, :], z[:, h, :], ALU.mult).then_inc(queries.sem, 1)

            def mask(h):
                dve.wait_ge(scored.sem, scored.base + h + 1)
                if h >= 2:
                    dve.wait_ge(made.sem, made.base + h - 1)
                nc.vector.tensor_tensor(mk[h % 2], ps[:, 4, 0:T].rearrange("p (t s) -> p t s", t=TT),
                                        c.block_causal.unsqueeze(1).to_broadcast([P, TT, P]), ALU.mult).then_inc(masked.sem, 1)

            def states(h):
                dve.wait_ge(drive_taken.sem, drive_taken.base + h + 1)
                if h >= 2:
                    dve.wait_ge(made.sem, made.base + h - 1)
                ins = nc.vector.tensor_copy(st[h % 2][:, 0, :], drive[h % 2][:, 0, :])
                for n in range(1, NB - 1):
                    link(ins)
                    ins = nc.vector.scalar_tensor_tensor(
                        out=st[h % 2][:, n, :], in0=st[h % 2][:, n - 1, :], scalar=z[:, h, L * n + L - 1:L * n + L],
                        in1=drive[h % 2][:, n, :], op0=ALU.mult, op1=ALU.add)
                ins.then_inc(stated.sem, 1)

            def take_sums(h):
                dve.wait_ge(square_summed.sem, square_summed.base + h + 1)
                nc.vector.tensor_copy(sums[:, h, :], ps[:, 7, 0:T]).then_inc(sums_taken.sem, 1)

            mask(0)
            for h in range(HG):
                states(h)
                if h + 1 < HG:
                    mask(h + 1)
                if h >= 2:
                    take_sums(h - 2)
            take_sums(HG - 2)
            take_sums(HG - 1)
            dve.wait_ge(rooted.sem, rooted.base + 1)
            link(nc.vector.reciprocal(sums, sums))
            for h in range(HG):
                nc.vector.scalar_tensor_tensor(out=out[:, h, :], in0=out[:, h, :], scalar=norm_gain, in1=sums[:, h, :],
                                               op0=ALU.mult, op1=ALU.mult).then_inc(scaled.sem, 1)

        @block.gpsimd
        def _(pool):
            for h in range(HG):
                pool.wait_ge(exped.sem, exped.base + h + 1)
                nc.gpsimd.tensor_tensor(E2[:, h, :], E2[:, h, :], K[:, h, :], ALU.mult)
                nc.gpsimd.tensor_tensor(out[:, h, :], out[:, h, :], K[:, h, :], ALU.mult).then_inc(keys.sem, 1)
            for h in range(HG):
                pool.wait_ge(scaled.sem, scaled.base + h + 1)
                nc.gpsimd.tensor_tensor(out[:, h, :], out[:, h, :], gate[:, h, :], ALU.mult)

        @block.tensor
        def _(pe):
            def score(h):
                pe.wait_ge(queries.sem, queries.base + h + 1)
                pe.wait_ge(keys.sem, keys.base + h + 1)
                if h:
                    pe.wait_ge(turned_taken.sem, turned_taken.base + h)
                    pe.wait_ge(masked.sem, masked.base + h)
                for t in range(TT):
                    at = slice(P * t, P * t + P)
                    nc.tensor.matmul(ps[:, 4, at], E2[:, h, at], E1[:, h, at], start=True, stop=True)
                    last = nc.tensor.transpose(ps[:, 5, at], out[:, h, at], c.ident)
                last.then_inc(scored.sem, 1)

            def drives(h):
                pe.wait_ge(turned_taken.sem, turned_taken.base + h + 1)
                if h:
                    pe.wait_ge(drive_taken.sem, drive_taken.base + h)
                for t in range(TT):
                    for n in range(4):
                        rows = slice(L * n, L * n + L)
                        last = nc.tensor.matmul(ps[:, n, P * t:P * t + P], kt[h % 2][rows, t, :],
                                                v[rows, t, P * h:P * h + P], start=True, stop=True)
                last.then_inc(driven.sem, 1)

            def output(h):
                pe.wait_ge(masked.sem, masked.base + h + 1)
                pe.wait_ge(stated.sem, stated.base + h + 1)
                if h:
                    pe.wait_ge(kept.sem, kept.base + h)
                for t in range(TT):
                    nc.tensor.matmul(ps[:, 6, P * t:P * t + P], v[:, t, P * h:P * h + P], mk[h % 2][:, t, :],
                                     start=(t == 0), stop=False, skip_group_check=True)
                for n in range(1, NB):
                    last = nc.tensor.matmul(ps[:, 6, L * n:L * n + L], st[h % 2][:, n - 1, :], q[:, h, L * n:L * n + L],
                                            start=False, stop=(n == NB - 1), skip_group_check=True)
                last.then_inc(made.sem, 1)

            def square_sum(h):
                pe.wait_ge(kept.sem, kept.base + h + 1)
                if h:
                    pe.wait_ge(sums_taken.sem, sums_taken.base + h)
                nc.tensor.matmul(ps[:, 7, 0:T], c.ones, sq[h % 2], start=True, stop=True).then_inc(square_summed.sem, 1)

            score(0)
            for h in range(HG):
                drives(h)
                if h + 1 < HG:
                    score(h + 1)
                if h:
                    output(h - 1)
                if h >= 2:
                    square_sum(h - 2)
            output(HG - 1)
            square_sum(HG - 2)
            square_sum(HG - 1)
    for s in signals(c, *names):
        s.advance(HG)
    rooted.advance(1)
    scaled.advance(HG)


ALPHA = (2.0 * 2) ** 0.25
EXPERTS = 8


def bounds_stage(c, raw, bound, rest):
    nc = c.nc
    diff_made, = signals(c, "bound_diff_made")
    with nc.Block() as block:
        @block.vector
        def _(dve):
            nc.vector.tensor_tensor(bound, raw[:, HG:2 * HG], raw[:, 0:HG], ALU.subtract).then_inc(diff_made.sem, 1)

        @block.scalar
        def _(act):
            act.wait_ge(diff_made.sem, diff_made.base + 1)
            nc.scalar.activation(rest, bound, ACT.Sigmoid, scale=-1.0).then_inc(c.achain.sem, 1)
            c.achain.n += 1
            act.wait_ge(c.achain.sem, c.achain.n)
            c.achain(act, nc.scalar.activation(bound, bound, ACT.Sigmoid))
    diff_made.advance(1)


def weigh_add_stage(c, total, part):
    with c.nc.Block() as block:
        @block.vector
        def _(dve):
            c.vchain(dve, c.nc.vector.tensor_tensor(total, total, part, ALU.add))


def gated_fm(c, dst, gate):
    return lambda g, r: c.nc.vector.tensor_tensor(dst[:, bass.ds(g * 2, 2), :], r, gate[:, bass.ds(g * 2, 2), :], ALU.mult)


def route_stage(c, router, lower, earlier, r):
    nc, ps = c.nc, c.ps
    E = EXPERTS
    logits_made, diff_made, exp_made, chosen_made, placed = signals(
        c, "logits_made", "logit_diff_made", "logit_exp_made", "chosen_made", "placed")
    w = c.work
    lg = w[:, 0:2 * E].rearrange("p (t e) -> p t e", t=TT)
    gt = w[:, 64:64 + 2 * E * E].rearrange("p (t e f) -> p t e f", t=TT, e=E)
    eq = w[:, 256:256 + 2 * E * E].rearrange("p (t e f) -> p t e f", t=TT, e=E)
    rank, one, two_, tmp = (w[:, 400 + 16 * n:416 + 16 * n].rearrange("p (t e) -> p t e", t=TT) for n in range(4))
    s = lambda n: w[:, 500 + 2 * n:502 + 2 * n]
    with nc.Block() as block:
        @block.tensor
        def _(pe):
            for t in range(TT):
                for k in range(KD):
                    last = nc.tensor.matmul(ps[:, t, 0:E], c.hT[:, k, P * t:P * t + P], router[:, k, :], start=(k == 0),
                                            stop=(k == KD - 1))
            last.then_inc(logits_made.sem, 1)
            pe.wait_ge(chosen_made.sem, chosen_made.base + 1)
            nc.tensor.matmul(ps[:, 2, 0:E], earlier, r.chosen[:, 0], start=True, stop=True)
            nc.tensor.matmul(ps[:, 2, E:2 * E], earlier, r.chosen[:, 1], start=True, stop=False)
            nc.tensor.matmul(ps[:, 2, E:2 * E], c.ones, r.chosen[:, 0], start=False, stop=True)
            for t in range(TT):
                last = nc.tensor.matmul(ps[:, 2, 2 * E:3 * E], c.ones, r.chosen[:, t], start=(t == 0), stop=(t == TT - 1))
            last.then_inc(placed.sem, 1)

        @block.vector
        def _(dve):
            link = lambda ins: c.vchain(dve, ins)
            V = nc.vector
            dve.wait_ge(logits_made.sem, logits_made.base + 1)
            link(V.tensor_copy(lg, ps[:, 0:TT, 0:E]))
            for t in range(TT):
                other = lg[:, t].unsqueeze(1).to_broadcast([P, E, E])
                own = lg[:, t].unsqueeze(2).to_broadcast([P, E, E])
                link(V.tensor_tensor(gt[:, t], other, own, ALU.is_gt))
                link(V.tensor_tensor(eq[:, t], other, own, ALU.is_equal))
                link(V.tensor_tensor(eq[:, t], eq[:, t], lower, ALU.mult))
                link(V.tensor_tensor(gt[:, t], gt[:, t], eq[:, t], ALU.add))
            link(V.tensor_reduce(rank, gt, axis=AX.X, op=ALU.add))
            link(V.tensor_scalar(one, rank, 0.0, None, ALU.is_equal))
            link(V.tensor_scalar(two_, rank, 1.0, None, ALU.is_equal))
            V.tensor_tensor(r.chosen, one, two_, ALU.add).then_inc(chosen_made.sem, 1)
            link(V.tensor_tensor(tmp, one, two_, ALU.subtract))
            link(V.tensor_tensor(tmp, tmp, lg, ALU.mult))
            link(V.tensor_reduce(s(0), tmp, axis=AX.X, op=ALU.add))
            V.tensor_scalar(s(1), s(0), -1.0, None, ALU.mult).then_inc(diff_made.sem, 1)
            dve.wait_ge(exp_made.sem, exp_made.base + 1)
            link(V.tensor_scalar(s(3), s(2), 1.0, None, ALU.add))
            link(V.reciprocal(s(4), s(3)))
            link(V.tensor_tensor(s(5), s(2), s(4), ALU.mult))
            for t in range(TT):
                link(V.tensor_scalar(tmp[:, t], two_[:, t], s(5)[:, t:t + 1], None, ALU.mult))
                link(V.scalar_tensor_tensor(out=r.weight[:, t], in0=one[:, t], scalar=s(4)[:, t:t + 1], in1=tmp[:, t],
                                            op0=ALU.mult, op1=ALU.add))
            dve.wait_ge(placed.sem, placed.base + 1)
            link(V.tensor_copy(r.place, ps[:, 2, 0:2 * E].rearrange("p (t e) -> p t e", t=TT)))
            link(V.tensor_reduce(s(0)[:, 0:1], ps[:, 2, 2 * E:3 * E], axis=AX.X, op=ALU.max))
            link(V.tensor_copy(r.most, s(0)[0:1, 0:1]))

        @block.scalar
        def _(act):
            act.wait_ge(diff_made.sem, diff_made.base + 1)
            nc.scalar.activation(s(2), s(1), ACT.Exp).then_inc(exp_made.sem, 1)
    for sig in (logits_made, diff_made, exp_made, chosen_made, placed):
        sig.advance(1)


def spread_stage(c, weight, mix):
    nc, ps = c.nc, c.ps
    spread, = signals(c, "mix_spread")
    with nc.Block() as block:
        @block.tensor
        @when(c)
        def _(pe):
            for e in range(EXPERTS):
                for t in range(TT):
                    at = T * (e % 2) + P * t
                    last = nc.tensor.matmul(ps[:, 4 + e // 2, at:at + P], weight[:, t, e:e + 1].to_broadcast([P, P]),
                                            c.ident, start=True, stop=True)
                if e % 2:
                    last.then_inc(spread.sem, 1)

        @block.vector
        @when(c)
        def _(dve):
            for b in range(4):
                dve.wait_ge(spread.sem, spread.base + b + 1)
                c.vchain(dve, nc.vector.tensor_copy(mix[:, 2 * b:2 * b + 2, :],
                                                    ps[:, 4 + b, :].rearrange("p (e t) -> p e t", e=2)))
    spread.advance(4)


SLOTS = 128


def gather_stage(c, r, iota, taken_from, given_to, picks, weighed, units):
    nc, ps, E = c.nc, c.ps, EXPERTS
    picked, weighed_made, turned, turned_taken, gathered, taken = signals(
        c, "moe_picked", "moe_weighed", "moe_turned", "moe_turned_taken", "moe_gathered", "moe_taken")
    with nc.Block() as block:
        @block.sync
        @when(c)
        def _(sp):
            for n, unit in enumerate(units):
                loaded, = signals(c, "moe_loaded%d" % n)
                sp.dma_start(c.slots[n], unit).then_inc(loaded.sem, 16)

        @block.vector
        @when(c)
        def _(dve):
            for scale, dst, made in ((r.chosen, picks, picked), (r.weight, weighed, weighed_made)):
                for e in range(E):
                    for t in range(TT):
                        last = nc.vector.tensor_scalar(dst[:, t, e, :], iota, r.place[:, t, e:e + 1], scale[:, t, e:e + 1],
                                                       ALU.is_equal, ALU.mult)
                    last.then_inc(made.sem, 1)

        @block.tensor
        @when(c)
        def _(pe):
            n = 0
            for half in range(2):
                pe.wait_ge(picked.sem, picked.base + 4 * half + 4)
                for k in range(KD):
                    if n >= 4:
                        pe.wait_ge(taken.sem, taken.base + n - 3)
                    for t in range(TT):
                        last = nc.tensor.matmul(ps[:, n % 4, :], c.x[:, t, P * k:P * k + P],
                                                picks[:, t, 4 * half:4 * half + 4, :].rearrange("p e s -> p (e s)"),
                                                start=(t == 0), stop=(t == TT - 1))
                    last.then_inc(gathered.sem, 1)
                    n += 1
            for b in range(4):
                pe.wait_ge(weighed_made.sem, weighed_made.base + 2 * b + 2)
                for e in range(2):
                    for t in range(TT):
                        at = T * e + P * t
                        last = nc.tensor.transpose(ps[:, 4 + b, at:at + P], weighed[:, t, 2 * b + e, :], c.ident)
                last.then_inc(turned.sem, 1)

        @block.scalar
        @when(c)
        def _(act):
            for n in range(2 * KD):
                act.wait_ge(gathered.sem, gathered.base + n + 1)
                half, k = n // KD, n % KD
                nc.scalar.activation(taken_from[:, 4 * half:4 * half + 4, k, :],
                                     ps[:, n % 4, :].rearrange("p (e s) -> p e s", e=4), ACT.Copy).then_inc(taken.sem, 1)
            for b in range(4):
                act.wait_ge(turned.sem, turned.base + b + 1)
                nc.scalar.activation(given_to[:, 2 * b:2 * b + 2, :], ps[:, 4 + b, :].rearrange("p (e t) -> p e t", e=2),
                                     ACT.Copy).then_inc(turned_taken.sem, 1)


def experts_stage(c, w_gate, w_up, w_down, G, inputs, outputs):
    nc, ps, E = c.nc, c.ps, EXPERTS
    assert G % 2 == 0
    PAIRS, STEPS = G // 2, E * G
    HALF = KD * GW // 2
    ON_DVE = 704
    loaded = signals(c, *("moe_loaded%d" % n for n in range(6)))
    (high, low, low2, used, silu_made, hidden_made, turned, hidden_high, hidden_low, inputs_high, inputs_low,
     output_taken) = signals(c, "moe_unit_high", "moe_unit_low_dve", "moe_unit_low_pool", "moe_parts_used", "moe_silu_made",
                             "moe_hidden_made", "moe_hidden_turned", "moe_hidden_high", "moe_hidden_low",
                             "moe_inputs_high", "moe_inputs_low", "moe_output_taken")
    lb = [s.base for s in loaded]
    hb, wb, vb, ub, sb, mb, tb = (s.base for s in (high, low, low2, used, silu_made, hidden_made, turned))
    flat = lambda m: m.rearrange("p s n -> p (s n)")
    weight_high, weight_low = flat(c.weight_high), flat(c.weight_low)
    flat_hidden = lambda m: flat(m)[:, 0:2 * SLOTS]
    high_hidden, low_hidden = flat_hidden(c.hidden_high), flat_hidden(c.hidden_low)
    silu, hidden = c.work[:, 0:GW], c.work[:, GW:2 * GW]
    gate_bank, up_bank = lambda parity: ps[:, parity % 2, 0:GW], lambda parity: ps[:, 2 + parity % 2, 0:GW]
    parts_of = lambda e: [m[:, :, SLOTS * (e % 2):SLOTS * (e % 2) + SLOTS] for m in (c.act_high, c.act_low)]

    class Unit:

        def __init__(self, pair, at):
            self.number, self.raw, self.turn = pair * 6 + at, at % 6, pair + at // 6
            self.halves = [slice(HALF * q, HALF * q + HALF) for q in ((2 * at) % 4, (2 * at + 1) % 4)]

        def half_number(self, h):
            return self.number * 2 + h

    class Step:

        def __init__(self, pair, odd):
            self.pair, self.odd, self.n = pair, odd, pair * 2 + odd

        def unit(self, j):
            return Unit(self.pair, 2 + 3 * self.odd + j)

    g0, u0 = Unit(0, 0), Unit(0, 1)
    up_used = lambda n: ub + 2 * (3 * n + 1)
    expert_done = lambda e: ub + 2 * min(3 * (G * e + G - 1) + 5, 3 * STEPS)

    def stream(eng, begin, triple, last, late=None):
        for e in range(E):
            begin(e)
            with eng.Fori(0, PAIRS - 1) as i:
                for odd in range(2):
                    triple(Step(i + e * PAIRS, odd), e, e)
            if late is not None:
                late(e)
            triple(Step(e * PAIRS + PAIRS - 1, 0), e, e)
            if e + 1 < E:
                triple(Step(e * PAIRS + PAIRS - 1, 1), e, e + 1)
        last(Step(E * PAIRS - 1, 1))

    with nc.Block() as block:
        @block.sync
        @when(c)
        def _(sp):
            def load(u, w, n):
                sp.wait_ge(low.sem, u.number * 2 + (wb - 10))
                sp.wait_ge(low2.sem, u.number * 2 + (vb - 10))
                sp.dma_start(c.slots[u.raw], w[bass.ds(n, 1), :, :].rearrange("o p n -> p (o n)"))\
                    .then_inc(loaded[u.raw].sem, 16)

            def triple(t):
                load(t.unit(0), w_gate, t.n + 1)
                load(t.unit(1), w_up, t.n + 1)
                load(t.unit(2), w_down, t.n)

            triple(Step(0, 1))
            with sp.Fori(1, STEPS // 2 - 1) as i:
                for odd in range(2):
                    triple(Step(i, odd))
            triple(Step(STEPS // 2 - 1, 0))
            load(Unit(STEPS // 2 - 1, 5), w_down, STEPS - 1)

        @block.scalar
        @when(c)
        def _(act):
            def make_high(u):
                act.wait_ge(loaded[u.raw].sem, u.turn * 16 + (lb[u.raw] + 16))
                for h in range(2):
                    act.wait_ge(used.sem, u.half_number(h) + (ub - 3))
                    nc.scalar.activation(weight_high[:, u.halves[h]], c.slots[u.raw][:, HALF * h:HALF * h + HALF],
                                         ACT.Copy).then_inc(high.sem, 1)

            def make_silu(g, parity):
                act.wait_ge(used.sem, g.half_number(1) + (ub + 1))
                nc.scalar.activation(silu, gate_bank(parity), ACT.Silu).then_inc(silu_made.sem, 1)

            def make_hidden_high(n, parity):
                act.wait_ge(turned.sem, n + (tb + 1))
                nc.scalar.activation(high_hidden, gate_bank(parity), ACT.Copy).then_inc(hidden_high.sem, 1)

            def inputs_of(e):
                nc.scalar.activation(parts_of(e)[0], inputs[:, e], ACT.Copy).then_inc(inputs_high.sem, 1)

            def begin(e):
                if e == 0:
                    inputs_of(0)
                    make_high(g0)
                    make_high(u0)
                    make_silu(g0, 0)
                if e + 1 < E:
                    if e > 0:
                        act.wait_ge(used.sem, up_used(G * e - 1))
                    inputs_of(e + 1)

            def triple(t, e, e_next):
                make_high(t.unit(0))
                make_high(t.unit(1))
                make_hidden_high(t.n, t.odd)
                make_silu(t.unit(0), t.odd + 1)
                make_high(t.unit(2))

            def unload(e):
                act.wait_ge(used.sem, expert_done(e))
                y = 4 + 2 * (e % 2)
                nc.scalar.activation(outputs[:, e, :].rearrange("p (a n) -> p a n", a=2), ps[:, y:y + 2, :],
                                     ACT.Copy).then_inc(output_taken.sem, 1)

            def last(t):
                make_high(t.unit(0))
                make_hidden_high(t.n, t.odd)
                unload(E - 1)

            stream(act, begin, triple, last, lambda e: unload(e - 1) if e > 0 else None)

        def low_of(eng, engine, u, part, sem):
            for h in range(2):
                eng.wait_ge(high.sem, u.half_number(h) + (hb + 1))
                at = slice(u.halves[h].start + part.start, u.halves[h].start + part.stop)
                raw = c.slots[u.raw][:, HALF * h + part.start:HALF * h + part.stop]
                engine.tensor_tensor(weight_low[:, at], raw, weight_high[:, at].bitcast(F32), ALU.subtract)\
                    .then_inc(sem, 1)

        @block.gpsimd
        @when(c)
        def _(pool):
            make = lambda u: low_of(pool, nc.gpsimd, u, slice(ON_DVE, HALF), low2.sem)
            stream(pool, lambda e: [make(g0), make(u0)] if e == 0 else None,
                   lambda t, e, e_next: [make(t.unit(j)) for j in range(3)], lambda t: make(t.unit(0)))

        @block.vector
        @when(c)
        def _(dve):
            make = lambda u: low_of(dve, nc.vector, u, slice(0, ON_DVE), low.sem)

            def make_hidden(n, up_made, parity):
                dve.wait_ge(silu_made.sem, n + (sb + 1))
                dve.wait_ge(used.sem, up_made)
                nc.vector.tensor_tensor(hidden, silu, up_bank(parity), ALU.mult).then_inc(hidden_made.sem, 1)

            def make_hidden_low(n, parity):
                dve.wait_ge(hidden_high.sem, n + (hidden_high.base + 1))
                nc.vector.tensor_tensor(low_hidden, gate_bank(parity), high_hidden.bitcast(F32), ALU.subtract)\
                    .then_inc(hidden_low.sem, 1)

            def inputs_of(e):
                dve.wait_ge(inputs_high.sem, inputs_high.base + e + 1)
                high_part, low_part = parts_of(e)
                nc.vector.tensor_tensor(low_part, inputs[:, e], high_part.bitcast(F32), ALU.subtract)\
                    .then_inc(inputs_low.sem, 1)

            def begin(e):
                if e == 0:
                    inputs_of(0)
                    make(g0)
                    make(u0)
                    make_hidden(0, ub + 4, 0)
                if e + 1 < E:
                    inputs_of(e + 1)

            def triple(t, e, e_next):
                make(t.unit(0))
                make(t.unit(1))
                make_hidden_low(t.n, t.odd)
                make(t.unit(2))
                make_hidden(t.n + 1, t.unit(1).half_number(1) + (ub + 1), t.odd + 1)

            def last(t):
                make(t.unit(0))
                make_hidden_low(t.n, t.odd)

            stream(dve, begin, triple, last)

        @block.tensor
        @when(c)
        def _(pe):
            def parts(u, h):
                pe.wait_ge(low.sem, u.half_number(h) + (wb + 1))
                pe.wait_ge(low2.sem, u.half_number(h) + (vb + 1))
                return weight_high[:, u.halves[h]], weight_low[:, u.halves[h]]

            def across(u, e, out):
                for h in range(2):
                    w = [m.rearrange("p (k f) -> p k f", k=KD // 2) for m in parts(u, h)]
                    for k in range(KD // 2):
                        at = h * (KD // 2) + k
                        last = three_passes(nc, out, [m[:, at, :] for m in parts_of(e)], [m[:, k, :] for m in w],
                                            at == 0, at == KD - 1)
                    last.then_inc(used.sem, 1)

            def turn(n, parity):
                pe.wait_ge(hidden_made.sem, n + (mb + 1))
                for h in range(2):
                    last = nc.tensor.transpose(ps[:, parity % 2, P * h:P * h + P], hidden[:, P * h:P * h + P], c.ident)
                last.then_inc(turned.sem, 1)

            def down(u, n, e):
                y = 4 + 2 * (e % 2)
                pe.wait_ge(hidden_low.sem, n + (hidden_low.base + 1))
                for h in range(2):
                    w = parts(u, h)
                    for q in range(2):
                        last = three_passes(nc, ps[:, y + q, :], [m[:, SLOTS * h:SLOTS * h + SLOTS] for m in
                                                                  (high_hidden, low_hidden)],
                                            [m[:, 512 * q:512 * q + 512] for m in w], False, False)
                    last.then_inc(used.sem, 1)

            def begin(e):
                if e >= 2:
                    pe.wait_ge(output_taken.sem, output_taken.base + e - 1)
                for q in range(2):
                    nc.tensor.matmul(ps[:, 4 + 2 * (e % 2) + q, :], c.zeros[:, 0:P], c.zeros, start=True, stop=False,
                                     skip_group_check=True)
                if e == 0:
                    pe.wait_ge(inputs_low.sem, inputs_low.base + 1)
                    across(g0, 0, gate_bank(0))
                    across(u0, 0, up_bank(0))

            def triple(t, e, e_next):
                if e_next != e:
                    pe.wait_ge(inputs_low.sem, inputs_low.base + e_next + 1)
                across(t.unit(0), e_next, gate_bank(t.odd + 1))
                turn(t.n, t.odd)
                across(t.unit(1), e_next, up_bank(t.odd + 1))
                down(t.unit(2), t.n, e)

            def last(t):
                turn(t.n, t.odd)
                down(t.unit(0), t.n, E - 1)

            stream(pe, begin, triple, last)


def combine_stage(c, given_to, outputs, keep):
    nc, ps, x = c.nc, c.ps, c.x
    combined, = signals(c, "moe_combined")
    with nc.Block() as block:
        @block.tensor
        @when(c)
        def _(pe):
            for t in range(TT):
                for n in range(2):
                    for e in range(EXPERTS):
                        last = nc.tensor.matmul(ps[:, 2 * t + n, :], given_to[:, e, P * t:P * t + P],
                                                outputs[:, e, 512 * n:512 * n + 512], start=(e == 0), stop=(e == EXPERTS - 1))
                    last.then_inc(combined.sem, 1)

        @block.vector
        @when(c)
        def _(dve):
            for t in range(TT):
                for n in range(2):
                    dve.wait_ge(combined.sem, combined.base + 2 * t + n + 1)
                    xn = x[:, t, 512 * n:512 * n + 512]
                    c.vchain(dve, nc.vector.scalar_tensor_tensor(out=xn, in0=xn, scalar=keep, in1=ps[:, 2 * t + n, :],
                                                                 op0=ALU.mult, op1=ALU.add))


class Routing:

    def __init__(self, chosen, weight, place, most):
        self.chosen, self.weight, self.place, self.most = chosen, weight, place, most


def moe_stage(c, router, lower, earlier, iota):
    nc, d, t = c.nc, c.dram, c.tables
    c.slots = [c.ring[:, n, :] for n in range(4)] + [m.rearrange("p a b -> p (a b)") for m in (c.vtm, c.merged)]
    te = lambda o: t[:, o:o + 16].rearrange("p (t e) -> p t e", t=TT)
    r = Routing(te(4400), te(4416), te(4432), c.most)
    route_stage(c, router, lower, earlier, r)
    G = d["l_moe_gate"].shape[0] // EXPERTS
    weights = (d["l_moe_gate"], d["l_moe_up"], d["l_moe_down"])
    flat = lambda s: s.rearrange("p a b -> p (a b)")
    xg = flat(c.seg).rearrange("p (e k s) -> p e k s", e=EXPERTS, k=KD)
    out = flat(c.seg).rearrange("p (e n) -> p e n", e=EXPERTS)
    picks = flat(c.merged).rearrange("p (t e s) -> p t e s", t=TT, e=EXPERTS)
    weighed = c.work[:, 0:2048].rearrange("p (t e s) -> p t e s", t=TT, e=EXPERTS)
    chain, mix = c.vchain, c.seg[:, 0:8]
    c.condition, c.vchain = lambda most: most > SLOTS, c.dense_chain
    spread_stage(c, r.weight, mix)
    ffn_stage(c, *weights, G, EXPERTS, mix, keep=ALPHA, add=1.0)
    c.condition, c.vchain = lambda most: most <= SLOTS, c.gathered_chain
    gate, up, down = weights
    gather_stage(c, r, iota, xg, c.cat, picks, weighed, [gate[0], up[0], gate[1], up[1], down[0]])
    experts_stage(c, *weights, G, xg, out)
    combine_stage(c, c.cat, out, ALPHA)
    c.condition, c.vchain = None, chain


def second_start(c):
    d, t = c.dram, c.tables
    norm_stage(c, gain_tm=d["final_norm_w"])
    norm_stage(c, layer=(d["ln_in_g"], d["ln_in_b"]))
    second_tables(c)


def second_tables(c):
    load_stage(c, [(c.tables[:, 0:4392], c.dram["l_second_tables"])])
    bounds_stage(c, c.tables[:, 4224:4240], c.bound[:, 0:HG], c.bound[:, HG:2 * HG])


def second_layer(c, layer):
    d, seg, vtm, t = c.dram, c.seg, c.vtm, c.tables
    decay = t[:, 0:2048].rearrange("p (h s t) -> p h s t", h=RET_HEADS, s=TT)
    rot, cos, sin = t[:, 2048:2176], t[:, 2176:2432], t[:, 2432:2688]
    c.block_causal, c.block_reset = t[:, 2688:2816], t[:, 2816:3072]
    mask = t[:, 3072:3584].rearrange("p (t k) -> p t k", t=TT)
    router = t[:, 3584:3648].rearrange("p (k e) -> p k e", k=KD)
    lower = t[:, 3648:3712].rearrange("p (e f) -> p e f", e=EXPERTS)
    sinks = t[:, 3712 + 16 * layer:3728 + 16 * layer]
    hg_gain = t[:, 3744 + layer:3745 + layer]
    w, wo = d["l_w_in"][46 * layer:46 * layer + 46], d["l_outs"][16 * layer:16 * layer + 16]

    def gated(n, gate, first, then):
        dst = c.merged if first else seg[:, 8:16]
        project_stage(c, [product(c, wo[4 * n:4 * n + 4], 4, gated_fm(c, dst, gate), src=c.cat)], "vector", then)
        if not first:
            weigh_add_stage(c, c.merged, dst)

    project_stage(c, [product(c, w[0:4], 4, to_fm(c, seg[:, 0:8])), product(c, w[4:8], 4, to_tm(c, vtm), tm=True),
                      product(c, w[8:12], 4, to_fm(c, seg[:, 8:16], ACT.Silu)),
                      product(c, w[34:38], 4, to_fm(c, seg[:, 16:24], ACT.Sigmoid))], then=first_groups(wo[0:4]))
    rope_stage(c, seg[:, 0:8], rot, cos, sin)
    retention_stage(c, seg[:, 0:4], seg[:, 4:8], vtm, decay, seg[:, 8:16], c.cat)
    gated(0, seg[:, 16:24], True, first_groups(w[12:20]))
    project_stage(c, [product(c, w[12:20], 8, to_fm(c, seg[:, 0:16])), product(c, w[20:24], 4, to_tm(c, vtm), tm=True),
                      product(c, w[24:28], 4, to_fm(c, seg[:, 16:24], ACT.Silu)),
                      product(c, w[38:42], 4, to_fm(c, seg[:, 24:32], ACT.Sigmoid))])
    hgrn_stage(c, seg[:, 0:8], seg[:, 8:16], vtm, seg[:, 16:24], c.bound[:, 0:HG], c.bound[:, HG:2 * HG], layer == 0,
               hg_gain, c.cat)
    gated(1, seg[:, 24:32], False, first_groups(w[28:32]))
    project_stage(c, [product(c, w[28:32], 4, to_fm(c, seg[:, 0:8])),
                      product(c, d["l_twice_sk"][2 * layer:2 * layer + 2], 2, to_fm(c, seg[:, 16:20])),
                      product(c, w[33:34], 1, to_tm(c, vtm), tm=True),
                      product(c, w[42:46], 4, to_fm(c, seg[:, 24:32], ACT.Sigmoid))])
    groups = []
    for g in range(4):
        for qt in range(TT):
            nk = P * (qt + 1)
            groups.append(([Pass(
                q=lambda p, j, g=g, qt=qt: seg[HD * p:HD * p + HD, 2 * g + j, P * qt:P * qt + P],
                k=lambda p, g=g, nk=nk: seg[HD * p:HD * p + HD, 16 + g, 0:nk], nk=nk,
                v=[vtm[:, l, HD * g:HD * g + HD] for l in range(qt + 1)], mask=mask[:, qt, 0:nk],
                sinks=sinks[:, 4 * g:4 * g + 4], gates=None, valid=None)],
                c.cat[:, 2 * g:2 * g + 2, P * qt:P * qt + P]))
    attention_stage(c, groups, HD ** -0.5)
    gated(2, seg[:, 24:32], False, first_groups(wo[12:16]))
    project_stage(c, [product(c, wo[12:16], 4, add_to_x(c, ALPHA), tm=True, src=c.merged)], "vector",
                  then=first_units(d["l_ffn2_gate"], d["l_ffn2_up"]) if layer == 0 else None)
    norm_stage(c, layer=(d["ln_mix_g"][layer], d["ln_mix_b"][layer]))
    if layer == 0:
        split_ffn_stage(c, d["l_ffn2_gate"], d["l_ffn2_up"], d["l_ffn2_down"], keep=ALPHA, add=1.0,
                        then=first_groups(d["l_w_in"][46:]))
    else:
        moe_stage(c, router, lower, t[:, 3760:3888], t[:, 3888:4016])
    norm_stage(c, layer=(d["ln_ffn_g"][layer], d["ln_ffn_b"][layer]))


def start_stage(c, ahead=None):
    nc = c.nc
    loads = [(c.x, c.dram["x"].rearrange("o (t p) d -> p (o t) d", p=P)), (c.ident, c.dram["c_ident"]),
             (c.gains, c.dram["l_gains"])]
    first, = signals(c, "first_loaded")
    c.ahead = ahead is not None
    with nc.Block() as block:
        @block.sync
        def _(sp):
            for dst, src in loads:
                sp.dma_start(dst, src).then_inc(first.sem, 16)
            if ahead is not None:
                load_ahead(c, sp, ahead, [])
            sp.wait_ge(first.sem, START + 16 * len(loads))

        @block.vector
        def _(dve):
            nc.vector.memset(c.zeros, 0.0)
            nc.vector.memset(c.ones, 1.0)
            nc.vector.memset(c.eps, RMS_EPS)


def end_stage(c):
    nc = c.nc
    stored, = signals(c, "stored")
    with nc.Block() as block:
        @block.sync
        def _(sp):
            sp.dma_start(c.dram["out"].rearrange("o (t p) d -> p (o t) d", p=P), c.x).then_inc(stored.sem, 16)
            sp.wait_ge(stored.sem, START + 16)


SIGNALS = ("stat_ready root_ready normed packed unloaded gains_loaded ffn_loaded0 ffn_loaded1 gate_made up_made "
           "silu_made weighed hidden_made hidden_used summed first_loaded stored vector_chain scalar_chain dense_chain gathered_chain "
           "weights_loaded0 weights_loaded1 product_made product_taken rope_turned rope_scaled roped scored biased "
           "exped factored weighted probs_turned turned_taken attended output_taken tables_loaded gm_var_made "
           "gm_root_made gm_normed gm_mixed cmp_hidden cmp_pe_made cmp_pe_taken cmp_gelued cmp_second cmp_rotated "
           "cmp_flipped pooled pooled_taken pool_mixed s5_angle_reduced s5_sines s5_driven s5_rotated "
           "s5_scanned s5_unrotated s5_read s5_skipped ret_scored ret_decayed ret_summed ret_kept ret_squared "
           "ret_square_summed ret_rooted ret_scaled ret_gated hg_sigmoid hg_bounded hg_logged hg_summed hg_exped "
           "hg_queries hg_keys hg_scored hg_turned_taken hg_masked hg_driven hg_drive_taken hg_stated hg_made hg_kept "
           "hg_square_summed hg_sums_taken hg_rooted hg_scaled bound_diff_made logits_made logit_diff_made "
           "logit_exp_made mix_spread chosen_made placed moe_picked moe_weighed moe_turned moe_turned_taken moe_gathered "
           "moe_taken moe_loaded0 moe_loaded1 moe_loaded2 moe_loaded3 moe_loaded4 moe_loaded5 moe_unit_high "
           "moe_unit_low_dve moe_unit_low_pool moe_parts_used moe_silu_made moe_hidden_made moe_hidden_turned "
           "moe_hidden_high moe_hidden_low moe_inputs_high moe_inputs_low "
           "moe_output_taken moe_combined input_high input_low weight_high_made weight_low_dve weight_low_pool unit_loaded0 unit_loaded1 "
           "unit_loaded2 unit_high unit_low_dve unit_low_pool s_down_made s_gate_made s_up_made s_silu_made "
           "s_hidden_made s_hidden_high s_hidden_low s_summed").split()


def allocate(c):
    nc = c.nc

    def sb(name, *shape):
        c.bytes = c.bytes + int(np.prod(shape)) * 4
        return c.stack.enter_context(nc.sbuf_tensor(name, [P, *shape], F32))[...]

    c.bytes, c.ahead = 0, False
    c.x = sb("x", TT, D)
    c.hT = sb("hT", KD, T)
    c.ring = sb("ring", 4, KD * GW)
    c.work = sb("work", 4096)
    c.rowbuf = sb("rowbuf", 2, D)
    c.small = sb("small", 64)
    c.ident = sb("ident", P)
    c.gains = sb("gains_fm", 6 * KD)
    c.zeros = c.stack.enter_context(nc.sbuf_tensor("zeros", [32, 512], mybir.dt.bfloat16))[...]
    c.ones = sb("ones", P)
    c.seg = sb("seg", 32, T)
    c.merged = sb("merged", KD, T)
    c.bound = sb("bound", 2 * HG)
    c.eps = sb("eps", 1)
    c.vtm = sb("vtm", TT, D)
    c.cat = sb("cat", KD, T)
    c.tables = sb("tables", 4800)
    c.most = c.stack.enter_context(nc.sbuf_tensor("most", [1, 1], mybir.dt.int32))[...]
    part = lambda n, *shape: c.stack.enter_context(nc.sbuf_tensor(n, [P, *shape], mybir.dt.float32r))[...]
    c.act_high, c.act_low = part("act_high", KD, T), part("act_low", KD, T)
    c.weight_high, c.weight_low = part("weight_high", 2, KD * GW), part("weight_low", 2, KD * GW)
    c.hidden_high, c.hidden_low = part("hidden_high", 2, T), part("hidden_low", 2, T)
    c.ps = c.stack.enter_context(nc.psum_tensor("ps", [P, 8, 512], F32))[...]


def program(nc, dram, stages):
    with ExitStack() as stack:
        c = Core(nc, dram, stack)
        allocate(c)
        signals(c, *SIGNALS)
        c.vchain = Chain(c.sig["vector_chain"].sem)
        c.dense_chain, c.gathered_chain = (Chain(c.sig[n].sem) for n in ("dense_chain", "gathered_chain"))
        c.achain = Chain(c.sig["scalar_chain"].sem)
        with nc.Block() as block:
            @block.gpsimd
            def _(pool):
                for s in c.sig.values():
                    nc.gpsimd.sem_inc(s.sem, START)
        start_stage(c, first_units(dram["l_ffn_gate"], dram["l_ffn_up"]))
        for s in stages:
            run_stage(c, s)
        end_stage(c)


def run_stage(c, s):
    d = c.dram
    kind, *a = s
    if kind == "ffn1":
        layer, half = a
        n = 3 * layer + 2 * half
        norm_stage(c, gain_fm=c.gains[:, KD * n:KD * n + KD])
        i = 2 * layer + half
        g = d["l_ffn_gate"].shape[0] // 4
        then = [first_groups(d["l_ev_in"]), first_units(d["l_ffn_gate"][2 * g:], d["l_ffn_up"][2 * g:]),
                first_groups(d["l_od_in"]), first_groups(d["l_w_in"])][i]
        split_ffn_stage(c, *(d[w][i * g:(i + 1) * g] for w in ("l_ffn_gate", "l_ffn_up", "l_ffn_down")), then=then)
    if kind == "even":
        even_mixer(c)
    if kind == "odd":
        odd_mixer(c)
    if kind == "second":
        second_start(c)
    if kind == "tables":
        second_tables(c)
    if kind == "moe":
        t = c.tables
        moe_stage(c, t[:, 3584:3648].rearrange("p (k e) -> p k e", k=KD),
                  t[:, 3648:3712].rearrange("p (e f) -> p e f", e=EXPERTS), t[:, 3760:3888], t[:, 3888:4016])
    if kind == "ln":
        norm_stage(c, layer=(d["ln_in_g"], d["ln_in_b"]))
    if kind == "layer":
        second_layer(c, *a)


def pack_in(w):
    k, n = w.shape
    return np.ascontiguousarray(w.reshape(k // P, P, n // GW, GW).transpose(2, 1, 0, 3)).reshape(n // GW, P, -1)


def pack_down(w):
    f, n = w.shape
    return np.ascontiguousarray(w.reshape(f // GW, 2, P, n).transpose(0, 2, 1, 3)).reshape(f // GW, P, -1)


def columns(v):
    return np.ascontiguousarray(v.reshape(-1, P).T)


def layout(i):
    i = {k: np.asarray(v) for k, v in i.items()}
    a = {"x": i["x"]}
    a["c_ident"] = np.eye(P, dtype=np.float32)
    a["l_gains"] = columns(i["norm_w"])
    a["l_ffn_gate"] = np.concatenate([pack_in(w) for l in i["ffn_w_gate"] for w in l])
    a["l_ffn_up"] = np.concatenate([pack_in(w) for l in i["ffn_w_up"] for w in l])
    a["l_ffn_down"] = np.concatenate([pack_down(w) for l in i["ffn_w_down"] for w in l])
    even_layout(i, a)
    odd_layout(i, a)
    second_layout(i, a)
    return a


def rope_tables(pos, half, steps):
    inv = (np.float32(10000.0) ** -steps).astype(np.float32)
    ang = (pos.astype(np.float32)[:, None] * inv[None, :]).astype(np.float32)
    return np.cos(ang).astype(np.float32), np.sin(ang).astype(np.float32)


def rotation(width):
    r, h = np.zeros((P, P), np.float32), width // 2
    for o in range(0, P, width):
        for n in range(h):
            r[o + h + n, o + n] = -1.0
            r[o + n, o + h + n] = 1.0
    return r


def even_layout(i, a):
    w = i["ev_w_in"][0]
    cut = np.cumsum([0, 512, 512, 512, 128, 128, 128, 128, 128, 128, 24])
    u, v, q, kc, vc, ks, vs, kw, vw, gl = (w[:, cut[n]:cut[n + 1]] for n in range(10))
    twice = lambda k: [k[:, 0:64], k[:, 0:64], k[:, 64:128], k[:, 64:128]]
    a["l_ev_in"] = pack_in(np.concatenate(
        [u, q, *twice(ks), *twice(kw), kc, vc, v, vs, vw, gl, np.zeros((D, GW - 24), np.float32)], axis=1))
    a["l_ev_out"] = pack_in(i["ev_w_out"][0])
    t = np.arange(T)
    qt = t.reshape(TT, P).T
    wT = i["gm_w_s"][0].transpose(2, 0, 1).reshape(P, -1)
    b = i["gm_b"][0]
    bias = np.repeat(np.tile(b, (1, TT)).reshape(4, 2, T), HD, axis=1).transpose(1, 0, 2).reshape(P, -1)
    causal = (np.arange(P)[:, None] <= np.arange(P)[None, :]).astype(np.float32)
    w2 = np.tile(i["nsa_cmp_w2"][0].transpose(1, 0, 2).reshape(HD, -1), (2, 1))
    pe = np.tile(i["nsa_cmp_pe"][0].transpose(2, 0, 1).reshape(HD, -1), (2, 1))
    steps = np.arange(32, dtype=np.float32) / 32
    cos, sin = rope_tables(t, 32, steps)
    fm = lambda m: np.tile(m.T, (4, 1))
    end = np.arange(NCMP) * CMP_STRIDE + CMP_LEN - 1
    cc, cs = rope_tables(end, 32, steps)
    pad = lambda m: np.concatenate([m, np.zeros((P - NCMP, 32), np.float32)])
    amask = np.where(t[None, None, :] <= qt[:, :, None], 0.0, NEG).astype(np.float32)
    cm = np.where(end[None, None, :] <= qt[:, :, None], 0.0, NEG).astype(np.float32)
    cmask = np.concatenate([cm, np.full((P, TT, 1), NEG, np.float32)], axis=2)
    valid = (qt >= end[0]).astype(np.float32)
    a["l_even_tables"] = np.concatenate(
        [wT, bias, causal, w2, pe, rotation(64), fm(cos), fm(sin), pad(cc), pad(cs), amask.reshape(P, -1),
         cmask.reshape(P, -1), valid], axis=1).astype(np.float32)
    a["l_cmp_w1"] = np.tile(i["nsa_cmp_w1"][0].reshape(2, CMP_LEN, HD, HD).transpose(2, 0, 1, 3).reshape(HD, -1), (2, 1))


def odd_layout(i, a):
    a["l_od_in"], a["l_od_out"], a["l_glu"] = (pack_in(i[n][0]) for n in ("od_w_in", "od_w_out", "s5_w_glu"))
    t = np.arange(T)
    ops = []
    for w in POOL_WINDOWS:
        seen = (t[:, None] <= t[None, :]) & (t[:, None] > t[None, :] - w)
        ops.append(seen / np.minimum(t + 1, w)[None, :] - np.eye(T))
    ops = np.stack(ops).astype(np.float32).reshape(4, TT, P, T).transpose(2, 0, 1, 3).reshape(P, -1)
    pw = i["pool_w"][0].transpose(1, 0, 2).reshape(P, -1)
    dt = np.repeat(i["s5_log_dt"][0], 64)
    b_in = np.zeros((2, 4, 4, 2, 16, 2, 64), np.float32)
    c_out = np.zeros((2, NT, 2, 64, 2, 16), np.float32)
    for n, (b, o) in enumerate(((i["s5_b_re"][0], i["s5_c_re"][0]), (i["s5_b_im"][0], i["s5_c_im"][0]))):
        for g in range(2):
            b_in[n, :, :, g, :, g, :] = b.reshape(4, 4, 2, 64, 16)[:, :, g].transpose(0, 1, 3, 2)
            c_out[n, :, g, :, g, :] = o.reshape(NT, 2, 16, 64)[:, g].transpose(0, 2, 1)
    b_in = b_in.reshape(2, 4, P, P).transpose(2, 0, 1, 3).reshape(P, -1)
    c_out = c_out.reshape(2, NT, P, CH).transpose(2, 0, 1, 3).reshape(P, -1)
    a["l_odd_tables"] = np.concatenate(
        [ops, pw, columns(i["pool_scale"]), columns(i["s5_d"]), columns(i["s5_lam_re"]), columns(i["s5_lam_im"]),
         columns(dt), b_in, c_out], axis=1)


def second_layout(i, a):
    for n in ("ln_in_g", "ln_in_b", "ln_mix_g", "ln_mix_b", "ln_ffn_g", "ln_ffn_b"):
        a[n] = i[n + "_2"]
    a["final_norm_w"] = i["final_norm_w"]
    w = i["w_in_2"]
    a["l_w_in"] = np.concatenate([pack_in(m) for m in w])
    sk = w[:, :, 8192:8448]
    a["l_twice_sk"] = np.concatenate([pack_in(np.repeat(m.reshape(D, 4, 1, HD), 2, axis=2).reshape(D, -1)) for m in sk])
    a["l_outs"] = np.concatenate([pack_in(i[n][l]) for l in range(2)
                                  for n in ("ret_w_out_2", "hgrn_w_out_2", "swa_w_out_2", "w_o_2")])
    a["l_ffn2_gate"], a["l_ffn2_up"] = pack_in(i["ffn_w_gate_2"][0]), pack_in(i["ffn_w_up_2"][0])
    a["l_ffn2_down"] = pack_down(i["ffn_w_down_2"][0])
    if "moe_w_gate_2" in i:
        a["l_moe_gate"] = np.concatenate([pack_in(m) for m in i["moe_w_gate_2"][0]])
        a["l_moe_up"] = np.concatenate([pack_in(m) for m in i["moe_w_up_2"][0]])
        a["l_moe_down"] = np.concatenate([pack_down(m) for m in i["moe_w_down_2"][0]])
    t = np.arange(T)
    gap = t[None, :] - t[:, None]
    gamma = 1.0 - 2.0 ** (-5.0 - np.arange(RET_HEADS))
    dec = np.where(gap >= 0, gamma[:, None, None] ** np.maximum(gap, 0), 0.0) * P ** -0.5
    dec = dec.reshape(RET_HEADS, TT, P, T).transpose(2, 0, 1, 3).reshape(P, -1)
    cos, sin = rope_tables(t, 64, np.linspace(0.0, 1.0, 64, dtype=np.float32))
    fm = lambda m: np.tile(m.T, (2, 1))
    p = np.arange(P)
    causal = (p[:, None] <= p[None, :]) & (p[:, None] // L == p[None, :] // L)
    reset = np.broadcast_to(t % L != 0, (P, T))
    chunk = np.arange(T) // 64
    qc = chunk.reshape(TT, P).T[:, :, None]
    mask = np.where((chunk <= qc) & (chunk >= qc - 2), 0.0, NEG).reshape(P, -1)
    router = i["moe_router_2"][0].reshape(KD, P, EXPERTS).transpose(1, 0, 2).reshape(P, -1)
    e = np.arange(EXPERTS)
    lower = np.broadcast_to((e[None, :] < e[:, None]).reshape(1, -1), (P, EXPERTS ** 2))
    sinks = np.broadcast_to(i["swa_sinks_2"].reshape(2, 4, 2, 2).transpose(0, 1, 3, 2).reshape(1, -1), (P, 32))
    gain = i["hgrn_norm_g_2"].T
    earlier = p[:, None] < p[None, :]
    iota = np.broadcast_to(p[None, :], (P, P))
    raw = columns(i["hgrn_lower_bounds_2"])
    a["l_second_tables"] = np.concatenate(
        [dec, rotation(P), fm(cos), fm(sin), causal, reset, mask, router, lower, sinks, gain,
         np.zeros((P, 14)), earlier, iota, np.zeros((P, 4224 - 4016)), raw,
         np.zeros((P, 4392 - 4240))], axis=1).astype(np.float32)


STAGES = [("ffn1", 0, 0), ("even",), ("ffn1", 0, 1), ("ffn1", 1, 0), ("odd",), ("ffn1", 1, 1), ("second",),
          ("layer", 0), ("layer", 1)]


def build(nc, arrays):
    dram = {n: nc.dram_tensor("in_" + n, v.shape, F32, kind="ExternalInput").ap() for n, v in arrays.items()}
    dram["out"] = nc.dram_tensor("out", (1, T, D), F32, kind="ExternalOutput").ap()
    program(nc, dram, STAGES)


def kernel(**inputs):
    import concourse.bacc as bacc
    from concourse.bass_utils import run_bass_kernel_spmd as run

    arrays = layout(inputs)
    nc = bacc.Bacc("TRN2", target_bir_lowering=False, num_devices=1)
    build(nc, arrays)
    r = run(nc, [{"in_" + n: v for n, v in arrays.items()}], core_ids=[0])
    return r.results[0]["out"]
```
